# Optimizing a Trainium2 kernel written in Bass

```python
import math
import jax, jax.numpy as jnp
from jax import lax
import numpy as np

D_MODEL = 1024
BATCH = 1
SEQ = 512
DEPTH = 1
DEC_BATCH = 8
DEC_SEQ = 1
PAST_LEN = 4096
PAGE_SIZE = 128

N_META = 16
POOL_WIDTH = D_MODEL // 2
POOL_WINDOWS = (2, 4, 8, 16)
N_POOL_GROUPS = len(POOL_WINDOWS)
POOL_GROUP = POOL_WIDTH // N_POOL_GROUPS
POOL_STATE = max(POOL_WINDOWS) - 1
HEAD_DIM = 64
N_HEADS = (D_MODEL // 2) // HEAD_DIM
N_KV_HEADS = 2
GQA_GROUP = N_HEADS // N_KV_HEADS
ATTN_WIDTH = N_HEADS * HEAD_DIM
KV_WIDTH = N_KV_HEADS * HEAD_DIM
MIX_WIDTH = POOL_WIDTH + ATTN_WIDTH
IN_WIDTH = POOL_WIDTH + ATTN_WIDTH + 2 * KV_WIDTH
WINDOW = 128
BLOCK = 128
ROPE_DIM = HEAD_DIM // 4
ROPE_THETA = 500000.0
D_FF = ((8 * D_MODEL // 3 + 127) // 128) * 128
EPS = 1e-6
SCALE = HEAD_DIM ** -0.5
NEG_INF = -1e30

kernel_name = 'hymba_pool_swa_sink_macaron_step'

def _rmsnorm(x, g):
    xf = x.astype(jnp.float32)
    y = xf * lax.rsqrt(jnp.mean(jnp.square(xf), axis=-1, keepdims=True) + EPS)
    return (y * g.astype(jnp.float32)).astype(x.dtype)

def _half_ffn(x, norm_g, w_gate, w_up, w_down):
    h = _rmsnorm(x, norm_g)
    return x + 0.5 * ((jax.nn.silu(h @ w_gate) * (h @ w_up)) @ w_down)

def _rope_partial(x, pos):
    half = ROPE_DIM // 2
    inv_freq = jnp.exp(-math.log(ROPE_THETA) * jnp.arange(half, dtype=jnp.float32) * (2.0 / ROPE_DIM))
    ang = pos.astype(jnp.float32)[:, None] * inv_freq[None, :]
    cos = jnp.cos(ang)[:, None, :]
    sin = jnp.sin(ang)[:, None, :]
    xf = x.astype(jnp.float32)
    x1 = xf[..., :half]
    x2 = xf[..., half:ROPE_DIM]
    out = jnp.concatenate([x1 * cos - x2 * sin, x2 * cos + x1 * sin, xf[..., ROPE_DIM:]], axis=-1)
    return out.astype(x.dtype)

def _project(h, pos, w_in, q_norm, k_norm):
    B, T, _ = h.shape
    z = h @ w_in
    o1 = POOL_WIDTH
    o2 = o1 + ATTN_WIDTH
    o3 = o2 + KV_WIDTH
    u = z[..., :o1]
    q = z[..., o1:o2].reshape(B, T, N_HEADS, HEAD_DIM)
    k = z[..., o2:o3].reshape(B, T, N_KV_HEADS, HEAD_DIM)
    v = z[..., o3:].reshape(B, T, N_KV_HEADS, HEAD_DIM)
    q = _rope_partial(_rmsnorm(q, q_norm), pos)
    k = _rope_partial(_rmsnorm(k, k_norm), pos)
    return u, q, k, v

def _pool_mix(u_ext, pos_out, pool_w, pool_scale):
    n_out = pos_out.shape[0]
    uf = u_ext.astype(jnp.float32)
    cs = jnp.cumsum(uf, axis=1)
    outs = []
    for g, w in enumerate(POOL_WINDOWS):
        sl = slice(g * POOL_GROUP, (g + 1) * POOL_GROUP)
        cp = jnp.pad(cs[..., sl], ((0, 0), (w, 0), (0, 0)))
        wsum = cp[:, w:] - cp[:, :-w]
        cnt = jnp.minimum(pos_out + 1, w).astype(jnp.float32)[None, :, None]
        d = wsum[:, -n_out:] / cnt - uf[:, -n_out:, sl]
        outs.append(d @ pool_w[g].astype(jnp.float32))
    y = jnp.concatenate(outs, axis=-1) * pool_scale.astype(jnp.float32)
    return y.astype(u_ext.dtype)

def _sink_probs(s, mask, sink):
    s = jnp.where(mask, s, NEG_INF)
    m = jnp.maximum(jnp.max(s, axis=-1, keepdims=True), sink)
    p = jnp.exp(s - m)
    return p / (jnp.sum(p, axis=-1, keepdims=True) + jnp.exp(sink - m))

def _swa_prompt(q, k, v, sinks):
    B, T = q.shape[0], q.shape[1]
    pad_front = (BLOCK - N_META % BLOCK) % BLOCK
    pad_end = (-(T + pad_front)) % BLOCK
    L = T + pad_front + pad_end
    nb = L // BLOCK
    padt = lambda a: jnp.pad(a.astype(jnp.float32), ((0, 0), (pad_front, pad_end), (0, 0), (0, 0)))
    qb = padt(q).reshape(B, nb, BLOCK, N_KV_HEADS, GQA_GROUP, HEAD_DIM)
    kb = padt(k).reshape(B, nb, BLOCK, N_KV_HEADS, HEAD_DIM)
    vb = padt(v).reshape(B, nb, BLOCK, N_KV_HEADS, HEAD_DIM)
    prev = lambda a: jnp.concatenate([jnp.zeros_like(a[:, :1]), a[:, :-1]], axis=1)
    k_band = jnp.concatenate([prev(kb), kb], axis=2)
    v_band = jnp.concatenate([prev(vb), vb], axis=2)
    pos = (jnp.arange(L) - pad_front).reshape(nb, BLOCK)
    kpos = jnp.concatenate([pos - BLOCK, pos], axis=1)
    diff = pos[:, :, None] - kpos[:, None, :]
    mask = (diff >= 0) & (diff < WINDOW) & (kpos[:, None, :] >= 0)
    s = jnp.einsum('bnqhgd,bnkhd->bnhgqk', qb, k_band) * SCALE
    sink = sinks.astype(jnp.float32).reshape(N_KV_HEADS, GQA_GROUP)[:, :, None, None]
    p = _sink_probs(s, mask[None, :, None, None], sink)
    o = jnp.einsum('bnhgqk,bnkhd->bnqhgd', p, v_band).reshape(B, L, ATTN_WIDTH)
    return o[:, pad_front:pad_front + T].astype(q.dtype)

def _swa_sample(q, k_new, v_new, cache_k, cache_v, sinks):
    B, S = q.shape[0], q.shape[1]
    n_win = cache_k.shape[1]
    k_ext = jnp.concatenate([cache_k.astype(k_new.dtype), k_new], axis=1)
    v_ext = jnp.concatenate([cache_v.astype(v_new.dtype), v_new], axis=1)
    qpos = PAST_LEN + jnp.arange(S)
    kpos = PAST_LEN - n_win + jnp.arange(n_win + S)
    diff = qpos[:, None] - kpos[None, :]
    mask = (diff >= 0) & (diff < WINDOW)
    qg = q.astype(jnp.float32).reshape(B, S, N_KV_HEADS, GQA_GROUP, HEAD_DIM)
    s = jnp.einsum('bqhgd,bkhd->bhgqk', qg, k_ext.astype(jnp.float32)) * SCALE
    sink = sinks.astype(jnp.float32).reshape(N_KV_HEADS, GQA_GROUP)[:, :, None, None]
    p = _sink_probs(s, mask, sink)
    o = jnp.einsum('bhgqk,bkhd->bqhgd', p, v_ext.astype(jnp.float32)).reshape(B, S, ATTN_WIDTH)
    return o.astype(q.dtype), k_ext[:, -n_win:], v_ext[:, -n_win:]

def setup_inputs(seed: int = 0) -> dict:
    key = jax.random.key(seed)
    ks = jax.random.split(key, 24)
    nrm = lambda k, shape, scale: scale * jax.random.normal(k, shape, jnp.float32)
    gain = lambda k, shape: 1.0 + 0.05 * jax.random.normal(k, shape, jnp.float32)
    n_win = min(WINDOW, PAST_LEN)
    return {
        'x_prompt': nrm(ks[0], (BATCH, SEQ, D_MODEL), 1.0),
        'x_sample': nrm(ks[1], (DEC_BATCH, DEC_SEQ, D_MODEL), 1.0),
        'state_pool': nrm(ks[2], (DEPTH, DEC_BATCH, POOL_STATE, POOL_WIDTH), 1.0),
        'cache_k': nrm(ks[3], (DEPTH, DEC_BATCH, n_win, N_KV_HEADS, HEAD_DIM), 1.0),
        'cache_v': nrm(ks[4], (DEPTH, DEC_BATCH, n_win, N_KV_HEADS, HEAD_DIM), 1.0),
        'meta_tokens': nrm(ks[5], (N_META, D_MODEL), 1.0),
        'ffn1_norm': gain(ks[6], (DEPTH, D_MODEL)),
        'ffn1_w_gate': nrm(ks[7], (DEPTH, D_MODEL, D_FF), D_MODEL ** -0.5),
        'ffn1_w_up': nrm(ks[8], (DEPTH, D_MODEL, D_FF), D_MODEL ** -0.5),
        'ffn1_w_down': nrm(ks[9], (DEPTH, D_FF, D_MODEL), D_FF ** -0.5),
        'mix_norm': gain(ks[10], (DEPTH, D_MODEL)),
        'w_in': nrm(ks[11], (DEPTH, D_MODEL, IN_WIDTH), D_MODEL ** -0.5),
        'q_norm': gain(ks[12], (DEPTH, HEAD_DIM)),
        'k_norm': gain(ks[13], (DEPTH, HEAD_DIM)),
        'attn_sinks': nrm(ks[14], (DEPTH, N_HEADS), 1.0),
        'pool_w': nrm(ks[15], (DEPTH, N_POOL_GROUPS, POOL_GROUP, POOL_GROUP), POOL_GROUP ** -0.5),
        'pool_scale': gain(ks[16], (DEPTH, POOL_WIDTH)),
        'w_out': nrm(ks[17], (DEPTH, MIX_WIDTH, D_MODEL), MIX_WIDTH ** -0.5),
        'ffn2_norm': gain(ks[18], (DEPTH, D_MODEL)),
        'ffn2_w_gate': nrm(ks[19], (DEPTH, D_MODEL, D_FF), D_MODEL ** -0.5),
        'ffn2_w_up': nrm(ks[20], (DEPTH, D_MODEL, D_FF), D_MODEL ** -0.5),
        'ffn2_w_down': nrm(ks[21], (DEPTH, D_FF, D_MODEL), D_FF ** -0.5),
    }

def reference(x_prompt, x_sample, state_pool, cache_k, cache_v, meta_tokens,
              ffn1_norm, ffn1_w_gate, ffn1_w_up, ffn1_w_down,
              mix_norm, w_in, q_norm, k_norm, attn_sinks, pool_w, pool_scale, w_out,
              ffn2_norm, ffn2_w_gate, ffn2_w_up, ffn2_w_down):
    B = x_prompt.shape[0]
    S = x_sample.shape[1]
    meta = jnp.broadcast_to(meta_tokens.astype(x_prompt.dtype)[None], (B, N_META, D_MODEL))
    xp = jnp.concatenate([meta, x_prompt], axis=1)
    T = xp.shape[1]
    pos_p = jnp.arange(T)
    pos_s = PAST_LEN + jnp.arange(S)
    xs = x_sample
    pool_p, k_p, v_p, pool_s, k_s, v_s = [], [], [], [], [], []
    for l in range(DEPTH):
        xp = _half_ffn(xp, ffn1_norm[l], ffn1_w_gate[l], ffn1_w_up[l], ffn1_w_down[l])
        u, q, k, v = _project(_rmsnorm(xp, mix_norm[l]), pos_p, w_in[l], q_norm[l], k_norm[l])
        mixed = jnp.concatenate([_pool_mix(u, pos_p, pool_w[l], pool_scale[l]),
                                 _swa_prompt(q, k, v, attn_sinks[l])], axis=-1)
        xp = xp + mixed @ w_out[l]
        xp = _half_ffn(xp, ffn2_norm[l], ffn2_w_gate[l], ffn2_w_up[l], ffn2_w_down[l])
        pool_p.append(u[:, -POOL_STATE:])
        k_p.append(k[:, -WINDOW:])
        v_p.append(v[:, -WINDOW:])
        xs = _half_ffn(xs, ffn1_norm[l], ffn1_w_gate[l], ffn1_w_up[l], ffn1_w_down[l])
        us, qs, ks_, vs_ = _project(_rmsnorm(xs, mix_norm[l]), pos_s, w_in[l], q_norm[l], k_norm[l])
        u_ext = jnp.concatenate([state_pool[l].astype(us.dtype), us], axis=1)
        attn_s, k_new, v_new = _swa_sample(qs, ks_, vs_, cache_k[l], cache_v[l], attn_sinks[l])
        mixed_s = jnp.concatenate([_pool_mix(u_ext, pos_s, pool_w[l], pool_scale[l]), attn_s], axis=-1)
        xs = xs + mixed_s @ w_out[l]
        xs = _half_ffn(xs, ffn2_norm[l], ffn2_w_gate[l], ffn2_w_up[l], ffn2_w_down[l])
        pool_s.append(u_ext[:, -POOL_STATE:])
        k_s.append(k_new)
        v_s.append(v_new)
    y_prompt = xp[:, N_META:]
    y_sample = xs
    return (y_prompt, y_sample, jnp.stack(pool_p), jnp.stack(k_p), jnp.stack(v_p),
            jnp.stack(pool_s), jnp.stack(k_s), jnp.stack(v_s))


_drawn_inputs = setup_inputs


def setup_inputs(seed=0):
    import zlib

    import numpy as np

    out = dict(_drawn_inputs(seed))
    spreads = {}
    factors = {'q_norm': 8.0, 'attn_sinks': 8.0, 'ffn2_norm': 3.401}
    for name, (base, spread) in spreads.items():
        noise = np.random.default_rng([zlib.crc32(name.encode()), seed]).standard_normal(out[name].shape)
        drawn = base * np.exp(spread * noise) if base else spread * noise
        out[name] = __import__('jax').numpy.asarray(drawn.astype(out[name].dtype))
    for name, factor in factors.items():
        out[name] = (out[name] * factor).astype(out[name].dtype)
    return out
```

```python
import math
from contextlib import ExitStack

import numpy as np

import concourse.bass as bass
from concourse import mybir

ALU = mybir.AluOpType
ACT = mybir.ActivationFunctionType
F32 = mybir.dt.float32
F32R = mybir.dt.float32r
BF16 = mybir.dt.bfloat16
AX = mybir.AxisListType.X

P = 128
D = 1024
KD = D // P
F = 2816
KF = F // P
META, SEQ, NDEC = 16, 512, 8
TP = META + SEQ
NT = TP + NDEC
NH_ALL = NT // 2
NOUT = SEQ + NDEC
NH_OUT = NOUT // 2
HD = 64
HEADS, KVH = 8, 2
GQ = HEADS // KVH
WIN = 128
POOLW = 512
NG = 4
WINDOWS = (2, 4, 8, 16)
STATE = 15
PAD = (-META) % P
NBLK = (PAD + TP) // P
QT = SEQ // P
PAST = 4096
ROPE = HD // 4
EPS = 1e-6
SCALE = HD ** -0.5
NEG = -1e30

N_CONST = 13
G_POOL, G_Q, G_K = 3 * KD, 3 * KD + NG, 3 * KD + NG + 1
N_GAIN = G_K + 1
RAW = 4
DOWN_T = KF // 2
A_UNITS, B_UNITS, IN_UNITS, OUT_UNITS = 2 * KF, 2 * KD, 10, KD
U_A1 = 0
U_B1 = U_A1 + A_UNITS
U_IN = U_B1 + B_UNITS
U_OUT = U_IN + IN_UNITS
U_A2 = U_OUT + OUT_UNITS
U_B2 = U_A2 + A_UNITS
U_END = U_B2 + B_UNITS
OUT_LOADS = 3

MIX = ["k", "v", "q0", "q1", "q2", "q3", "u0", "u1", "u2", "u3"]
PAIR_USES = ["k", "v", "q0", "q1", "q2", "q3", "u0", "ck", "st", "u1", "P0", "ss", "u2", "P1",
             "sr", "u3", "P2", "sp", "P3", "so"]
PAIR1 = {"v", "q1", "q3", "ck", "st"}
NS_USES = ["ffn1", "mix", "k", "tok", "q0", "q1", "q2", "q3"]
ROT_USES = ["k", "q0", "q1", "q2", "q3"]


def raw_counts():
    count, total = [], [0] * RAW
    for u in range(U_END):
        q = U_IN <= u < U_OUT and MIX[u - U_IN][0] == "q"
        total[u % RAW] += OUT_LOADS if U_OUT <= u < U_A2 else KVH if q else 1
        count.append(total[u % RAW])
    return count


def tiles_of(u):
    down = U_B1 <= u < U_IN or U_B2 <= u < U_END
    return DOWN_T if down else KD


def build(nc, a):
    rawc = raw_counts()
    ctx = ExitStack()
    at = [0]

    base = (nc.sbuf_base + 31) // 32 * 32
    ARENA = (nc.sbuf_usable_end - base) // 32 * 32 - 32
    ctx.enter_context(nc.sbuf_tensor("arena", [P, ARENA // 4], F32))

    def place(name, shape, dt=F32, offset=None):
        size = int(np.prod(shape[1:])) * (2 if dt == BF16 else 4)
        size = (size + 31) // 32 * 32
        o = at[0] if offset is None else offset
        if offset is None:
            at[0] += size
            assert at[0] <= ARENA, (name, at[0])
        return nc.alloc_sbuf_tensor_at(name, list(shape), dt, offset=base + o), o + size

    xT, _ = place("xT", [P, KD, NT])
    xhi_at = at[0]
    xhi, _ = place("xhi", [P, KD, NT], F32R)
    xlo, _ = place("xlo", [P, KD, NT], F32R)
    h_at = at[0]
    hhi, _ = place("hhi", [P, KF, NT], F32R)
    hlo, _ = place("hlo", [P, KF, NT], F32R)
    h_end = at[0]
    raw, _ = place("raw", [P, RAW, DOWN_T, P])
    whi, _ = place("whi", [P, 2, DOWN_T, P], F32R)
    wlo, _ = place("wlo", [P, 2, DOWN_T, P], F32R)
    rstd, _ = place("rstd", [P, NT])
    rms, _ = place("rms", [P, NT])
    gate, _ = place("gate", [P, NT])
    act_gate, _ = place("act_gate", [P, NT])
    hid, _ = place("hid", [P, NT])
    sq, _ = place("sq", [P, NT])
    sqsum, _ = place("sqsum", [P, NT])
    ident, _ = place("ident", [P, P])
    ones, _ = place("ones", [P, P])
    headsum, _ = place("headsum", [P, P])
    swap, _ = place("swap", [P, P])
    identb, _ = place("identb", [P, P], BF16)
    maskb, _ = place("maskb", [P, 2, 2 * P], BF16)
    eps, _ = place("eps", [P, 1])
    dsum, _ = place("dsum", [P, NDEC])
    small, _ = place("small", [P, 2, 32])
    gains, _ = place("gains", [P, N_GAIN])
    sink, _ = place("sink", [P, HEADS])
    nsink, _ = place("nsink", [P, HEADS])
    ssink, _ = place("ssink", [HD, 2])
    o = h_at
    xtok, o = place("xtok", [P, 5, D], offset=o)
    junk, o = place("junk", [P, D], offset=o)
    maskf, o = place("maskf", [P, 2, 2 * P], offset=o)
    diag, o = place("diag", [P, 5, P], offset=o)
    ssq, o = place("ssq", [P, 5], offset=o)
    grow, o = place("grow", [N_GAIN, P], offset=o)
    srow, o = place("srow", [1, HD], offset=o)
    o = h_at
    cosT, o = place("cosT", [P, NT], offset=o)
    sinT, o = place("sinT", [P, NT], offset=o)
    ck_at = o
    ck, o = place("ck", [P, NDEC, P], offset=o)
    ckT, _ = place("ckT", [P, NDEC, P], offset=ck_at)
    cv, o = place("cv", [P, NDEC, P], offset=o)
    state, o = place("state", [P, POOLW], offset=o)
    poolw, o = place("poolw", [P, NG, P], offset=o)
    qT, o = place("qT", [P, GQ, NOUT], offset=o)
    kT, o = place("kT", [P, PAD + NT], offset=o)
    vT, o = place("vT", [P, PAD + NT], offset=o)
    tok, o = place("tok", [P, 2 * 512], offset=o)
    stT, o = place("stT", [P, NG, NDEC, STATE + 1], offset=o)
    mhi, o = place("mhi", [P, KD, NOUT], F32R, offset=o)
    mlo, o = place("mlo", [P, KD, NOUT], F32R, offset=o)
    utok, o = place("utok", [32, POOLW], offset=o)
    up, o = place("up", [P, 2, 16 + NT], offset=o)
    wsum, o = place("wsum", [P, 2, 16 + NT], offset=o)
    probT, o = place("probT", [P, 2, GQ * P], offset=o)
    dscoreT, o = place("dscoreT", [P, HD], offset=o)
    dprobT, o = place("dprobT", [P, HD], offset=o)
    dprob, o = place("dprob", [HD, P], offset=o)
    dsmall, o = place("dsmall", [HD, 8], offset=o)
    prob_at = o
    zg, o = place("zg", [P, 2, NT], offset=prob_at)
    zsq, o = place("zsq", [P, 2, NT], offset=o)
    prob, _ = place("prob", [P, 2, GQ, 2 * P], offset=prob_at)
    assert o <= h_end, (o, h_end)
    ytok, o = place("ytok", [P, 2, QT, P], offset=xhi_at)
    ysmp, o = place("ysmp", [NDEC, 2, P], offset=o)
    ybuf, o = place("ybuf", [P, 2, NOUT], offset=o)

    ps = ctx.enter_context(nc.psum_tensor("ps", [P, 8, 512], F32))
    pair = [ps[:, 0:2, :], ps[:, 2:4, :]]
    nsum = ps[:, 4:6, :]
    turn = ps[:, 6:8, :]
    scorebank = [ps[:, 2:4, :], ps[:, 4:6, :]]

    def sem(name):
        return ctx.enter_context(nc.semaphore(name))

    x_loaded = [sem(f"x_loaded{c}") for c in range(5)]
    consts_loaded = sem("consts_loaded")
    mixin_loaded = sem("mixin_loaded")
    raw_loaded = [sem(f"raw_loaded{r}") for r in range(RAW)]
    whi_ready = sem("whi_ready")
    wlo_ready = sem("wlo_ready")
    unit_done = sem("unit_done")
    evacuated = sem("evacuated")
    consts_made = sem("consts_made")
    gains_turned = sem("gains_turned")
    gains_ready = sem("gains_ready")
    x_turned = sem("x_turned")
    ssq_ready = sem("ssq_ready")
    diag_ready = sem("diag_ready")
    xhi_ready = sem("xhi_ready")
    xlo_ready = sem("xlo_ready")
    sq_ready = sem("sq_ready")
    sqsum_ready = sem("sqsum_ready")
    sqsum_zero = sem("sqsum_zero")
    nsum_filled = sem("nsum_filled")
    root_ready = sem("root_ready")
    inv_ready = sem("inv_ready")
    silu_ready = sem("silu_ready")
    silu_scaled = sem("silu_scaled")
    hhi_ready = sem("hhi_ready")
    hlo_ready = sem("hlo_ready")
    zg_ready = sem("zg_ready")
    rot_filled = sem("rot_filled")
    cos_ready = sem("cos_ready")
    sin_ready = sem("sin_ready")
    rot_ready = sem("rot_ready")
    qk_ready = sem("qk_ready")
    pads_zero = sem("pads_zero")
    tok_ready = sem("tok_ready")
    newv_placed = sem("newv_placed")
    pair_filled = sem("pair_filled")
    summed = sem("summed")
    pooled = sem("pooled")
    phi_ready = sem("phi_ready")
    step = sem("step")
    newk_placed = sem("newk_placed")
    scored = sem("scored")
    nmax_ready = sem("nmax_ready")
    exp_ready = sem("exp_ready")
    prob_ready = sem("prob_ready")
    probs_turned = sem("probs_turned")
    probT_a = sem("probT_a")
    probT_b = sem("probT_b")
    attended = sem("attended")
    ohi_ready = sem("ohi_ready")
    olo_ready = sem("olo_ready")
    dnmax_ready = sem("dnmax_ready")
    dexp_ready = sem("dexp_ready")
    dprob_ready = sem("dprob_ready")
    dohi_ready = sem("dohi_ready")
    y_turned = sem("y_turned")
    y_copied = sem("y_copied")
    y_sent = [sem("y_sent0"), sem("y_sent1")]
    mix_sent = sem("mix_sent")

    E_A1 = 5
    E_B1 = E_A1 + 2 * KF
    E_MIX = E_B1 + KD
    E_OUT = E_MIX + len(PAIR_USES)
    E_A2 = E_OUT + KD
    E_B2 = E_A2 + 2 * KF
    pair_of = {u: int(u in PAIR1) for u in PAIR_USES}
    extra = [u for u in PAIR_USES if u not in MIX]
    E_USE = {u: E_MIX + i for i, u in enumerate(PAIR_USES)}
    before = {}
    for i, u in enumerate(PAIR_USES):
        prev = [v for v in PAIR_USES[:i] if pair_of[v] == pair_of[u]]
        before[u] = E_USE[prev[-1]] + 1 if prev else E_MIX - 1 + pair_of[u]
    filled = {u: i + 1 for i, u in enumerate(extra)}
    summed_at = {0: 1, 1: 3, 2: 6, 3: 10}

    def up_to(const, slope=0, it=None):
        return const if it is None else const + it * slope

    STAGES = [dict(ua=U_A1, ub=U_B1, ea=E_A1, eb=E_B1, c0=0, n=NH_ALL, f0=0, x0=0, w=(0, 1)),
              dict(ua=U_A2, ub=U_B2, ea=E_A2, eb=E_B2, c0=META, n=NH_OUT, f0=KF, x0=2 * KD, w=(2, 3))]

    def halves(tile2d, n):
        return tile2d.rearrange("p (s n) -> p s n", n=n)

    def tile(t, d, it, c0, w, step=2):
        if it is None:
            return t[:, d, c0:c0 + w]
        return t[:, :, :].rearrange("p k n -> p (k n)")[:, bass.ds((it * step + d) * NT + c0, w)]

    def gain(g, d, it):
        if it is None:
            return gains[:, g * KD + d:g * KD + d + 1]
        return gains[:, bass.ds(it * 2 + g * KD + d, 1)]

    block = ctx.enter_context(nc.Block())

    @block.sync
    def _(sp):
        first = P - META
        sp.dma_start(xtok[0:META, 0, :], a["meta"]).then_inc(x_loaded[0], 16)
        sp.dma_start(xtok[META:P, 0, :], a["xp"][0:first, :]).then_inc(x_loaded[0], 16)
        for c in range(1, 4):
            lo = first + P * (c - 1)
            sp.dma_start(xtok[:, c, :], a["xp"][lo:lo + P, :]).then_inc(x_loaded[c], 16)
        sp.dma_start(xtok[0:META, 4, :], a["xp"][SEQ - META:SEQ, :]).then_inc(x_loaded[4], 16)
        sp.dma_start(xtok[META:META + NDEC, 4, :], a["xs"]).then_inc(x_loaded[4], 16)

        def free(c, it=None):
            if c >= RAW:
                sp.wait_ge(wlo_ready, up_to(c - RAW + 1, RAW, it))

        def load(c, src, it=None):
            free(c, it)
            t = src.shape[1]
            sp.dma_start(raw[:, c % RAW, 0:t, :], src).then_inc(raw_loaded[c % RAW], 16)

        def ffn_up(s, f0, it=None, f=None):
            for i in range(2):
                for j, w in enumerate((s["gate_w"], s["up_w"])):
                    col = (f0 + i) * P if it is None else (it * 2 + f0 + i) * P
                    load(s["ua"] + 2 * (f0 + i) + j,
                         w.rearrange("(k p) f -> p k f", p=P)[:, :, bass.ds(col, P)], it)

        def ffn_down(s, it):
            for i in range(2):
                for j in range(2):
                    col = (it * 2 + i) * P
                    load(s["ub"] + 2 * i + j,
                         s["down_w"].rearrange("(k p) d -> p k d", p=P)[
                             :, j * DOWN_T:(j + 1) * DOWN_T, bass.ds(col, P)], it)

        def ffn(s):
            if s["ua"] == 0:
                ffn_up(s, 0)
                with sp.Fori(0, KF // 2 - 1) as it:
                    ffn_up(s, 2, it)
            else:
                with sp.Fori(0, KF // 2) as it:
                    ffn_up(s, 0, it)
            with sp.Fori(0, KD // 2) as it:
                ffn_down(s, it)

        for s, i in zip(STAGES, (1, 2)):
            s.update(gate_w=a[f"g{i}"], up_w=a[f"u{i}"], down_w=a[f"d{i}"])
        ffn(STAGES[0])

        w_in = a["w_in"].rearrange("(k p) n -> p k n", p=P)
        srcs = {"k": w_in[:, :, 2 * POOLW:2 * POOLW + P],
                "v": w_in[:, :, 2 * POOLW + P:2 * POOLW + 2 * P]}
        for g in range(NG):
            srcs[f"u{g}"] = w_in[:, :, g * P:(g + 1) * P]

        def load_in(m):
            c, name = U_IN + m, MIX[m]
            if name[0] != "q":
                return load(c, srcs[name])
            j = int(name[1])
            free(c)
            for h in range(KVH):
                col = POOLW + (h * GQ + j) * HD
                sp.dma_start(raw[:, c % RAW, 0:KD, h * HD:(h + 1) * HD], w_in[:, :, col:col + HD]
                             ).then_inc(raw_loaded[c % RAW], 16)

        for m in range(4):
            load_in(m)
        sp.wait_ge(unit_done, U_IN)
        for dst, src in ((cosT[:], a["cos"]), (sinT[:], a["sin"]),
                         (ck[0:WIN - 1], a["ck"][:, 1:WIN, :].rearrange("b t c -> t b c")),
                         (cv[0:WIN - 1], a["cv"][:, 1:WIN, :].rearrange("b t c -> t b c")),
                         (state[0:NDEC * STATE], a["state"].rearrange("b t c -> (b t) c")),
                         (poolw[:], a["pool_w"].rearrange("g c e -> c g e"))):
            sp.dma_start(dst, src).then_inc(mixin_loaded, 16)
        for dst, src in ((a["o_ks"][:, 0:WIN - 1, :], a["ck"][:, 1:WIN, :]),
                         (a["o_vs"][:, 0:WIN - 1, :], a["cv"][:, 1:WIN, :]),
                         (a["o_ps"][:, 0:STATE - 1, :], a["state"][:, 1:STATE, :])):
            sp.dma_start(dst, src).then_inc(mix_sent, 16)
        for m in range(4, IN_UNITS):
            load_in(m)

        def load_out(d):
            c = U_OUT + d
            free(c)
            cols = slice(d * P, (d + 1) * P)
            dst = raw[:, c % RAW]
            sp.dma_start(dst[:, 0:NG, :], a["w_out"][0:POOLW, cols].rearrange(
                "(k p) d -> p k d", p=P)).then_inc(raw_loaded[c % RAW], 16)
            for h in range(KVH):
                r = POOLW + h * GQ * HD
                sp.dma_start(dst[h * HD:(h + 1) * HD, NG:NG + GQ, :],
                             a["w_out"][r:r + GQ * HD, cols].rearrange("(j e) d -> e j d", e=HD)
                             ).then_inc(raw_loaded[c % RAW], 16)

        load_out(0)
        sp.wait_ge(tok_ready, 2)
        vblk4 = tok[:, 4 * P:5 * P]
        sp.dma_start(a["o_vp"], vblk4).then_inc(mix_sent, 16)
        sp.dma_start(a["o_kp"], tok[:, 5 * P:6 * P]).then_inc(mix_sent, 16)
        sp.dma_start(a["o_vs"][:, WIN - 1, :], tok[0:NDEC, 6 * P:7 * P]).then_inc(mix_sent, 16)
        sp.dma_start(a["o_ks"][:, WIN - 1, :], tok[0:NDEC, 7 * P:8 * P]).then_inc(mix_sent, 16)
        for b in range(NDEC):
            sp.dma_start(cv[WIN - 1:WIN, b, :], tok[b:b + 1, 6 * P:7 * P]).then_inc(newv_placed, 16)
        for d in range(1, KD):
            load_out(d)
        sp.wait_ge(evacuated, E_USE["P3"] + 1)
        sp.dma_start(a["o_pp"], utok[0:STATE, :]).then_inc(mix_sent, 16)
        sp.dma_start(a["o_ps"][:, STATE - 1, :], utok[STATE:STATE + NDEC, :]).then_inc(mix_sent, 16)
        ffn(STAGES[1])
        sp.wait_ge(mix_sent, 16 * 9)

    @block.tensor
    def _(pe):
        def product(c, it, slope, dst, tiles, hi, lo, k0, kall, c0, n, wait_k=None, ks=None):
            if ks is None or ks[0] == 0:
                pe.wait_ge(wlo_ready, up_to(c + 1, slope, it))
            for kk in ks or range(tiles):
                k = k0 + kk
                if wait_k:
                    wait_k(k)
                for w, x in ((whi, hi), (whi, lo), (wlo, hi)):
                    for s in range(2):
                        last = nc.tensor.matmul(
                            dst[:, s, 0:n], w[:, c % 2, kk, :], x[:, k, c0 + s * n:c0 + (s + 1) * n],
                            start=(k == 0 and w is whi and x is hi), stop=(k == kall - 1 and w is wlo))
            if not ks or ks[-1] == tiles - 1:
                last.then_inc(unit_done, 1)

        pe.wait_ge(consts_made, 3)
        nc.tensor.transpose(turn[:, 0, 0:N_GAIN], grow[:, :], ident[0:N_GAIN, 0:N_GAIN])
        nc.tensor.transpose(turn[0:HD, 1, 0:1], srow[0:1, :], ident[0:1, 0:1]).then_inc(gains_turned, 1)
        for c in range(5):
            rows = P if c < 4 else NT - 4 * P
            pe.wait_ge(x_loaded[c], 16 if 0 < c < 4 else 32)
            if c >= 2:
                pe.wait_ge(evacuated, c - 1)
            dst = pair[(c + 1) % 2].rearrange("p s n -> p (s n)")
            for k in range(KD):
                last = nc.tensor.transpose(dst[:, k * P:k * P + rows], xtok[0:rows, c, k * P:(k + 1) * P],
                                           ident[0:rows, 0:rows])
            last.then_inc(x_turned, 1)
        flat = nsum.rearrange("p s n -> p (s n)")
        for c in range(5):
            rows = P if c < 4 else NT - 4 * P
            pe.wait_ge(diag_ready, c + 1)
            last = nc.tensor.matmul(flat[:, c * P:c * P + rows], ones[0:rows, :], diag[0:rows, c, 0:rows],
                                    start=True, stop=True)
        last.then_inc(nsum_filled, 1)

        def norm_sums(i, c0, n):
            pe.wait_ge(sqsum_ready, KD * i)
            for s in range(2):
                last = nc.tensor.matmul(nsum[:, s, 0:n], ones[:, :], sqsum[:, c0 + s * n:c0 + (s + 1) * n],
                                        start=True, stop=True)
            last.then_inc(nsum_filled, 1)

        def ffn_products(s, second):
            ua, ub, ea, eb, c0, n = (s[x] for x in ("ua", "ub", "ea", "eb", "c0", "n"))

            def gate_or_up(j, it, ks=None, f=0, wait_k=None):
                if ks is None or ks[0] == 0:
                    pe.wait_ge(evacuated, up_to(ea + 2 * f + j - 1, 2, it))
                product(ua + 2 * f + j, it, 2, pair[j], KD, xhi, xlo, 0, KD, c0, n, wait_k, ks)

            def x_there(k):
                pe.wait_ge(xlo_ready, s["x0"] + k + 1)

            gate_or_up(0, None, [0, 1, 2, 3, 4, 5], wait_k=x_there)
            if second:
                norm_sums(2, c0, n)
            gate_or_up(0, None, [6, 7], wait_k=x_there)
            with pe.Fori(0, KF - 1) as it:
                gate_or_up(1, it)
                gate_or_up(0, it, f=1)
            gate_or_up(1, None, f=KF - 1)

            def down(d, it, after_first=None):
                for j in range(2):
                    if j == 0:
                        pe.wait_ge(evacuated, up_to(eb + d - 1, 2, it))

                    def h_there(k):
                        if k in (0, KF - 1):
                            pe.wait_ge(hlo_ready, s["f0"] + KF - (k == 0))
                    product(ub + 2 * d + j, it, 4, pair[d % 2], DOWN_T, hhi, hlo, j * DOWN_T, KF,
                            c0, n, h_there)
                    if j == 0 and after_first:
                        after_first()

            if not second:
                with pe.Fori(0, KD // 2) as it:
                    down(0, it)
                    down(1, it)
                return

            def turn_y(d, it=None):
                pe.wait_ge(evacuated, up_to(eb + d + 1, 2, it))
                if d >= 2:
                    pe.wait_ge(y_copied, up_to(d - 1, 2, it))
                bank = (nsum, turn)[d % 2]
                for t in range(QT):
                    nc.tensor.transpose(bank[:, 0, t * P:(t + 1) * P], ybuf[:, d % 2, t * P:(t + 1) * P],
                                        ident[:, :])
                nc.tensor.transpose(bank[0:NDEC, 1, 0:P], ybuf[:, d % 2, SEQ:NOUT], ident[:, :]
                                    ).then_inc(y_turned, 1)

            down(0, None)
            down(1, None, lambda: turn_y(0))
            with pe.Fori(0, KD // 2 - 1) as it:
                down(2, it, lambda: turn_y(1, it))
                down(3, it, lambda: turn_y(2, it))
            turn_y(KD - 1)

        ffn_products(STAGES[0], False)

        def project(m, ks=None, wait_k=None):
            name = MIX[m]
            if ks is None or ks[0] == 0:
                pe.wait_ge(evacuated, before[name])
            q = name[0] == "q"
            product(U_IN + m, None, 0, pair[pair_of[name]], KD, xhi, xlo, 0, KD,
                    META if q else 0, NH_OUT if q else NH_ALL, wait_k, ks)

        def head_norm(x):
            c0, n = (0, NH_ALL) if x == 0 else (META, NH_OUT)
            pe.wait_ge(zg_ready, x + 1)
            if x == 1:
                pe.wait_ge(tok_ready, 2)
            else:
                pe.wait_ge(root_ready, x + 2)
            for s in range(2):
                last = nc.tensor.matmul(nsum[:, s, 0:n], headsum[:, :], zsq[:, x % 2, c0 + s * n:c0 + (s + 1) * n],
                                        start=True, stop=True)
            last.then_inc(nsum_filled, 1)
            if x >= 1:
                pe.wait_ge(sin_ready, x)
            for s in range(2):
                last = nc.tensor.matmul(turn[:, s, 0:n], swap[:, :], zg[:, x % 2, c0 + s * n:c0 + (s + 1) * n],
                                        start=True, stop=True)
            last.then_inc(rot_filled, 1)

        def x_there(k):
            pe.wait_ge(xlo_ready, KD + k + 1)

        project(0, [0, 1, 2, 3, 4, 5], x_there)
        norm_sums(1, 0, NH_ALL)
        project(0, [6, 7], x_there)
        project(1)
        head_norm(0)
        project(2)
        project(3)
        pe.wait_ge(root_ready, 3)
        pe.wait_ge(qk_ready, 1)
        pe.wait_ge(evacuated, E_USE["v"] + 1)
        pe.wait_ge(pads_zero, 2)
        for b in range(NBLK):
            nc.tensor.transpose(flat[:, b * P:(b + 1) * P], vT[:, b * P:(b + 1) * P], ident[:, :])
        nc.tensor.transpose(flat[:, 5 * P:6 * P], kT[:, PAD + TP - WIN:PAD + TP], ident[:, :])
        nc.tensor.transpose(flat[0:NDEC, 6 * P:7 * P], vT[:, PAD + TP:PAD + NT], ident[:, :])
        nc.tensor.transpose(flat[0:NDEC, 7 * P:8 * P], kT[:, PAD + TP:PAD + NT], ident[:, :]
                            ).then_inc(nsum_filled, 1)
        half = [[0, 1, 2, 3], [4, 5, 6, 7]]
        project(4, half[0])
        head_norm(1)
        project(4, half[1])
        project(5, half[0])
        head_norm(2)
        project(5, half[1])
        project(6, half[0])
        head_norm(3)
        project(6, half[1])

        def use(name):
            pe.wait_ge(evacuated, before[name])
            return pair[pair_of[name]]

        def turn_cache():
            dst = use("ck").rearrange("p s n -> p (s n)")
            pe.wait_ge(mixin_loaded, 16 * 6)
            for b in range(NDEC):
                last = nc.tensor.transpose(dst[:, b * P:b * P + WIN - 1], ck[0:WIN - 1, b, :],
                                           ident[0:WIN - 1, 0:WIN - 1])
            last.then_inc(pair_filled, 1)

        def turn_state():
            dst = use("st")
            rows = NDEC * STATE
            for g in range(NG):
                last = nc.tensor.transpose(dst[:, 0, g * rows:(g + 1) * rows], state[0:rows, g * P:(g + 1) * P],
                                           ident[0:rows, 0:rows])
            last.then_inc(pair_filled, 1)

        def pool_map(g):
            dst = use(f"P{g}")
            pe.wait_ge(pooled, g + 1)
            for s in range(2):
                nc.tensor.matmul(dst[:, s, 0:NH_OUT], poolw[:, g, :], gate[:, s * NH_OUT:(s + 1) * NH_OUT],
                                 start=True, stop=True)
            last0 = 16 + TP - STATE
            nc.tensor.transpose(dst[0:STATE + NDEC, 0, 384:512], up[:, g % 2, last0:16 + NT], ident[:, :]
                                ).then_inc(pair_filled, 1)

        def scores(i):
            t, g = divmod(i, 2)
            rows = slice(g * HD, (g + 1) * HD)
            if i < 2:
                pe.wait_ge(qk_ready, 5)
                pe.wait_ge(root_ready, 7)
                pe.wait_ge(evacuated, E_USE["st"] + 1)
            else:
                pe.wait_ge(olo_ready, i - 1)
            for j in range(GQ):
                dst = scorebank[i % 2][:, j // 2, (j % 2) * 2 * P:(j % 2 + 1) * 2 * P]
                nc.tensor.matmul(dst, identb[:, :], maskb[:, min(t, 1), :], start=(j % 2 == 0), stop=False,
                                 skip_group_check=True)
                last = nc.tensor.matmul(dst, qT[rows, j, t * P:(t + 1) * P], kT[rows, t * P:(t + 2) * P],
                                        start=False, stop=True, skip_group_check=True)
            last.then_inc(scored, 1)

        def turn_probs(i):
            pe.wait_ge(prob_ready, i + 1)
            if i == 0:
                pe.wait_ge(sin_ready, 5)
            else:
                pe.wait_ge(probT_a, i)
                pe.wait_ge(probT_b, i)
            for b in range(2):
                for j in range(GQ):
                    last = nc.tensor.transpose(turn[:, b, j * P:(j + 1) * P], prob[:, i % 2, j, b * P:(b + 1) * P],
                                               ident[:, :])
            last.then_inc(probs_turned, 1)

        def attend(i):
            t, g = divmod(i, 2)
            rows = slice(g * HD, (g + 1) * HD)
            pe.wait_ge(probT_a, i + 1)
            pe.wait_ge(probT_b, i + 1)
            for b in range(2):
                last = nc.tensor.matmul(scorebank[i % 2][rows, 0, :],
                                        tok[:, (t + b) * P + g * HD:(t + b) * P + (g + 1) * HD],
                                        probT[:, b, :], start=(b == 0), stop=(b == 1))
            last.then_inc(attended, 1)

        def decode_scores():
            dst = use("ss")
            pe.wait_ge(newk_placed, 1)
            for g in range(KVH):
                rows = slice(g * HD, (g + 1) * HD)
                for b in range(NDEC):
                    last = nc.tensor.matmul(dst[:, g, b * GQ:(b + 1) * GQ], ckT[rows, b, :],
                                            qT[rows, :, SEQ + b], start=True, stop=True)
            last.then_inc(pair_filled, 1)

        def decode_turn():
            dst = use("sr")
            pe.wait_ge(evacuated, E_USE["ss"] + 1)
            nc.tensor.transpose(dst[0:HD, 0, 0:P], dscoreT[:, :], ident[:, :]).then_inc(pair_filled, 1)

        def decode_turn_back():
            dst = use("sp")
            pe.wait_ge(dprob_ready, 1)
            nc.tensor.transpose(dst[:, 0, 0:HD], dprob[:, :], ident[0:HD, 0:HD]).then_inc(pair_filled, 1)

        def decode_attend():
            dst = use("so")
            pe.wait_ge(evacuated, E_USE["sp"] + 1)
            pe.wait_ge(newv_placed, 16 * NDEC)
            for g in range(KVH):
                rows = slice(g * HD, (g + 1) * HD)
                for b in range(NDEC):
                    c = (g * NDEC + b) * GQ
                    last = nc.tensor.matmul(dst[rows, g, b * GQ:(b + 1) * GQ], cv[:, b, rows],
                                            dprobT[:, c:c + GQ], start=True, stop=True)
            last.then_inc(pair_filled, 1)

        turn_cache()
        head_norm(4)
        turn_state()
        project(7)
        scores(0)
        pool_map(0)
        decode_scores()
        scores(1)
        project(8, half[0])
        turn_probs(0)
        project(8, half[1])
        attend(0)
        turn_probs(1)
        scores(2)
        pool_map(1)
        decode_turn()
        project(9, half[0])
        attend(1)
        turn_probs(2)
        scores(3)
        project(9, half[1])
        attend(2)
        turn_probs(3)
        scores(4)
        pool_map(2)
        decode_turn_back()
        for i in range(3, 2 * QT):
            attend(i)
            if i + 1 < 2 * QT:
                turn_probs(i + 1)
            if i + 2 < 2 * QT:
                scores(i + 2)
            if i == 4:
                pool_map(3)
            if i == 5:
                decode_attend()

        for d in range(KD):
            if d == 0:
                pe.wait_ge(evacuated, E_OUT)
            elif d == 1:
                pe.wait_ge(olo_ready, 2 * QT)
            else:
                pe.wait_ge(evacuated, E_OUT + d - 1)

            def mixed_there(k):
                if d == 0 and k == NG:
                    pe.wait_ge(olo_ready, 2 * QT)
            product(U_OUT + d, None, 0, pair[d % 2], KD, mhi, mlo, 0, KD, 0, NH_OUT, mixed_there)
        ffn_products(STAGES[1], True)

    @block.scalar
    def _(act):
        for dst, src in ((ident[:], a["const"][:, 0:P]), (headsum[:], a["const"][:, P:2 * P]),
                         (swap[:], a["const"][:, 2 * P:3 * P]), (maskf[:], a["const"][:, 3 * P:7 * P]),
                         (grow[0:KD, :], a["n1"]), (grow[KD:2 * KD, :], a["nm"]),
                         (grow[2 * KD:3 * KD, :], a["n2"]), (grow[3 * KD:3 * KD + NG, :], a["pool_scale"]),
                         (grow[G_Q:G_Q + 1, 0:HD], a["qn"]), (grow[G_Q:G_Q + 1, HD:P], a["qn"]),
                         (grow[G_K:G_K + 1, 0:HD], a["kn"]), (grow[G_K:G_K + 1, HD:P], a["kn"]),
                         (sink[:], a["sinks"].to_broadcast([P, HEADS]))):
            act.dma_start(dst, src).then_inc(consts_loaded, 16)

        def split_hi(c, it=None, slope=4):
            t = tiles_of(c)
            act.wait_ge(raw_loaded[c % RAW], up_to(16 * rawc[c], 16, it))
            if c >= 2:
                act.wait_ge(unit_done, up_to(c - 1, slope, it))
            nc.scalar.copy(whi[:, c % 2, 0:t, :], raw[:, c % RAW, 0:t, :]).then_inc(whi_ready, 1)

        def x_hi(d, g, c0, n, base, it=None):
            nc.scalar.activation(tile(xhi, d, it, c0, 2 * n), tile(xT, d, it, c0, 2 * n), ACT.Copy,
                                 scale=gain(g, d, it)).then_inc(xhi_ready, 1)

        def root(i, c0, n, wait):
            act.wait_ge(nsum_filled, wait)
            nc.scalar.activation(halves(rms[:, c0:c0 + 2 * n], n), nsum[:, :, 0:n], ACT.Sqrt,
                                 scale=1.0 / D, bias=eps[:, 0:1]).then_inc(root_ready, 1)

        for c in range(5):
            rows = P if c < 4 else NT - 4 * P
            act.wait_ge(x_loaded[c], 16 if 0 < c < 4 else 32)
            if c:
                act.wait_ge(ssq_ready, c)
            nc.scalar.activation(junk[0:rows, :], xtok[0:rows, c, :], ACT.Square,
                                 accum_out=ssq[0:rows, c:c + 1]).then_inc(ssq_ready, 1)
        split_hi(0)
        split_hi(1)
        act.wait_ge(consts_made, 3)
        act.wait_ge(nsum_filled, 1)
        nc.scalar.activation(rms[:, :], nsum.rearrange("p s n -> p (s n)")[:, 0:NT], ACT.Sqrt,
                             scale=1.0 / D, bias=eps[:, 0:1]).then_inc(root_ready, 1)
        act.wait_ge(gains_ready, 1)
        act.wait_ge(evacuated, 5)
        for d in range(KD):
            x_hi(d, 0, 0, NH_ALL, 0)

        def ffn_act(s, second):
            ua, ub, ea, eb, c0, n = (s[x] for x in ("ua", "ub", "ea", "eb", "c0", "n"))
            cols = slice(c0, c0 + 2 * n)

            def step_a(f, it=None):
                split_hi(ua + 2 * f + 2, it)
                act.wait_ge(evacuated, up_to(ea + 2 * f + 1, 4, it))
                nc.scalar.activation(act_gate[:, cols], gate[:, cols], ACT.Silu).then_inc(silu_ready, 1)
                split_hi(ua + 2 * f + 3, it)
                act.wait_ge(evacuated, up_to(ea + 2 * f + 2, 4, it))
                nc.scalar.copy(tile(hhi, f, it, c0, 2 * n), hid[:, cols]).then_inc(hhi_ready, 1)

            with act.Fori(0, KF // 2 - 1) as it:
                step_a(0, it)
                step_a(1, it)
            step_a(KF - 2)
            step_a(KF - 1)

            def step_b(d, it=None):
                if ub + 2 * d + 2 < U_END:
                    split_hi(ub + 2 * d + 2, it)
                    split_hi(ub + 2 * d + 3, it)
                if second:
                    act.wait_ge(y_turned, up_to(d + 1, 2, it))
                    if d >= 2:
                        act.wait_ge(y_sent[d % 2], up_to(32 * (d // 2), 32, it))
                    bank = (nsum, turn)[d % 2]
                    nc.scalar.copy(ytok[:, d % 2, :, :], bank[:, 0, :])
                    nc.scalar.copy(ysmp[:, d % 2, :], bank[0:NDEC, 1, 0:P]).then_inc(y_copied, 1)
                    act.wait_ge(y_copied, up_to(d + 1, 2, it))
                    col = d * P if it is None else (it * 2 + d) * P
                    act.dma_start(a["o_y"].rearrange("(t p) d -> p t d", p=P)[:, :, bass.ds(col, P)],
                                  ytok[:, d % 2, :, :]).then_inc(y_sent[d % 2], 16)
                    act.dma_start(a["o_ysm"][:, bass.ds(col, P)], ysmp[:, d % 2, :]).then_inc(y_sent[d % 2], 16)
                else:
                    act.wait_ge(evacuated, up_to(eb + d + 1, 2, it))
                    x_hi(d, 1, c0, n, KD, it)

            if second:
                step_b(0)
                step_b(1)
                with act.Fori(0, KD // 2 - 2) as it:
                    step_b(2, it)
                    step_b(3, it)
            else:
                with act.Fori(0, KD // 2 - 1) as it:
                    step_b(0, it)
                    step_b(1, it)
            step_b(KD - 2)
            step_b(KD - 1)

        ffn_act(STAGES[0], False)
        root(1, 0, NH_ALL, 2)

        def split_next(m):
            split_hi(U_IN + m + 2)

        def spread_z(x):
            c0, n = (0, NH_ALL) if x == 0 else (META, NH_OUT)
            act.wait_ge(evacuated, E_USE[MIX[x + (x > 0)]] + 1)
            if x >= 2:
                act.wait_ge(rot_filled, x - 1)
                act.wait_ge(cos_ready, x - 1)
            nc.scalar.activation(zg[:, x % 2, c0:c0 + 2 * n], gate[:, c0:c0 + 2 * n], ACT.Copy,
                                 scale=gains[:, G_Q + (x == 0):G_Q + (x == 0) + 1])
            nc.scalar.activation(zsq[:, x % 2, c0:c0 + 2 * n], gate[:, c0:c0 + 2 * n], ACT.Square
                                 ).then_inc(zg_ready, 1)

        def head_root(x):
            c0, n = (0, NH_ALL) if x == 0 else (META, NH_OUT)
            act.wait_ge(nsum_filled, x + 3 + (x > 0))
            act.wait_ge(inv_ready, x + 2)
            nc.scalar.activation(halves(rms[:, c0:c0 + 2 * n], n), nsum[:, :, 0:n], ACT.Sqrt,
                                 scale=1.0 / HD, bias=eps[:, 0:1]).then_inc(root_ready, 1)

        def exps(i):
            act.wait_ge(nmax_ready, i + 1)
            if i >= 2:
                act.wait_ge(probs_turned, i - 1)
            s = i % 2
            for j in range(GQ):
                nc.scalar.activation(prob[:, s, j, :], scorebank[s][:, j // 2, (j % 2) * 2 * P:(j % 2 + 1) * 2 * P],
                                     ACT.Exp, scale=SCALE, bias=small[:, s, 4 + j:5 + j],
                                     accum_out=small[:, s, 12 + j:13 + j])
            nc.scalar.activation(small[:, s, 16:20], small[:, s, 8:12], ACT.Exp).then_inc(exp_ready, 1)

        def out_probT(i):
            act.wait_ge(probs_turned, i + 1)
            if i >= 1:
                act.wait_ge(attended, i)
            nc.scalar.copy(probT[:, 0, :], turn[:, 0, :]).then_inc(probT_a, 1)

        def out_hi(i):
            t, g = divmod(i, 2)
            rows = slice(g * HD, (g + 1) * HD)
            act.wait_ge(attended, i + 1)
            nc.scalar.copy(mhi[rows, NG:NG + GQ, t * P:(t + 1) * P],
                           scorebank[i % 2][rows, 0, :].rearrange("p (j q) -> p j q", j=GQ)).then_inc(ohi_ready, 1)

        def pool_hi(g):
            act.wait_ge(pair_filled, filled[f"P{g}"])
            nc.scalar.activation(halves(mhi[:, g, :], NH_OUT), pair[0][:, :, 0:NH_OUT], ACT.Copy,
                                 scale=gains[:, G_POOL + g:G_POOL + g + 1]).then_inc(phi_ready, 1)

        split_next(0)
        spread_z(0)
        split_next(1)
        head_root(0)
        split_next(2)
        spread_z(1)
        split_next(3)
        spread_z(2)
        head_root(1)
        split_next(4)
        spread_z(3)
        head_root(2)
        split_next(5)
        spread_z(4)
        head_root(3)
        split_next(6)
        head_root(4)
        split_next(7)
        pool_hi(0)
        exps(0)
        exps(1)
        out_probT(0)
        split_next(8)
        out_hi(0)
        out_probT(1)
        pool_hi(1)
        exps(2)
        act.wait_ge(dnmax_ready, 1)
        nc.scalar.activation(dprob[:, :], pair[0][0:HD, 0, 0:P], ACT.Exp, scale=SCALE, bias=dsmall[:, 1:2],
                             accum_out=dsmall[:, 3:4])
        nc.scalar.activation(dsmall[:, 4:5], dsmall[:, 2:3], ACT.Exp).then_inc(dexp_ready, 1)
        out_hi(1)
        out_probT(2)
        exps(3)
        split_next(9)
        out_hi(2)
        out_probT(3)
        pool_hi(2)
        exps(4)
        for i in range(3, 2 * QT):
            out_hi(i)
            if i + 1 < 2 * QT:
                out_probT(i + 1)
            if i + 2 < 2 * QT:
                exps(i + 2)
            if i == 4:
                pool_hi(3)
            if i == 5:
                act.wait_ge(pair_filled, filled["so"])
                for g in range(KVH):
                    rows = slice(g * HD, (g + 1) * HD)
                    last = nc.scalar.copy(mhi[rows, NG:NG + GQ, SEQ:NOUT],
                                          pair[0][rows, g, 0:NDEC * GQ].rearrange("p (b j) -> p j b", b=NDEC))
                last.then_inc(dohi_ready, 1)

        for d in range(KD):
            split_hi(U_OUT + d + 2)
            act.wait_ge(evacuated, E_OUT + d + 1)
            x_hi(d, 2, META, NH_OUT, 2 * KD)
        root(2, META, NH_OUT, 9)
        act.wait_ge(mix_sent, 16 * 9)
        ffn_act(STAGES[1], True)
        for r in range(2):
            act.wait_ge(y_sent[r], 32 * (KD // 2))

    @block.vector
    def _(dve):
        steps = [0]

        def chain(ins):
            steps[0] += 1
            ins.then_inc(step, 1)
            dve.wait_ge(step, steps[0])

        nc.vector.memset(ones[:, :], 1.0).then_inc(consts_made, 1)
        nc.vector.memset(eps[:, :], EPS).then_inc(consts_made, 1)
        dve.wait_ge(consts_loaded, 16 * N_CONST)
        nc.vector.tensor_copy(identb[:, :], ident[:, :])
        nc.vector.tensor_copy(maskb[:], maskf[:])
        nc.vector.tensor_scalar(nsink[:, :], sink[:, :], -1.0, None, ALU.mult)
        nc.vector.tensor_copy(srow[0:1, :].rearrange("p (g b j) -> p g b j", g=KVH, b=NDEC),
                              sink[0:1, :].rearrange("p (g o j) -> p g o j", g=KVH, o=1).to_broadcast(
                                  [1, KVH, NDEC, GQ])).then_inc(consts_made, 1)
        dve.wait_ge(gains_turned, 1)
        nc.vector.tensor_copy(gains[:, :], turn[:, 0, 0:N_GAIN])
        nc.vector.tensor_copy(ssink[:, 0:1], turn[0:HD, 1, 0:1])
        nc.vector.tensor_scalar(ssink[:, 1:2], turn[0:HD, 1, 0:1], -1.0, None, ALU.mult).then_inc(gains_ready, 1)

        def split_lo(c, it=None, slope=4):
            t = tiles_of(c)
            dve.wait_ge(whi_ready, up_to(c + 1, slope, it))
            nc.vector.tensor_tensor(wlo[:, c % 2, 0:t, :], raw[:, c % RAW, 0:t, :],
                                    whi[:, c % 2, 0:t, :].bitcast(F32), ALU.subtract).then_inc(wlo_ready, 1)

        def x_lo(d, g, c0, n, base, it=None):
            dve.wait_ge(xhi_ready, up_to(base + d + 1, 2, it))
            nc.vector.scalar_tensor_tensor(out=tile(xlo, d, it, c0, 2 * n), in0=tile(xT, d, it, c0, 2 * n),
                                           scalar=gain(g, d, it), in1=tile(xhi, d, it, c0, 2 * n).bitcast(F32),
                                           op0=ALU.mult, op1=ALU.subtract).then_inc(xlo_ready, 1)

        def invert(i, dst, c0, n):
            dve.wait_ge(root_ready, i + 1)
            nc.vector.reciprocal(dst[:, c0:c0 + 2 * n], rms[:, c0:c0 + 2 * n]).then_inc(inv_ready, 1)

        for c in range(5):
            rows = P if c < 4 else NT - 4 * P
            dve.wait_ge(x_turned, c + 1)
            src = pair[(c + 1) % 2].rearrange("p s n -> p (s n)").rearrange("p (k n) -> p k n", k=KD)
            nc.vector.tensor_copy(xT[:, :, c * P:c * P + rows], src[:, :, 0:rows]).then_inc(evacuated, 1)
            dve.wait_ge(ssq_ready, c + 1)
            nc.vector.tensor_scalar(diag[0:rows, c, 0:rows], ident[0:rows, 0:rows], ssq[0:rows, c:c + 1], None,
                                    ALU.mult).then_inc(diag_ready, 1)
        split_lo(0)
        split_lo(1)
        for d in range(KD):
            x_lo(d, 0, 0, NH_ALL, 0)
        invert(0, rstd, 0, NH_ALL)
        dve.wait_ge(inv_ready, 1)

        def ffn_vector(s, second):
            ua, ub, ea, eb, c0, n, f0 = (s[x] for x in ("ua", "ub", "ea", "eb", "c0", "n", "f0"))
            cols = slice(c0, c0 + 2 * n)

            def step_a(f, it=None):
                dve.wait_ge(unit_done, up_to(ua + 2 * f + 1, 4, it))
                dve.wait_ge(silu_ready, up_to(f0 + f, 2, it))
                nc.vector.tensor_tensor(halves(gate[:, cols], n), pair[0][:, :, 0:n], halves(rstd[:, cols], n),
                                        ALU.mult).then_inc(evacuated, 1)
                split_lo(ua + 2 * f + 2, it)
                dve.wait_ge(silu_ready, up_to(f0 + f + 1, 2, it))
                nc.vector.tensor_tensor(hid[:, cols], act_gate[:, cols], rstd[:, cols], ALU.mult
                                        ).then_inc(silu_scaled, 1)
                dve.wait_ge(unit_done, up_to(ua + 2 * f + 2, 4, it))
                dve.wait_ge(silu_scaled, up_to(f0 + f + 1, 2, it))
                nc.vector.tensor_tensor(halves(hid[:, cols], n), pair[1][:, :, 0:n], halves(hid[:, cols], n),
                                        ALU.mult).then_inc(evacuated, 1)
                split_lo(ua + 2 * f + 3, it)
                dve.wait_ge(hhi_ready, up_to(f0 + f + 1, 2, it))
                nc.vector.tensor_tensor(tile(hlo, f, it, c0, 2 * n), hid[:, cols],
                                        tile(hhi, f, it, c0, 2 * n).bitcast(F32), ALU.subtract
                                        ).then_inc(hlo_ready, 1)

            with dve.Fori(0, KF // 2 - 1) as it:
                step_a(0, it)
                step_a(1, it)
            step_a(KF - 2)
            step_a(KF - 1)

            def step_b(d, it=None):
                if ub + 2 * d + 2 < U_END:
                    split_lo(ub + 2 * d + 2, it)
                dve.wait_ge(unit_done, up_to(ub + 2 * d + 2, 4, it))
                x_d = halves(tile(xT, d, it, c0, 2 * n), n)
                if second and d >= 2:
                    dve.wait_ge(y_turned, up_to(d - 1, 2, it))
                dst = halves(ybuf[:, d % 2, :], n) if second else x_d
                nc.vector.scalar_tensor_tensor(out=dst, in0=pair[d % 2][:, :, 0:n], scalar=0.5, in1=x_d,
                                               op0=ALU.mult, op1=ALU.add).then_inc(evacuated, 1)
                if ub + 2 * d + 3 < U_END:
                    split_lo(ub + 2 * d + 3, it)
                if not second:
                    x_lo(d, 1, c0, n, KD, it)

            if second:
                step_b(0)
                step_b(1)
                with dve.Fori(0, KD // 2 - 2) as it:
                    step_b(2, it)
                    step_b(3, it)
            else:
                with dve.Fori(0, KD // 2 - 1) as it:
                    step_b(0, it)
                    step_b(1, it)
            step_b(KD - 2)
            step_b(KD - 1)

        ffn_vector(STAGES[0], False)
        invert(1, rstd, 0, NH_ALL)
        dve.wait_ge(inv_ready, 2)

        def split_next(m):
            split_lo(U_IN + m + 2)

        def scaled(m, dst, c0, n):
            dve.wait_ge(unit_done, U_IN + m + 1)
            nc.vector.tensor_tensor(halves(dst, n), pair[pair_of[MIX[m]]][:, :, 0:n],
                                    halves(rstd[:, c0:c0 + 2 * n], n), ALU.mult).then_inc(evacuated, 1)

        def take_z(x):
            c0, n = (0, NH_ALL) if x == 0 else (META, NH_OUT)
            dve.wait_ge(zg_ready, x) if x else None
            scaled(x + (x > 0), gate[:, c0:c0 + 2 * n], c0, n)

        def rotate(x):
            c0, n = (0, NH_ALL) if x == 0 else (META, NH_OUT)
            cols = slice(c0, c0 + 2 * n)
            if x:
                dve.wait_ge(qk_ready, x)
            invert(x + 2, act_gate, c0, n)
            dve.wait_ge(rot_filled, x + 1)
            nc.vector.tensor_tensor(halves(sq[:, cols], n), turn[:, :, 0:n], halves(sinT[:, cols], n),
                                    ALU.mult).then_inc(sin_ready, 1)
            dve.wait_ge(rot_ready, x + 1)
            dve.wait_ge(inv_ready, x + 3)
            dst = kT[:, PAD:PAD + NT] if x == 0 else qT[:, x - 1, :]
            nc.vector.tensor_tensor(dst, hid[:, cols], act_gate[:, cols], ALU.mult).then_inc(qk_ready, 1)

        def pool_mean(g):
            w = WINDOWS[g]
            src = up[:, g % 2, :]
            win = wsum[:, g % 2, :]
            if g:
                dve.wait_ge(pair_filled, filled[f"P{g - 1}"])
            dve.wait_ge(summed, summed_at[g])
            nc.vector.scalar_tensor_tensor(out=gate[:, 0:SEQ], in0=win[:, 16 + META:16 + TP], scalar=1.0 / w,
                                           in1=src[:, 16 + META:16 + TP], op0=ALU.mult, op1=ALU.subtract)
            chain(nc.vector.tensor_copy(stT[:, g, :, STATE], src[:, 16 + TP:16 + NT]))
            chain(nc.vector.tensor_reduce(dsum[:, :], stT[:, g, :, STATE + 1 - w:STATE + 1], AX, ALU.add))
            nc.vector.scalar_tensor_tensor(out=gate[:, SEQ:NOUT], in0=dsum[:, :], scalar=1.0 / w,
                                           in1=src[:, 16 + TP:16 + NT], op0=ALU.mult, op1=ALU.subtract
                                           ).then_inc(pooled, 1)

        def pool_lo(g):
            dve.wait_ge(phi_ready, g + 1)
            nc.vector.scalar_tensor_tensor(out=halves(mlo[:, g, :], NH_OUT), in0=pair[0][:, :, 0:NH_OUT],
                                           scalar=gains[:, G_POOL + g:G_POOL + g + 1], in1=halves(mhi[:, g, :].bitcast(F32), NH_OUT),
                                           op0=ALU.mult, op1=ALU.subtract)
            nc.vector.tensor_copy(utok[0:STATE + NDEC, g * P:(g + 1) * P], pair[0][0:STATE + NDEC, 0, 384:512]
                                  ).then_inc(evacuated, 1)

        def take_u(g):
            if g >= 2:
                dve.wait_ge(pair_filled, filled[f"P{g - 2}"])
                dve.wait_ge(summed, summed_at[g - 2])
            scaled(6 + g, up[:, g % 2, 16:16 + NT], 0, NH_ALL)

        def maxima(i):
            s = i % 2
            g = i % 2
            dve.wait_ge(scored, i + 1)
            sc = scorebank[s].rearrange("p s (j k) -> p (s j) k", k=2 * P)
            chain(nc.vector.tensor_reduce(small[:, s, 0:4], sc, AX, ALU.max))
            chain(nc.vector.scalar_tensor_tensor(out=small[:, s, 4:8], in0=small[:, s, 0:4], scalar=-SCALE,
                                                 in1=nsink[:, g * GQ:(g + 1) * GQ], op0=ALU.mult, op1=ALU.min))
            nc.vector.tensor_tensor(small[:, s, 8:12], small[:, s, 4:8], sink[:, g * GQ:(g + 1) * GQ], ALU.add
                                    ).then_inc(nmax_ready, 1)

        def normalise(i):
            s = i % 2
            dve.wait_ge(exp_ready, i + 1)
            chain(nc.vector.tensor_tensor(small[:, s, 20:24], small[:, s, 12:16], small[:, s, 16:20], ALU.add))
            chain(nc.vector.reciprocal(small[:, s, 24:28], small[:, s, 20:24]))
            for j in range(GQ):
                last = nc.vector.tensor_scalar(prob[:, s, j, :], prob[:, s, j, :], small[:, s, 24 + j:25 + j], None,
                                               ALU.mult)
            last.then_inc(prob_ready, 1)

        def out_probT(i):
            dve.wait_ge(probs_turned, i + 1)
            if i >= 1:
                dve.wait_ge(attended, i)
            nc.vector.tensor_copy(probT[:, 1, :], turn[:, 1, :]).then_inc(probT_b, 1)

        def out_lo(i):
            t, g = divmod(i, 2)
            rows = slice(g * HD, (g + 1) * HD)
            dve.wait_ge(ohi_ready, i + 1)
            nc.vector.tensor_tensor(mlo[rows, NG:NG + GQ, t * P:(t + 1) * P],
                                    scorebank[i % 2][rows, 0, :].rearrange("p (j q) -> p j q", j=GQ),
                                    mhi[rows, NG:NG + GQ, t * P:(t + 1) * P].bitcast(F32), ALU.subtract
                                    ).then_inc(olo_ready, 1)

        take_z(0)
        split_next(0)
        scaled(1, vT[:, PAD:PAD + NT], 0, NH_ALL)
        dve.wait_ge(evacuated, E_USE["v"] + 1)
        split_next(1)
        dve.wait_ge(mixin_loaded, 16 * 6)
        rotate(0)
        take_z(1)
        split_next(2)
        take_z(2)
        split_next(3)
        dve.wait_ge(nsum_filled, 4)
        tokps = nsum.rearrange("p s n -> p (s n)")
        nc.vector.tensor_copy(tok[:, 0:6 * P], tokps[:, 0:6 * P]).then_inc(tok_ready, 1)
        nc.vector.tensor_copy(tok[0:NDEC, 6 * P:8 * P], tokps[0:NDEC, 6 * P:8 * P]).then_inc(tok_ready, 1)
        rotate(1)
        take_z(3)
        split_next(4)
        rotate(2)
        take_z(4)
        split_next(5)
        rotate(3)
        dve.wait_ge(pads_zero, 3)
        take_u(0)
        split_next(6)
        dve.wait_ge(pair_filled, filled["ck"])
        nc.vector.tensor_copy(ckT[:, :, 0:WIN - 1],
                              pair[1].rearrange("p s n -> p (s n)").rearrange("p (b k) -> p b k", b=NDEC)[
                                  :, :, 0:WIN - 1]).then_inc(evacuated, 1)
        nc.vector.tensor_copy(ckT[:, :, WIN - 1], kT[:, PAD + TP:PAD + NT]).then_inc(newk_placed, 1)
        rotate(4)
        dve.wait_ge(pair_filled, filled["st"])
        nc.vector.tensor_copy(stT[:, :, :, 0:STATE],
                              pair[1][:, 0, 0:NG * NDEC * STATE].rearrange("p (g b t) -> p g b t", g=NG, b=NDEC)
                              ).then_inc(evacuated, 1)
        dve.wait_ge(evacuated, E_USE["st"] + 1)
        pool_mean(0)
        take_u(1)
        split_next(7)
        maxima(0)
        pool_lo(0)
        dve.wait_ge(pair_filled, filled["ss"])
        nc.vector.tensor_copy(dscoreT[:, :].rearrange("p (g c) -> p g c", g=KVH), pair[0][:, :, 0:NDEC * GQ]
                              ).then_inc(evacuated, 1)
        normalise(0)
        maxima(1)
        pool_mean(1)
        normalise(1)
        out_probT(0)
        take_u(2)
        split_next(8)
        out_lo(0)
        out_probT(1)
        maxima(2)
        pool_lo(1)
        dve.wait_ge(pair_filled, filled["sr"])
        chain(nc.vector.tensor_reduce(dsmall[:, 0:1], pair[0][0:HD, 0, 0:P], AX, ALU.max))
        chain(nc.vector.scalar_tensor_tensor(out=dsmall[:, 1:2], in0=dsmall[:, 0:1], scalar=-SCALE,
                                             in1=ssink[:, 1:2], op0=ALU.mult, op1=ALU.min))
        nc.vector.tensor_tensor(dsmall[:, 2:3], dsmall[:, 1:2], ssink[:, 0:1], ALU.add).then_inc(dnmax_ready, 1)
        normalise(2)
        pool_mean(2)
        dve.wait_ge(dexp_ready, 1)
        nc.vector.tensor_tensor(dsmall[:, 5:6], dsmall[:, 3:4], dsmall[:, 4:5], ALU.add).then_inc(evacuated, 1)
        dve.wait_ge(evacuated, E_USE["sr"] + 1)
        chain(nc.vector.reciprocal(dsmall[:, 6:7], dsmall[:, 5:6]))
        nc.vector.tensor_scalar(dprob[:, :], dprob[:, :], dsmall[:, 6:7], None, ALU.mult).then_inc(dprob_ready, 1)
        out_lo(1)
        out_probT(2)
        maxima(3)
        take_u(3)
        split_next(9)
        normalise(3)
        out_lo(2)
        out_probT(3)
        maxima(4)
        pool_lo(2)
        dve.wait_ge(pair_filled, filled["sp"])
        nc.vector.tensor_copy(dprobT[:, :], pair[0][:, 0, 0:HD]).then_inc(evacuated, 1)
        normalise(4)
        for i in range(3, 2 * QT):
            out_lo(i)
            if i + 1 < 2 * QT:
                out_probT(i + 1)
            if i + 2 < 2 * QT:
                maxima(i + 2)
            if i == 3:
                pool_mean(3)
            if i + 2 < 2 * QT:
                normalise(i + 2)
            if i == 4:
                pool_lo(3)
            if i == 5:
                dve.wait_ge(dohi_ready, 1)
                for g in range(KVH):
                    rows = slice(g * HD, (g + 1) * HD)
                    last = nc.vector.tensor_tensor(
                        mlo[rows, NG:NG + GQ, SEQ:NOUT],
                        pair[0][rows, g, 0:NDEC * GQ].rearrange("p (b j) -> p j b", b=NDEC),
                        mhi[rows, NG:NG + GQ, SEQ:NOUT].bitcast(F32), ALU.subtract)
                last.then_inc(evacuated, 1)

        for d in range(KD):
            dve.wait_ge(unit_done, U_OUT + d + 1)
            x_d = halves(xT[:, d, META:NT], NH_OUT)
            nc.vector.tensor_tensor(x_d, pair[d % 2][:, :, 0:NH_OUT], x_d, ALU.add).then_inc(evacuated, 1)
            split_lo(U_OUT + d + 2)
            x_lo(d, 2, META, NH_OUT, 2 * KD)
        invert(7, rstd, META, NH_OUT)
        dve.wait_ge(inv_ready, 8)
        dve.wait_ge(mix_sent, 16 * 9)
        ffn_vector(STAGES[1], True)

    @block.gpsimd
    def _(pool):
        def square(d, e0, c0, n, done, it=None):
            pool.wait_ge(evacuated, up_to(e0 + d + 1, 1, it))
            x_d = tile(xT, d, it, c0, 2 * n, 1)
            nc.gpsimd.tensor_tensor(sq[:, c0:c0 + 2 * n], x_d, x_d, ALU.mult).then_inc(sq_ready, 1)
            pool.wait_ge(sq_ready, up_to(done + d + 1, 1, it))
            nc.gpsimd.tensor_tensor(sqsum[:, c0:c0 + 2 * n], sqsum[:, c0:c0 + 2 * n], sq[:, c0:c0 + 2 * n],
                                    ALU.add).then_inc(sqsum_ready, 1)
            pool.wait_ge(sqsum_ready, up_to(done + d + 1, 1, it))

        nc.gpsimd.memset(sqsum[:, :], 0.0).then_inc(sqsum_zero, 1)
        pool.wait_ge(sqsum_zero, 1)
        with pool.Fori(0, KD) as it:
            square(0, E_B1, 0, NH_ALL, 0, it)
        pool.wait_ge(unit_done, U_IN)
        nc.gpsimd.memset(kT[:, 0:PAD], 0.0).then_inc(pads_zero, 1)
        nc.gpsimd.memset(vT[:, 0:PAD], 0.0).then_inc(pads_zero, 1)
        nc.gpsimd.memset(up[:, :, 0:16], 0.0).then_inc(pads_zero, 1)
        nc.gpsimd.memset(wsum[:, :, 0:16], 0.0).then_inc(pads_zero, 1)
        pool.wait_ge(nsum_filled, 2)
        nc.gpsimd.memset(sqsum[:, :], 0.0).then_inc(sqsum_zero, 1)
        pool.wait_ge(mixin_loaded, 16 * 6)
        for x in range(5):
            cols = slice(0 if x == 0 else META, NT)
            pool.wait_ge(zg_ready, x + 1)
            if x:
                pool.wait_ge(qk_ready, x)
            nc.gpsimd.tensor_tensor(hid[:, cols], zg[:, x % 2, cols], cosT[:, cols], ALU.mult
                                    ).then_inc(cos_ready, 1)
            pool.wait_ge(cos_ready, x + 1)
            pool.wait_ge(sin_ready, x + 1)
            nc.gpsimd.tensor_tensor(hid[:, cols], hid[:, cols], sq[:, cols], ALU.add).then_inc(rot_ready, 1)
        pool.wait_ge(pads_zero, 4)
        done = 0
        for g in range(NG):
            pool.wait_ge(evacuated, E_USE[f"u{g}"] + 1)
            if g:
                pool.wait_ge(pooled, g)
            src = up[:, g % 2, :]
            for s in range(g + 1):
                dst = wsum[:, (2 * g - s) % 2, :]
                nc.gpsimd.tensor_tensor(dst[:, 16:16 + TP], src[:, 16:16 + TP],
                                        src[:, 16 - (1 << s):16 + TP - (1 << s)], ALU.add).then_inc(summed, 1)
                done += 1
                pool.wait_ge(summed, done)
                src = dst
        pool.wait_ge(sqsum_zero, 2)
        with pool.Fori(0, KD) as it:
            square(0, E_OUT, META, NH_OUT, KD, it)

    ctx.close()


def constants():
    eye = np.eye(P, dtype=np.float32)
    headsum = np.kron(np.eye(P // HD), np.ones((HD, HD))).astype(np.float32)
    swap = np.zeros((P, P), np.float32)
    half = ROPE // 2
    for h in range(0, P, HD):
        for i in range(half):
            swap[h + i, h + half + i] = swap[h + half + i, h + i] = 1
    i, j = np.arange(P)[:, None], np.arange(2 * P)[None, :]
    band = (j > i) & (j <= i + WIN)
    masks = [np.where(m, 0.0, NEG).astype(np.float32) for m in (band & (j >= PAD), band)]
    pos = np.concatenate([np.arange(TP), np.full(NDEC, PAST)]).astype(np.float32)
    freq = np.exp(np.float32(-math.log(500000.0)) * np.arange(half, dtype=np.float32) * np.float32(2.0 / ROPE))
    ang = (pos[None, :] * freq.astype(np.float32)[:, None]).astype(np.float64)
    cos, sin = np.ones((P, NT), np.float32), np.zeros((P, NT), np.float32)
    for h in range(0, P, HD):
        for b, sign in ((0, -1), (half, 1)):
            cos[h + b:h + b + half] = np.cos(ang)
            sin[h + b:h + b + half] = sign * np.sin(ang)
    return {"const": np.concatenate([eye, headsum, swap, *masks], 1), "cos": cos, "sin": sin}


def kernel(**inputs):
    import numpy as _np
    import concourse.bacc as _bacc
    from concourse import mybir as _mybir
    from concourse.bass_utils import run_bass_kernel_spmd as _run

    nc = _bacc.Bacc("TRN2", target_bir_lowering=False, num_devices=1)
    one = lambda name, shape: _np.ascontiguousarray(_np.asarray(inputs[name]).reshape(shape))
    given = {
        "xp": one("x_prompt", (SEQ, D)), "xs": one("x_sample", (NDEC, D)), "meta": one("meta_tokens", (META, D)),
        "state": one("state_pool", (NDEC, STATE, POOLW)),
        "ck": one("cache_k", (NDEC, WIN, P)), "cv": one("cache_v", (NDEC, WIN, P)),
        "n1": one("ffn1_norm", (KD, P)), "g1": one("ffn1_w_gate", (D, F)), "u1": one("ffn1_w_up", (D, F)),
        "d1": one("ffn1_w_down", (F, D)),
        "nm": one("mix_norm", (KD, P)), "w_in": one("w_in", (D, 2 * POOLW + 2 * P)),
        "qn": one("q_norm", (1, HD)), "kn": one("k_norm", (1, HD)), "sinks": one("attn_sinks", (1, HEADS)),
        "pool_w": one("pool_w", (NG, P, P)), "pool_scale": one("pool_scale", (NG, P)),
        "w_out": one("w_out", (D, D)),
        "n2": one("ffn2_norm", (KD, P)), "g2": one("ffn2_w_gate", (D, F)), "u2": one("ffn2_w_up", (D, F)),
        "d2": one("ffn2_w_down", (F, D)),
    } | constants()
    outs = {"o_y": (SEQ, D), "o_ysm": (NDEC, D), "o_pp": (STATE, POOLW), "o_kp": (WIN, P), "o_vp": (WIN, P),
            "o_ps": (NDEC, STATE, POOLW), "o_ks": (NDEC, WIN, P), "o_vs": (NDEC, WIN, P)}
    f32 = _mybir.dt.float32
    a = {n: nc.dram_tensor(n, v.shape, f32, kind="ExternalInput").ap() for n, v in given.items()}
    a |= {n: nc.dram_tensor(n, v, f32, kind="ExternalOutput").ap() for n, v in outs.items()}
    build(nc, a)
    r = _run(nc, [given], core_ids=[0]).results[0]
    return (r["o_y"].reshape(1, SEQ, D), r["o_ysm"].reshape(NDEC, 1, D), r["o_pp"].reshape(1, 1, STATE, POOLW),
            r["o_kp"].reshape(1, 1, WIN, KVH, HD), r["o_vp"].reshape(1, 1, WIN, KVH, HD),
            r["o_ps"].reshape(1, NDEC, STATE, POOLW), r["o_ks"].reshape(1, NDEC, WIN, KVH, HD),
            r["o_vs"].reshape(1, NDEC, WIN, KVH, HD))
```

```python
import math
from contextlib import ExitStack

import numpy as np

import concourse.bass as bass
from concourse import mybir

ALU = mybir.AluOpType
ACT = mybir.ActivationFunctionType
F32 = mybir.dt.float32
F32R = mybir.dt.float32r
BF16 = mybir.dt.bfloat16
AX = mybir.AxisListType.X

P = 128
D = 1024
KD = D // P
F = 2816
KF = F // P
META, SEQ, NDEC = 16, 512, 8
TP = META + SEQ
NT = TP + NDEC
NH_ALL = NT // 2
NOUT = SEQ + NDEC
NH_OUT = NOUT // 2
HD = 64
HEADS, KVH = 8, 2
GQ = HEADS // KVH
WIN = 128
POOLW = 512
NG = 4
WINDOWS = (2, 4, 8, 16)
STATE = 15
BLKS = 6
PAD = (-META) % P
NBLK = (PAD + TP) // P
QT = SEQ // P
PAST = 4096
ROPE = HD // 4
EPS = 1e-6
SCALE = HD ** -0.5
NEG = -1e30

G_POOL, G_Q, G_K = 3 * KD, 3 * KD + NG, 3 * KD + NG + 1
N_GAIN = G_K + 1
C_SINK = N_GAIN
C_DSINK = C_SINK + HEADS
C_IDENT = C_DSINK + 1
N_FIXED = C_IDENT + P
RAW = 4
DOWN_T = KF // 2
A_UNITS, B_UNITS, IN_UNITS, OUT_UNITS = 2 * KF, 2 * KD, 10, KD
U_A1 = 0
U_B1 = U_A1 + A_UNITS
U_IN = U_B1 + B_UNITS
U_OUT = U_IN + IN_UNITS
U_A2 = U_OUT + OUT_UNITS
U_B2 = U_A2 + A_UNITS
U_END = U_B2 + B_UNITS

MIX = ["k", "v", "q0", "q1", "q2", "q3", "u0", "u1", "u2", "u3"]
PAIR_USES = ["k", "v", "q0", "q1", "q2", "q3", "u0", "u1", "ss", "sr", "P0", "u2", "P1",
             "u3", "sp", "P2", "so", "P3"]
PAIR1 = {"v", "q1", "q3"}
NORM_AT = (1, 2, 5)
POOL_SQ = 3
SQSUM_AT = (POOL_SQ, POOL_SQ + KD, POOL_SQ + 2 * KD)


def tiles_of(u):
    down = U_B1 <= u < U_IN or U_B2 <= u < U_END
    return DOWN_T if down else KD


def build(nc, a):
    ctx = ExitStack()
    at = [0]

    base = (nc.sbuf_base + 31) // 32 * 32
    ARENA = (nc.sbuf_usable_end - base) // 32 * 32 - 32
    ctx.enter_context(nc.sbuf_tensor("arena", [P, ARENA // 4], F32))

    def place(name, shape, dt=F32, offset=None):
        size = int(np.prod(shape[1:])) * (2 if dt == BF16 else 4)
        size = (size + 31) // 32 * 32
        o = at[0] if offset is None else offset
        if offset is None:
            at[0] += size
            assert at[0] <= ARENA, (name, at[0])
        return nc.alloc_sbuf_tensor_at(name, list(shape), dt, offset=base + o), o + size

    xT, _ = place("xT", [P, KD, NT])
    xhi_at = at[0]
    xhi, _ = place("xhi", [P, KD, NT], F32R)
    xlo, _ = place("xlo", [P, KD, NT], F32R)
    h_at = at[0]
    hhi, _ = place("hhi", [P, KF, NT], F32R)
    hlo, _ = place("hlo", [P, KF, NT], F32R)
    h_end = at[0]
    raw, _ = place("raw", [P, RAW, DOWN_T, P])
    whi, _ = place("whi", [P, 2, DOWN_T, P], F32R)
    wlo, _ = place("wlo", [P, 2, DOWN_T, P], F32R)
    rstd, _ = place("rstd", [P, NT])
    gate, _ = place("gate", [P, NT])
    act_gate, _ = place("act_gate", [P, NT])
    hid, _ = place("hid", [P, NT])
    sq, _ = place("sq", [P, NT])
    sqsum, _ = place("sqsum", [P, NT])
    fixed, _ = place("fixed", [P, N_FIXED])
    ones, _ = place("ones", [P, 1])
    headsel, _ = place("headsel", [P, 2])
    nrm, _ = place("nrm", [P, 2, 2 * BLKS])
    qnrm, _ = place("qnrm", [P, 2, GQ * QT * KVH])
    dnrm, _ = place("dnrm", [HD, 2])
    eps64, _ = place("eps64", [P, 1])
    swap, _ = place("swap", [P, P])
    identb, _ = place("identb", [P, P], BF16)
    maskb, _ = place("maskb", [P, 2, 2 * P], BF16)
    eps, _ = place("eps", [P, 1])
    dsum, _ = place("dsum", [P, NDEC])
    small, _ = place("small", [P, 2, 32])
    nsink, _ = place("nsink", [P, HEADS + 1])
    gains, sink, ident = fixed[:, 0:N_GAIN], fixed[:, C_SINK:C_DSINK], fixed[:, C_IDENT:N_FIXED]
    dsink, ndsink = fixed[0:HD, C_DSINK:C_IDENT], nsink[0:HD, HEADS:HEADS + 1]
    o = h_at
    maskf, o = place("maskf", [P, 2, 2 * P], offset=o)
    sqx, o = place("sqx", [P, KD, NT], offset=o)
    o = h_at
    cosT, o = place("cosT", [P, NT], offset=o)
    sinT, o = place("sinT", [P, NT], offset=o)
    ckT, o = place("ckT", [P, NDEC, P], offset=o)
    cv, o = place("cv", [P, NDEC, P], offset=o)
    stT, o = place("stT", [P, NG, NDEC, STATE + 1], offset=o)
    poolw, o = place("poolw", [P, NG, P], offset=o)
    qT, o = place("qT", [P, GQ, NOUT], offset=o)
    kT, o = place("kT", [P, PAD + NT], offset=o)
    vT, o = place("vT", [P, PAD + NT], offset=o)
    tok, o = place("tok", [P, (NBLK + 1) * P], offset=o)
    mhi, o = place("mhi", [P, KD, NOUT], F32R, offset=o)
    mlo, o = place("mlo", [P, KD, NOUT], F32R, offset=o)
    ulast, o = place("ulast", [P, NG, STATE], offset=o)
    up, o = place("up", [P, 2, 16 + NT], offset=o)
    wsum, o = place("wsum", [P, 2, 16 + NT], offset=o)
    knrm, _ = place("knrm", [P, BLKS, P], offset=o)
    dscore, _ = place("dscore", [HD, P], offset=o)
    probT, o = place("probT", [P, 2, GQ * P], offset=o)
    dscoreT, _ = place("dscoreT", [P, HD], offset=o)
    dprobT, o = place("dprobT", [P, HD], offset=o)
    dprob, o = place("dprob", [HD, P], offset=o)
    dout, o = place("dout", [P, NDEC, GQ], offset=o)
    dsmall, o = place("dsmall", [HD, 8], offset=o)
    dzsq, o = place("dzsq", [P, NDEC, GQ], offset=o)
    prob_at = o
    zg, o = place("zg", [P, 2, NT], offset=prob_at)
    zsq, o = place("zsq", [P, 2, NT], offset=o)
    prob, _ = place("prob", [P, 2, GQ, 2 * P], offset=prob_at)
    assert o <= h_end, (o, h_end)
    ybuf, _ = place("ybuf", [P, 2, NOUT], offset=xhi_at)
    pooled_out = act_gate[:, 0:NOUT]

    ps = ctx.enter_context(nc.psum_tensor("ps", [P, 8, 512], F32))
    pair = [ps[:, 0:2, :], ps[:, 2:4, :]]
    nsum = ps[:, 4:6, :]
    turn = ps[:, 6:8, :]
    scorebank = [ps[:, 2:4, :], ps[:, 4:6, :]]

    def sem(name):
        return ctx.enter_context(nc.semaphore(name))

    x_loaded = [sem(f"x_loaded{k}") for k in range(KD)]
    fixed_loaded = sem("fixed_loaded")
    mixin_loaded = sem("mixin_loaded")
    raw_loaded = [sem(f"raw_loaded{r}") for r in range(RAW)]
    whi_ready = sem("whi_ready")
    wlo_ready = sem("wlo_ready")
    unit_done = sem("unit_done")
    evacuated = sem("evacuated")
    consts_made = sem("consts_made")
    masks_loaded = sem("masks_loaded")
    masks_made = sem("masks_made")
    spread = sem("spread")
    rstd_ready = sem("rstd_ready")
    xhi_ready = sem("xhi_ready")
    xlo_ready = sem("xlo_ready")
    sq_ready = sem("sq_ready")
    sqx_ready = sem("sqx_ready")
    sqx_summed = sem("sqx_summed")
    sqsum_ready = sem("sqsum_ready")
    sqsum_zero = sem("sqsum_zero")
    nsum_filled = sem("nsum_filled")
    root_ready = sem("root_ready")
    inv_ready = sem("inv_ready")
    tok_filled = sem("tok_filled")
    silu_ready = sem("silu_ready")
    silu_scaled = sem("silu_scaled")
    hhi_ready = sem("hhi_ready")
    hlo_ready = sem("hlo_ready")
    zg_ready = sem("zg_ready")
    rot_filled = sem("rot_filled")
    cos_ready = sem("cos_ready")
    sin_ready = sem("sin_ready")
    rot_ready = sem("rot_ready")
    qk_ready = sem("qk_ready")
    pads_zero = sem("pads_zero")
    tok_ready = sem("tok_ready")
    newv_placed = sem("newv_placed")
    pair_filled = sem("pair_filled")
    summed = sem("summed")
    pooled = sem("pooled")
    phi_ready = sem("phi_ready")
    plo_ready = sem("plo_ready")
    step = sem("step")
    newk_placed = sem("newk_placed")
    scored = sem("scored")
    nmax_ready = sem("nmax_ready")
    exp_ready = sem("exp_ready")
    prob_ready = sem("prob_ready")
    probs_turned = sem("probs_turned")
    probT_a = sem("probT_a")
    probT_b = sem("probT_b")
    attended = sem("attended")
    ohi_ready = sem("ohi_ready")
    olo_ready = sem("olo_ready")
    dnmax_ready = sem("dnmax_ready")
    dexp_ready = sem("dexp_ready")
    dprob_ready = sem("dprob_ready")
    dohi_ready = sem("dohi_ready")
    dolo_ready = sem("dolo_ready")
    y_sent = [sem("y_sent0"), sem("y_sent1")]
    mix_sent = sem("mix_sent")

    E_A1 = 0
    E_B1 = E_A1 + 2 * KF
    E_MIX = E_B1 + KD
    E_OUT = E_MIX + len(PAIR_USES)
    E_A2 = E_OUT + KD
    E_B2 = E_A2 + 2 * KF
    pair_of = {u: int(u in PAIR1) for u in PAIR_USES}
    extra = [u for u in PAIR_USES if u not in MIX]
    E_USE = {u: E_MIX + i for i, u in enumerate(PAIR_USES)}
    before = {}
    for i, u in enumerate(PAIR_USES):
        prev = [v for v in PAIR_USES[:i] if pair_of[v] == pair_of[u]]
        before[u] = E_USE[prev[-1]] + 1 if prev else E_MIX - 1 + pair_of[u]
    filled = {u: i + 1 for i, u in enumerate(extra)}
    summed_at = {0: 1, 1: 3, 2: 6, 3: 10}

    def up_to(const, slope=0, it=None):
        return const if it is None else const + it * slope

    STAGES = [dict(ua=U_A1, ub=U_B1, ea=E_A1, eb=E_B1, c0=0, n=NH_ALL, f0=0, x0=0, w=(0, 1)),
              dict(ua=U_A2, ub=U_B2, ea=E_A2, eb=E_B2, c0=META, n=NH_OUT, f0=KF, x0=2 * KD, w=(2, 3))]

    def blocks(c0, n):
        return [(h, o) for h in range(2) for o in (0, P, n - P)]

    def halves(tile2d, n):
        return tile2d.rearrange("p (s n) -> p s n", n=n)

    def tile(t, d, it, c0, w, step=2):
        if it is None:
            return t[:, d, c0:c0 + w]
        return t[:, :, :].rearrange("p k n -> p (k n)")[:, bass.ds((it * step + d) * NT + c0, w)]

    def gain(g, d, it):
        if it is None:
            return gains[:, g * KD + d:g * KD + d + 1]
        return gains[:, bass.ds(it * 2 + g * KD + d, 1)]

    def qscale(i, j=None):
        t, g = divmod(i, KVH)
        if j is not None:
            c = (j * QT + t) * KVH + g
            return qnrm[:, 1, c:c + 1]
        return qnrm[:, 1, :].rearrange("p (j t g) -> p j t g", j=GQ, t=QT)[:, :, t, g]

    block = ctx.enter_context(nc.Block())

    @block.sync
    def _(sp):
        def free(c, it=None):
            if c >= RAW:
                sp.wait_ge(wlo_ready, up_to(c - RAW + 1, RAW, it))

        def load(c, src, u, it=None, slope=RAW):
            free(c, it)
            w = tiles_of(c) * P
            at = u * w if it is None else (it * slope + u) * w
            sp.dma_start(raw[:, c % RAW, 0:tiles_of(c), :].rearrange("p t c -> p (t c)"),
                         src[:, bass.ds(at, w)]).then_inc(raw_loaded[c % RAW], 16)

        def ffn(s, first):
            for u in range(first, RAW):
                load(s["ua"] + u, s["gate_up_w"], u)
            with sp.Fori(0, A_UNITS // RAW - 1) as it:
                for u in range(RAW, 2 * RAW):
                    load(s["ua"] + u, s["gate_up_w"], u, it)
            with sp.Fori(0, B_UNITS // RAW) as it:
                for u in range(RAW):
                    load(s["ub"] + u, s["down_w"], u, it)

        for s, i in zip(STAGES, (1, 2)):
            s.update(gate_up_w=a[f"gu{i}"], down_w=a[f"d{i}"])
        load(0, a["gu1"], 0)
        for k in range(KD):
            sp.dma_start(xT[:, k, :], a["x"][:, k, :]).then_inc(x_loaded[k], 16)
        ffn(STAGES[0], 1)

        for m in range(4):
            load(U_IN + m, a["w_in"], m)
        sp.wait_ge(unit_done, U_IN)
        for dst, src in ((cosT[:], a["cos"]), (sinT[:], a["sin"]), (ckT[:], a["ck"]), (cv[:], a["cv"]),
                         (stT[:], a["state"]), (poolw[:], a["pool_w"])):
            sp.dma_start(dst, src).then_inc(mixin_loaded, 16)
        for m in range(4, IN_UNITS):
            load(U_IN + m, a["w_in"], m)
        load(U_OUT, a["w_out"], 0)
        sp.wait_ge(qk_ready, 1)
        last = slice(PAD + TP - WIN, PAD + TP)
        sp.dma_start(a["o_kp"], kT[:, last]).then_inc(mix_sent, 16)
        sp.dma_start(a["o_vp"], vT[:, last]).then_inc(mix_sent, 16)
        sp.wait_ge(newk_placed, 1)
        sp.dma_start(a["o_ks"], ckT[:]).then_inc(mix_sent, 16)
        sp.wait_ge(tok_ready, 2)
        sp.wait_ge(mixin_loaded, 16 * 6)
        for b in range(NDEC):
            sp.dma_start(cv[WIN - 1:WIN, b, :], tok[b:b + 1, NBLK * P:(NBLK + 1) * P]).then_inc(newv_placed, 16)
        load(U_OUT + 1, a["w_out"], 1)
        sp.wait_ge(newv_placed, 16 * NDEC)
        sp.dma_start(a["o_vs"], cv[:]).then_inc(mix_sent, 16)
        for d in range(2, KD):
            load(U_OUT + d, a["w_out"], d)
        sp.wait_ge(pooled, NG)
        sp.dma_start(a["o_pp"], ulast[:]).then_inc(mix_sent, 16)
        sp.dma_start(a["o_ps"], stT[:]).then_inc(mix_sent, 16)
        ffn(STAGES[1], 0)
        sp.wait_ge(mix_sent, 16 * 6)

    @block.tensor
    def _(pe):
        def product(c, it, slope, dst, tiles, hi, lo, k0, kall, c0, n, wait_k=None, ks=None):
            if ks is None or ks[0] == 0:
                pe.wait_ge(wlo_ready, up_to(c + 1, slope, it))
            for kk in ks or range(tiles):
                k = k0 + kk
                if wait_k:
                    wait_k(k)
                for w, x in ((whi, hi), (whi, lo), (wlo, hi)):
                    for s in range(2):
                        last = nc.tensor.matmul(
                            dst[:, s, 0:n], w[:, c % 2, kk, :], x[:, k, c0 + s * n:c0 + (s + 1) * n],
                            start=(k == 0 and w is whi and x is hi), stop=(k == kall - 1 and w is wlo))
            if not ks or ks[-1] == tiles - 1:
                last.then_inc(unit_done, 1)

        flat = nsum.rearrange("p s n -> p (s n)")

        def norm_sums(i, c0, n):
            pe.wait_ge(sqsum_ready, SQSUM_AT[i])
            if i == 0:
                pe.wait_ge(sqx_summed, KD - POOL_SQ - 1)
            for b, (h, o) in enumerate(blocks(c0, n)):
                col = c0 + h * n + o
                last = nc.tensor.matmul(nsum[:, 0, b:b + 1], sqsum[:, col:col + P], ones[:, :],
                                        start=True, stop=(i > 0))
                if i == 0:
                    last = nc.tensor.matmul(nsum[:, 0, b:b + 1], sqx[:, KD - 1, col:col + P], ones[:, :],
                                            start=False, stop=True)
            last.then_inc(nsum_filled, 1)

        def norm_spread(i, c0, n, inv):
            pe.wait_ge(inv_ready, inv)
            for b, (h, o) in enumerate(blocks(c0, n)):
                last = nc.tensor.transpose(nsum[:, h, o:o + P], nrm[:, 1, b:b + 1].to_broadcast([P, P]), ident[:, :])
            last.then_inc(spread, 1)

        def ffn_products(s, second):
            ua, ub, ea, eb, c0, n = (s[x] for x in ("ua", "ub", "ea", "eb", "c0", "n"))

            def gate_or_up(j, it, ks=None, f=0, wait_k=None):
                if (ks is None or ks[0] == 0) and ea + 2 * f + j > 1:
                    pe.wait_ge(evacuated, up_to(ea + 2 * f + j - 1, 2, it))
                product(ua + 2 * f + j, it, 2, pair[j], KD, xhi, xlo, 0, KD, c0, n, wait_k, ks)

            def x_there(k):
                pe.wait_ge(xlo_ready, s["x0"] + k + 1)

            if second:
                gate_or_up(0, None, [0, 1, 2, 3, 4, 5], wait_k=x_there)
                norm_sums(2, c0, n)
                gate_or_up(0, None, [6, 7], wait_k=x_there)
                norm_spread(2, c0, n, 5)
                gate_or_up(1, None)
            else:
                gate_or_up(0, None, wait_k=x_there)
                gate_or_up(1, None, [0, 1, 2])
                norm_sums(0, c0, n)
                gate_or_up(1, None, [3, 4])
                norm_spread(0, c0, n, 1)
                gate_or_up(1, None, [5, 6, 7])
            with pe.Fori(0, KF - 1) as it:
                gate_or_up(0, it, f=1)
                gate_or_up(1, it, f=1)

            def down(d, it):
                for j in range(2):
                    if j == 0:
                        pe.wait_ge(evacuated, up_to(eb + d - 1, 2, it))

                    def h_there(k):
                        if k in (0, KF - 1):
                            pe.wait_ge(hlo_ready, s["f0"] + KF - (k == 0))
                    product(ub + 2 * d + j, it, 4, pair[d % 2], DOWN_T, hhi, hlo, j * DOWN_T, KF, c0, n, h_there)

            with pe.Fori(0, KD // 2) as it:
                down(0, it)
                down(1, it)

        ffn_products(STAGES[0], False)

        def project(m, ks=None, wait_k=None):
            name = MIX[m]
            if ks is None or ks[0] == 0:
                pe.wait_ge(evacuated, before[name])
            q = name[0] == "q"
            product(U_IN + m, None, 0, pair[pair_of[name]], KD, xhi, xlo, 0, KD,
                    META if q else 0, NH_OUT if q else NH_ALL, wait_k, ks)

        def rotated(x):
            c0, n = (0, NH_ALL) if x == 0 else (META, NH_OUT)
            pe.wait_ge(zg_ready, x + 1)
            if x >= 1:
                pe.wait_ge(sin_ready, x)
            for s in range(2):
                last = nc.tensor.matmul(turn[:, s, 0:n], swap[:, :], zg[:, x % 2, c0 + s * n:c0 + (s + 1) * n],
                                        start=True, stop=True)
            last.then_inc(rot_filled, 1)

        def k_sums():
            pe.wait_ge(zg_ready, 1)
            pe.wait_ge(rstd_ready, 2)
            for b, (h, o) in enumerate(blocks(0, NH_ALL)):
                col = h * NH_ALL + o
                last = nc.tensor.matmul(nsum[:, 0, 2 * b:2 * b + 2], zsq[:, 0, col:col + P], headsel[:, :],
                                        start=True, stop=True)
            last.then_inc(nsum_filled, 1)

        def k_spread():
            pe.wait_ge(inv_ready, 3)
            for b, (h, o) in enumerate(blocks(0, NH_ALL)):
                src = knrm[:, b, :]
                last = nc.tensor.transpose(nsum[:, h, o:o + P], src, ident[:, :])
            last.then_inc(spread, 1)

        def q_sums(j):
            if j == 0:
                pe.wait_ge(tok_ready, 2)
            pe.wait_ge(zg_ready, j + 2)
            for t in range(QT):
                c = (j * QT + t) * KVH
                nc.tensor.matmul(nsum[:, 0, c:c + KVH], zsq[:, (j + 1) % 2, META + t * P:META + (t + 1) * P],
                                 headsel[:, :], start=True, stop=True)
            if j == GQ - 1:
                for g in range(KVH):
                    rows = slice(g * HD, (g + 1) * HD)
                    last = nc.tensor.matmul(nsum[g * NDEC * GQ:(g + 1) * NDEC * GQ, 1, 0:1], dzsq[rows, :, :],
                                            headsel[rows, g:g + 1], start=True, stop=True)
                last.then_inc(nsum_filled, 1)

        def x_there(k):
            pe.wait_ge(xlo_ready, KD + k + 1)

        half = [[0, 1, 2, 3], [4, 5, 6, 7]]
        project(0, [0, 1, 2, 3, 4, 5], x_there)
        norm_sums(1, 0, NH_ALL)
        project(0, [6, 7], x_there)
        norm_spread(1, 0, NH_ALL, 2)
        project(1)
        k_sums()
        rotated(0)
        project(2, half[0])
        k_spread()
        project(2, half[1])
        project(3, half[0])
        pe.wait_ge(qk_ready, 1)
        pe.wait_ge(evacuated, E_USE["v"] + 1)
        pe.wait_ge(pads_zero, 2)
        for b in range(NBLK):
            nc.tensor.transpose(flat[:, b * P:(b + 1) * P], vT[:, b * P:(b + 1) * P], ident[:, :])
        nc.tensor.transpose(flat[0:NDEC, NBLK * P:(NBLK + 1) * P], vT[:, PAD + TP:PAD + NT], ident[:, :]
                            ).then_inc(tok_filled, 1)
        project(3, half[1])
        project(4, half[0])
        q_sums(0)
        rotated(1)
        project(4, half[1])
        project(5, half[0])
        q_sums(1)
        rotated(2)
        project(5, half[1])
        project(6, half[0])
        q_sums(2)
        rotated(3)
        project(6, half[1])

        def use(name):
            pe.wait_ge(evacuated, before[name])
            return pair[pair_of[name]]

        def pool_map(g):
            dst = use(f"P{g}")
            pe.wait_ge(pooled, g + 1)
            for s in range(2):
                last = nc.tensor.matmul(dst[:, s, 0:NH_OUT], poolw[:, g, :], gate[:, s * NH_OUT:(s + 1) * NH_OUT],
                                        start=True, stop=True)
            last.then_inc(pair_filled, 1)

        def scores(i):
            t, g = divmod(i, 2)
            rows = slice(g * HD, (g + 1) * HD)
            if i < 2:
                pe.wait_ge(masks_made, 1)
                pe.wait_ge(rot_ready, 5)
                pe.wait_ge(root_ready, 4)
                pe.wait_ge(evacuated, E_USE["q3"] + 1)
            else:
                pe.wait_ge(exp_ready, i - 1)
            for j in range(GQ):
                dst = scorebank[i % 2][:, j // 2, (j % 2) * 2 * P:(j % 2 + 1) * 2 * P]
                nc.tensor.matmul(dst, identb[:, :], maskb[:, min(t, 1), :], start=(j % 2 == 0), stop=False,
                                 skip_group_check=True)
                last = nc.tensor.matmul(dst, qT[rows, j, t * P:(t + 1) * P], kT[rows, t * P:(t + 2) * P],
                                        start=False, stop=True, skip_group_check=True)
            last.then_inc(scored, 1)

        def turn_probs(i):
            pe.wait_ge(prob_ready, i + 1)
            if i == 0:
                pe.wait_ge(sin_ready, 5)
            else:
                pe.wait_ge(olo_ready, i)
            for b in range(2):
                for j in range(GQ):
                    last = nc.tensor.transpose(turn[:, b, j * P:(j + 1) * P], prob[:, i % 2, j, b * P:(b + 1) * P],
                                               ident[:, :])
            last.then_inc(probs_turned, 1)

        def attend(i):
            t, g = divmod(i, 2)
            rows = slice(g * HD, (g + 1) * HD)
            pe.wait_ge(probT_a, i + 1)
            pe.wait_ge(probT_b, i + 1)
            for b in range(2):
                last = nc.tensor.matmul(turn[rows, 0, :],
                                        tok[:, (t + b) * P + g * HD:(t + b) * P + (g + 1) * HD],
                                        probT[:, b, :], start=(b == 0), stop=(b == 1))
            last.then_inc(attended, 1)

        def decode_scores():
            dst = use("ss")
            pe.wait_ge(newk_placed, 1)
            for g in range(KVH):
                rows = slice(g * HD, (g + 1) * HD)
                for b in range(NDEC):
                    last = nc.tensor.matmul(dst[:, g, b * GQ:(b + 1) * GQ], ckT[rows, b, :],
                                            qT[rows, :, SEQ + b], start=True, stop=True)
            last.then_inc(pair_filled, 1)

        def decode_turn():
            dst = use("sr")
            pe.wait_ge(evacuated, E_USE["ss"] + 1)
            nc.tensor.transpose(dst[0:HD, 0, 0:P], dscoreT[:, :], ident[:, :]).then_inc(pair_filled, 1)

        def decode_turn_back():
            dst = use("sp")
            pe.wait_ge(dprob_ready, 1)
            nc.tensor.transpose(dst[:, 0, 0:HD], dprob[:, :], ident[0:HD, 0:HD]).then_inc(pair_filled, 1)

        def decode_attend():
            dst = use("so")
            pe.wait_ge(evacuated, E_USE["sp"] + 1)
            pe.wait_ge(newv_placed, 16 * NDEC)
            for g in range(KVH):
                rows = slice(g * HD, (g + 1) * HD)
                for b in range(NDEC):
                    c = (g * NDEC + b) * GQ
                    last = nc.tensor.matmul(dst[rows, g, b * GQ:(b + 1) * GQ], cv[:, b, rows],
                                            dprobT[:, c:c + GQ], start=True, stop=True)
            last.then_inc(pair_filled, 1)

        project(7, half[0])
        q_sums(3)
        rotated(4)
        project(7, half[1])
        scores(0)
        decode_scores()
        scores(1)
        decode_turn()
        pool_map(0)
        project(8)

        def out_product(d, ks):
            def mixed_there(k):
                if k == 0:
                    pe.wait_ge(plo_ready, NG)
                if k == NG and d == 0:
                    pe.wait_ge(dolo_ready, 1)
                    pe.wait_ge(olo_ready, 2 * QT)
            if d == 0 and ks[0] == 0:
                pe.wait_ge(evacuated, E_OUT)
            elif d >= 2:
                pe.wait_ge(evacuated, E_OUT + d - 1)
            product(U_OUT + d, None, 0, pair[d % 2], KD, mhi, mlo, 0, KD, 0, NH_OUT, mixed_there, ks)

        for i in range(2 * QT):
            turn_probs(i)
            if i + 2 < 2 * QT:
                scores(i + 2)
            attend(i)
            if i == 0:
                pool_map(1)
            elif i == 1:
                project(9, half[0])
            elif i == 2:
                project(9, half[1])
            elif i == 3:
                decode_turn_back()
                pool_map(2)
            elif i == 4:
                decode_attend()
            elif i == 5:
                pool_map(3)
            elif i == 6:
                out_product(0, [0, 1, 2, 3])
        out_product(0, [4, 5, 6, 7])
        for d in range(1, KD):
            out_product(d, list(range(KD)))
        ffn_products(STAGES[1], True)

    @block.scalar
    def _(act):
        act.dma_start(fixed[:], a["fixed"]).then_inc(fixed_loaded, 16)

        def late_consts():
            act.dma_start(swap[:], a["const"][:, 0:P]).then_inc(masks_loaded, 16)
            act.dma_start(maskf[:], a["const"][:, P:5 * P]).then_inc(masks_loaded, 16)

        def split_hi(c, it=None, slope=4):
            t = tiles_of(c)
            act.wait_ge(raw_loaded[c % RAW], up_to(16 * (c // RAW + 1), slope // RAW * 16, it))
            if c >= 2:
                act.wait_ge(unit_done, up_to(c - 1, slope, it))
            nc.scalar.copy(whi[:, c % 2, 0:t, :], raw[:, c % RAW, 0:t, :]).then_inc(whi_ready, 1)

        def x_hi(d, g, c0, n, base, it=None):
            nc.scalar.activation(tile(xhi, d, it, c0, 2 * n), tile(xT, d, it, c0, 2 * n), ACT.Copy,
                                 scale=gain(g, d, it)).then_inc(xhi_ready, 1)

        def root(dst, src, mean, i):
            act.wait_ge(nsum_filled, i)
            return nc.scalar.activation(dst, src, ACT.Sqrt, scale=1.0 / mean, bias=eps[0:dst.shape[0], 0:1])

        def norm(i, c0, n):
            root(nrm[:, 0, 0:BLKS], nsum[:, 0, 0:BLKS], D, NORM_AT[i]).then_inc(root_ready, 1)
            act.wait_ge(spread, i + 1 + (i == 2))
            nc.scalar.copy(halves(rstd[:, c0:c0 + 2 * n], n), nsum[:, :, 0:n]).then_inc(rstd_ready, 1)

        act.wait_ge(fixed_loaded, 16)
        split_hi(0)
        for k in range(KD):
            act.wait_ge(x_loaded[k], 16)
            x_hi(k, 0, 0, NH_ALL, 0)
        split_hi(1)
        for k in range(POOL_SQ, KD):
            nc.scalar.activation(sqx[:, k, :], xT[:, k, :], ACT.Square).then_inc(sqx_ready, 1)
        act.wait_ge(consts_made, 2)
        norm(0, 0, NH_ALL)
        late_consts()

        def ffn_act(s, second):
            ua, ub, ea, eb, c0, n = (s[x] for x in ("ua", "ub", "ea", "eb", "c0", "n"))
            cols = slice(c0, c0 + 2 * n)

            def step_a(f, it=None):
                split_hi(ua + 2 * f + 2, it)
                act.wait_ge(evacuated, up_to(ea + 2 * f + 1, 4, it))
                nc.scalar.activation(act_gate[:, cols], gate[:, cols], ACT.Silu).then_inc(silu_ready, 1)
                split_hi(ua + 2 * f + 3, it)
                act.wait_ge(evacuated, up_to(ea + 2 * f + 2, 4, it))
                nc.scalar.copy(tile(hhi, f, it, c0, 2 * n), hid[:, cols]).then_inc(hhi_ready, 1)

            with act.Fori(0, KF // 2 - 1) as it:
                step_a(0, it)
                step_a(1, it)
            step_a(KF - 2)
            step_a(KF - 1)

            def step_b(d, it=None):
                if ub + 2 * d + 2 < U_END:
                    split_hi(ub + 2 * d + 2, it)
                    split_hi(ub + 2 * d + 3, it)
                if second:
                    act.wait_ge(evacuated, up_to(eb + d + 1, 2, it))
                    at = d * NOUT if it is None else (it * 2 + d) * NOUT
                    act.dma_start(a["o_y"][:, bass.ds(at, NOUT)], ybuf[:, d % 2, :]).then_inc(y_sent[d % 2], 16)
                else:
                    act.wait_ge(evacuated, up_to(eb + d + 1, 2, it))
                    x_hi(d, 1, c0, n, KD, it)

            with act.Fori(0, KD // 2 - 1) as it:
                step_b(0, it)
                step_b(1, it)
            step_b(KD - 2)
            step_b(KD - 1)

        ffn_act(STAGES[0], False)
        norm(1, 0, NH_ALL)

        def split_next(m):
            split_hi(U_IN + m + 2)

        def spread_z(x):
            c0, n = (0, NH_ALL) if x == 0 else (META, NH_OUT)
            act.wait_ge(evacuated, E_USE[MIX[x + (x > 0)]] + 1)
            if x >= 2:
                act.wait_ge(rot_filled, x - 1)
                act.wait_ge(cos_ready, x - 1)
            nc.scalar.activation(zg[:, x % 2, c0:c0 + 2 * n], gate[:, c0:c0 + 2 * n], ACT.Copy,
                                 scale=gains[:, G_Q + (x == 0):G_Q + (x == 0) + 1])
            sq_x = nc.scalar.activation(zsq[:, x % 2, c0:c0 + 2 * n], gate[:, c0:c0 + 2 * n], ACT.Square)
            if x:
                sq_x = nc.scalar.activation(dzsq[:, :, x - 1], gate[:, TP:NT], ACT.Square)
            sq_x.then_inc(zg_ready, 1)

        def exps(i):
            act.wait_ge(nmax_ready, i + 1)
            if i >= 2:
                act.wait_ge(probs_turned, i - 1)
            s = i % 2
            for j in range(GQ):
                nc.scalar.activation(prob[:, s, j, :], scorebank[s][:, j // 2, (j % 2) * 2 * P:(j % 2 + 1) * 2 * P],
                                     ACT.Exp, scale=qscale(i, j), bias=small[:, s, 4 + j:5 + j],
                                     accum_out=small[:, s, 12 + j:13 + j])
            nc.scalar.activation(small[:, s, 16:20], small[:, s, 8:12], ACT.Exp).then_inc(exp_ready, 1)

        def out_probT(i):
            act.wait_ge(probs_turned, i + 1)
            if i >= 1:
                act.wait_ge(attended, i)
            else:
                act.wait_ge(dexp_ready, 1)
            nc.scalar.copy(probT[:, 0, :], turn[:, 0, :]).then_inc(probT_a, 1)

        def out_hi(i):
            t, g = divmod(i, 2)
            rows = slice(g * HD, (g + 1) * HD)
            act.wait_ge(attended, i + 1)
            nc.scalar.copy(mhi[rows, NG:NG + GQ, t * P:(t + 1) * P],
                           turn[rows, 0, :].rearrange("p (j q) -> p j q", j=GQ)).then_inc(ohi_ready, 1)

        def pool_hi(g):
            act.wait_ge(evacuated, E_USE[f"P{g}"] + 1)
            nc.scalar.copy(mhi[:, g, :], pooled_out[:, :]).then_inc(phi_ready, 1)

        split_next(0)
        spread_z(0)
        split_next(1)
        root(nrm[:, 0, :], nsum[:, 0, 0:2 * BLKS], HD, 3).then_inc(root_ready, 1)
        split_next(2)
        spread_z(1)
        split_next(3)
        spread_z(2)
        split_next(4)
        spread_z(3)
        split_next(5)
        spread_z(4)
        split_next(6)
        act.wait_ge(nsum_filled, 4)
        nc.scalar.activation(qnrm[:, 0, :], nsum[:, 0, 0:GQ * QT * KVH], ACT.Sqrt, scale=1.0, bias=eps64[:, 0:1])
        nc.scalar.activation(dnrm[:, 0:1], nsum[0:HD, 1, 0:1], ACT.Sqrt, scale=1.0, bias=eps64[0:HD, 0:1]
                             ).then_inc(root_ready, 1)
        split_next(7)
        exps(0)
        exps(1)
        act.wait_ge(dnmax_ready, 1)
        nc.scalar.activation(dprob[:, :], dscore[:, :], ACT.Exp, scale=dnrm[:, 1:2], bias=dsmall[:, 1:2],
                             accum_out=dsmall[:, 3:4])
        nc.scalar.activation(dsmall[:, 4:5], dsmall[:, 2:3], ACT.Exp).then_inc(dexp_ready, 1)
        pool_hi(0)
        split_next(8)
        for i in range(2 * QT):
            out_probT(i)
            out_hi(i)
            if i + 2 < 2 * QT:
                exps(i + 2)
            if i == 0:
                pool_hi(1)
            elif i == 2:
                split_next(9)
            elif i == 3:
                pool_hi(2)
            elif i == 4:
                act.wait_ge(evacuated, E_USE["so"] + 1)
                nc.scalar.copy(mhi[:, NG:NG + GQ, SEQ:NOUT], dout[:, :, :].rearrange("p b j -> p j b")
                               ).then_inc(dohi_ready, 1)
            elif i == 5:
                pool_hi(3)

        for d in range(KD):
            split_hi(U_OUT + d + 2)
            act.wait_ge(evacuated, E_OUT + d + 1)
            x_hi(d, 2, META, NH_OUT, 2 * KD)
        norm(2, META, NH_OUT)
        act.wait_ge(mix_sent, 16 * 6)
        ffn_act(STAGES[1], True)
        for r in range(2):
            act.wait_ge(y_sent[r], 16 * (KD // 2))

    @block.vector
    def _(dve):
        steps = [0]

        def chain(ins):
            steps[0] += 1
            ins.then_inc(step, 1)
            dve.wait_ge(step, steps[0])

        nc.vector.memset(ones[:, :], 1.0)
        for g in range(KVH):
            for h in range(KVH):
                nc.vector.memset(headsel[g * HD:(g + 1) * HD, h:h + 1], float(g == h))
        nc.vector.memset(eps[:, :], EPS).then_inc(consts_made, 1)
        nc.vector.memset(eps64[:, :], EPS * HD).then_inc(consts_made, 1)

        def split_lo(c, it=None, slope=4):
            t = tiles_of(c)
            dve.wait_ge(whi_ready, up_to(c + 1, slope, it))
            nc.vector.tensor_tensor(wlo[:, c % 2, 0:t, :], raw[:, c % RAW, 0:t, :],
                                    whi[:, c % 2, 0:t, :].bitcast(F32), ALU.subtract).then_inc(wlo_ready, 1)

        def x_lo(d, g, c0, n, base, it=None):
            dve.wait_ge(xhi_ready, up_to(base + d + 1, 2, it))
            nc.vector.scalar_tensor_tensor(out=tile(xlo, d, it, c0, 2 * n), in0=tile(xT, d, it, c0, 2 * n),
                                           scalar=gain(g, d, it), in1=tile(xhi, d, it, c0, 2 * n).bitcast(F32),
                                           op0=ALU.mult, op1=ALU.subtract).then_inc(xlo_ready, 1)

        def invert(i, dst, src):
            dve.wait_ge(root_ready, i)
            nc.vector.reciprocal(dst, src).then_inc(inv_ready, 1)

        dve.wait_ge(fixed_loaded, 16)
        nc.vector.tensor_scalar(nsink[:, :], fixed[:, C_SINK:C_IDENT], -1.0, None, ALU.mult)
        split_lo(0)
        for k in range(KD):
            x_lo(k, 0, 0, NH_ALL, 0)
        split_lo(1)
        for i, k in enumerate(range(POOL_SQ, KD - 1)):
            dve.wait_ge(sqx_ready, KD - POOL_SQ)
            if i:
                dve.wait_ge(sqx_summed, i)
            nc.vector.tensor_tensor(sqx[:, KD - 1, :], sqx[:, KD - 1, :], sqx[:, k, :], ALU.add
                                    ).then_inc(sqx_summed, 1)
        invert(1, nrm[:, 1, 0:BLKS], nrm[:, 0, 0:BLKS])
        dve.wait_ge(masks_loaded, 32)
        nc.vector.tensor_copy(identb[:, :], ident[:, :])
        nc.vector.tensor_copy(maskb[:], maskf[:]).then_inc(masks_made, 1)
        dve.wait_ge(rstd_ready, 1)

        def ffn_vector(s, second):
            ua, ub, ea, eb, c0, n, f0 = (s[x] for x in ("ua", "ub", "ea", "eb", "c0", "n", "f0"))
            cols = slice(c0, c0 + 2 * n)

            def step_a(f, it=None):
                dve.wait_ge(unit_done, up_to(ua + 2 * f + 1, 4, it))
                nc.vector.tensor_tensor(halves(gate[:, cols], n), pair[0][:, :, 0:n], halves(rstd[:, cols], n),
                                        ALU.mult).then_inc(evacuated, 1)
                split_lo(ua + 2 * f + 2, it)
                dve.wait_ge(silu_ready, up_to(f0 + f + 1, 2, it))
                nc.vector.tensor_tensor(hid[:, cols], act_gate[:, cols], rstd[:, cols], ALU.mult
                                        ).then_inc(silu_scaled, 1)
                dve.wait_ge(unit_done, up_to(ua + 2 * f + 2, 4, it))
                dve.wait_ge(silu_scaled, up_to(f0 + f + 1, 2, it))
                nc.vector.tensor_tensor(halves(hid[:, cols], n), pair[1][:, :, 0:n], halves(hid[:, cols], n),
                                        ALU.mult).then_inc(evacuated, 1)
                split_lo(ua + 2 * f + 3, it)
                dve.wait_ge(hhi_ready, up_to(f0 + f + 1, 2, it))
                nc.vector.tensor_tensor(tile(hlo, f, it, c0, 2 * n), hid[:, cols],
                                        tile(hhi, f, it, c0, 2 * n).bitcast(F32), ALU.subtract
                                        ).then_inc(hlo_ready, 1)

            with dve.Fori(0, KF // 2 - 1) as it:
                step_a(0, it)
                step_a(1, it)
            step_a(KF - 2)
            step_a(KF - 1)

            def step_b(d, it=None):
                if ub + 2 * d + 2 < U_END:
                    split_lo(ub + 2 * d + 2, it)
                dve.wait_ge(unit_done, up_to(ub + 2 * d + 2, 4, it))
                x_d = halves(tile(xT, d, it, c0, 2 * n), n)
                if second and d >= 2:
                    dve.wait_ge(y_sent[d % 2], up_to(16 * (d // 2), 16, it))
                dst = halves(ybuf[:, d % 2, :], n) if second else x_d
                nc.vector.scalar_tensor_tensor(out=dst, in0=pair[d % 2][:, :, 0:n], scalar=0.5, in1=x_d,
                                               op0=ALU.mult, op1=ALU.add).then_inc(evacuated, 1)
                if ub + 2 * d + 3 < U_END:
                    split_lo(ub + 2 * d + 3, it)
                if not second:
                    x_lo(d, 1, c0, n, KD, it)

            if second:
                step_b(0)
                step_b(1)
                with dve.Fori(0, KD // 2 - 2) as it:
                    step_b(2, it)
                    step_b(3, it)
            else:
                with dve.Fori(0, KD // 2 - 1) as it:
                    step_b(0, it)
                    step_b(1, it)
            step_b(KD - 2)
            step_b(KD - 1)

        ffn_vector(STAGES[0], False)
        invert(2, nrm[:, 1, 0:BLKS], nrm[:, 0, 0:BLKS])
        dve.wait_ge(rstd_ready, 2)

        def split_next(m):
            split_lo(U_IN + m + 2)

        def scaled(m, dst, c0, n):
            dve.wait_ge(unit_done, U_IN + m + 1)
            nc.vector.tensor_tensor(halves(dst, n), pair[pair_of[MIX[m]]][:, :, 0:n],
                                    halves(rstd[:, c0:c0 + 2 * n], n), ALU.mult).then_inc(evacuated, 1)

        def take_z(x):
            c0, n = (0, NH_ALL) if x == 0 else (META, NH_OUT)
            dve.wait_ge(zg_ready, x) if x else None
            scaled(x + (x > 0), gate[:, c0:c0 + 2 * n], c0, n)

        def rotate(x):
            c0, n = (0, NH_ALL) if x == 0 else (META, NH_OUT)
            cols = slice(c0, c0 + 2 * n)
            if x:
                dve.wait_ge(rot_ready, x)
            dve.wait_ge(rot_filled, x + 1)
            nc.vector.tensor_tensor(halves(sq[:, cols], n), turn[:, :, 0:n], halves(sinT[:, cols], n),
                                    ALU.mult).then_inc(sin_ready, 1)
            if x == 0:
                dve.wait_ge(rot_ready, 1)
                dve.wait_ge(spread, 3)
                nc.vector.tensor_tensor(halves(kT[:, PAD:PAD + NT], n), halves(hid[:, cols], n), nsum[:, :, 0:n],
                                        ALU.mult).then_inc(qk_ready, 1)

        def pool_mean(g):
            w = WINDOWS[g]
            src = up[:, g % 2, :]
            win = wsum[:, g % 2, :]
            if g:
                dve.wait_ge(pair_filled, filled[f"P{g - 1}"])
            dve.wait_ge(summed, summed_at[g])
            nc.vector.scalar_tensor_tensor(out=gate[:, 0:SEQ], in0=win[:, 16 + META:16 + TP], scalar=1.0 / w,
                                           in1=src[:, 16 + META:16 + TP], op0=ALU.mult, op1=ALU.subtract)
            nc.vector.tensor_copy(ulast[:, g, :], src[:, 16 + TP - STATE:16 + TP])
            chain(nc.vector.tensor_copy(stT[:, g, :, STATE], src[:, 16 + TP:16 + NT]))
            chain(nc.vector.tensor_reduce(dsum[:, :], stT[:, g, :, STATE + 1 - w:STATE + 1], AX, ALU.add))
            nc.vector.scalar_tensor_tensor(out=gate[:, SEQ:NOUT], in0=dsum[:, :], scalar=1.0 / w,
                                           in1=src[:, 16 + TP:16 + NT], op0=ALU.mult, op1=ALU.subtract
                                           ).then_inc(pooled, 1)

        def pool_out(g):
            dve.wait_ge(pair_filled, filled[f"P{g}"])
            if g:
                dve.wait_ge(plo_ready, g)
            nc.vector.tensor_scalar(halves(pooled_out[:, :], NH_OUT), pair[0][:, :, 0:NH_OUT],
                                    gains[:, G_POOL + g:G_POOL + g + 1], None, ALU.mult).then_inc(evacuated, 1)

        def take_u(g):
            if g >= 2:
                dve.wait_ge(pair_filled, filled[f"P{g - 2}"])
                dve.wait_ge(summed, summed_at[g - 2])
            scaled(6 + g, up[:, g % 2, 16:16 + NT], 0, NH_ALL)

        def maxima(i):
            s = i % 2
            g = i % 2
            dve.wait_ge(scored, i + 1)
            sc = scorebank[s].rearrange("p s (j k) -> p (s j) k", k=2 * P)
            chain(nc.vector.tensor_reduce(small[:, s, 0:4], sc, AX, ALU.max))
            chain(nc.vector.tensor_tensor(small[:, s, 28:32], small[:, s, 0:4], qscale(i), ALU.mult))
            chain(nc.vector.scalar_tensor_tensor(out=small[:, s, 4:8], in0=small[:, s, 28:32], scalar=-1.0,
                                                 in1=nsink[:, g * GQ:(g + 1) * GQ], op0=ALU.mult, op1=ALU.min))
            nc.vector.tensor_tensor(small[:, s, 8:12], small[:, s, 4:8], sink[:, g * GQ:(g + 1) * GQ], ALU.add
                                    ).then_inc(nmax_ready, 1)

        def normalise(i):
            s = i % 2
            dve.wait_ge(exp_ready, i + 1)
            chain(nc.vector.tensor_tensor(small[:, s, 20:24], small[:, s, 12:16], small[:, s, 16:20], ALU.add))
            chain(nc.vector.reciprocal(small[:, s, 24:28], small[:, s, 20:24]))
            for j in range(GQ):
                last = nc.vector.tensor_scalar(prob[:, s, j, :], prob[:, s, j, :], small[:, s, 24 + j:25 + j], None,
                                               ALU.mult)
            last.then_inc(prob_ready, 1)

        def out_probT(i):
            dve.wait_ge(probs_turned, i + 1)
            if i >= 1:
                dve.wait_ge(attended, i)
            nc.vector.tensor_copy(probT[:, 1, :], turn[:, 1, :]).then_inc(probT_b, 1)

        def out_lo(i):
            t, g = divmod(i, 2)
            rows = slice(g * HD, (g + 1) * HD)
            dve.wait_ge(ohi_ready, i + 1)
            nc.vector.tensor_tensor(mlo[rows, NG:NG + GQ, t * P:(t + 1) * P],
                                    turn[rows, 0, :].rearrange("p (j q) -> p j q", j=GQ),
                                    mhi[rows, NG:NG + GQ, t * P:(t + 1) * P].bitcast(F32), ALU.subtract
                                    ).then_inc(olo_ready, 1)

        take_z(0)
        split_next(0)
        scaled(1, vT[:, PAD:PAD + NT], 0, NH_ALL)
        split_next(1)
        dve.wait_ge(root_ready, 3)
        chain(nc.vector.reciprocal(nrm[:, 1, :], nrm[:, 0, :]))
        nc.vector.tensor_copy(knrm[:, :, :].rearrange("p b (g e) -> p (b g) e", g=KVH),
                              nrm[:, 1, :].rearrange("p (c o) -> p c o", o=1).to_broadcast([P, KVH * BLKS, HD])
                              ).then_inc(inv_ready, 1)
        dve.wait_ge(mixin_loaded, 16 * 6)
        rotate(0)
        take_z(1)
        split_next(2)
        dve.wait_ge(tok_filled, 1)
        tokps = nsum.rearrange("p s n -> p (s n)")
        vals, new = slice(0, NBLK * P), slice(NBLK * P, (NBLK + 1) * P)
        nc.vector.tensor_copy(tok[:, vals], tokps[:, vals]).then_inc(tok_ready, 1)
        nc.vector.tensor_copy(tok[0:NDEC, new], tokps[0:NDEC, new]).then_inc(tok_ready, 1)
        take_z(2)
        split_next(3)
        rotate(1)
        take_z(3)
        split_next(4)
        rotate(2)
        take_z(4)
        split_next(5)
        rotate(3)
        dve.wait_ge(pads_zero, 3)
        take_u(0)
        split_next(6)
        nc.vector.tensor_copy(ckT[:, :, WIN - 1], kT[:, PAD + TP:PAD + NT]).then_inc(newk_placed, 1)
        rotate(4)
        dve.wait_ge(root_ready, 4)
        nc.vector.reciprocal(qnrm[:, 1, :], qnrm[:, 0, :])
        nc.vector.reciprocal(dnrm[:, 1:2], dnrm[:, 0:1]).then_inc(inv_ready, 1)
        dve.wait_ge(inv_ready, 4)
        take_u(1)
        split_next(7)
        maxima(0)
        dve.wait_ge(pair_filled, filled["ss"])
        nc.vector.tensor_copy(dscoreT[:, :].rearrange("p (g c) -> p g c", g=KVH), pair[0][:, :, 0:NDEC * GQ]
                              ).then_inc(evacuated, 1)
        pool_mean(0)
        dve.wait_ge(pair_filled, filled["sr"])
        nc.vector.tensor_copy(dscore[:, :], pair[0][0:HD, 0, 0:P]).then_inc(evacuated, 1)
        dve.wait_ge(evacuated, E_USE["sr"] + 1)
        pool_out(0)
        maxima(1)
        normalise(0)
        chain(nc.vector.tensor_reduce(dsmall[:, 0:1], dscore[:, :], AX, ALU.max))
        chain(nc.vector.tensor_tensor(dsmall[:, 7:8], dsmall[:, 0:1], dnrm[:, 1:2], ALU.mult))
        chain(nc.vector.scalar_tensor_tensor(out=dsmall[:, 1:2], in0=dsmall[:, 7:8], scalar=-1.0,
                                             in1=ndsink, op0=ALU.mult, op1=ALU.min))
        nc.vector.tensor_tensor(dsmall[:, 2:3], dsmall[:, 1:2], dsink, ALU.add).then_inc(dnmax_ready, 1)
        pool_mean(1)
        normalise(1)
        dve.wait_ge(dexp_ready, 1)
        chain(nc.vector.tensor_tensor(dsmall[:, 5:6], dsmall[:, 3:4], dsmall[:, 4:5], ALU.add))
        chain(nc.vector.reciprocal(dsmall[:, 6:7], dsmall[:, 5:6]))
        nc.vector.tensor_scalar(dprob[:, :], dprob[:, :], dsmall[:, 6:7], None, ALU.mult).then_inc(dprob_ready, 1)
        take_u(2)
        split_next(8)
        for i in range(2 * QT):
            out_probT(i)
            if i + 2 < 2 * QT:
                maxima(i + 2)
            out_lo(i)
            if i == 0:
                pool_out(1)
            elif i == 2:
                pool_mean(2)
            elif i == 3:
                dve.wait_ge(pair_filled, filled["sp"])
                nc.vector.tensor_copy(dprobT[:, :], pair[0][:, 0, 0:HD]).then_inc(evacuated, 1)
                pool_out(2)
            elif i == 4:
                pool_mean(3)
                dve.wait_ge(pair_filled, filled["so"])
                for g in range(KVH):
                    rows = slice(g * HD, (g + 1) * HD)
                    last = nc.vector.tensor_copy(dout[rows, :, :],
                                                 pair[0][rows, g, 0:NDEC * GQ].rearrange("p (b j) -> p b j", b=NDEC))
                last.then_inc(evacuated, 1)
            elif i == 5:
                pool_out(3)
            if i + 2 < 2 * QT:
                normalise(i + 2)
            if i == 2:
                take_u(3)
                split_next(9)

        for d in range(KD):
            dve.wait_ge(unit_done, U_OUT + d + 1)
            x_d = halves(xT[:, d, META:NT], NH_OUT)
            nc.vector.tensor_tensor(x_d, pair[d % 2][:, :, 0:NH_OUT], x_d, ALU.add).then_inc(evacuated, 1)
            split_lo(U_OUT + d + 2)
            x_lo(d, 2, META, NH_OUT, 2 * KD)
        invert(5, nrm[:, 1, 0:BLKS], nrm[:, 0, 0:BLKS])
        dve.wait_ge(rstd_ready, 3)
        dve.wait_ge(mix_sent, 16 * 6)
        ffn_vector(STAGES[1], True)

    @block.gpsimd
    def _(pool):
        def square(d, e0, c0, n, i, it=None):
            pool.wait_ge(evacuated, up_to(e0 + d + 1, 1, it))
            x_d = tile(xT, d, it, c0, 2 * n, 1)
            nc.gpsimd.tensor_tensor(sq[:, c0:c0 + 2 * n], x_d, x_d, ALU.mult).then_inc(sq_ready, 1)
            pool.wait_ge(sq_ready, up_to(SQSUM_AT[i - 1] + d, 1, it))
            nc.gpsimd.tensor_tensor(sqsum[:, c0:c0 + 2 * n], sqsum[:, c0:c0 + 2 * n], sq[:, c0:c0 + 2 * n],
                                    ALU.add).then_inc(sqsum_ready, 1)
            pool.wait_ge(sqsum_ready, up_to(SQSUM_AT[i - 1] + d + 1, 1, it))

        pool.wait_ge(x_loaded[0], 16)
        nc.gpsimd.tensor_tensor(sqsum[:, :], xT[:, 0, :], xT[:, 0, :], ALU.mult).then_inc(sqsum_ready, 1)
        for k in range(1, POOL_SQ):
            pool.wait_ge(x_loaded[k], 16)
            nc.gpsimd.tensor_tensor(sqx[:, k, :], xT[:, k, :], xT[:, k, :], ALU.mult).then_inc(sq_ready, 1)
            pool.wait_ge(sq_ready, k)
            pool.wait_ge(sqsum_ready, k)
            nc.gpsimd.tensor_tensor(sqsum[:, :], sqsum[:, :], sqx[:, k, :], ALU.add).then_inc(sqsum_ready, 1)
        pool.wait_ge(nsum_filled, 1)
        nc.gpsimd.memset(sqsum[:, :], 0.0).then_inc(sqsum_zero, 1)
        pool.wait_ge(sqsum_zero, 1)
        with pool.Fori(0, KD) as it:
            square(0, E_B1, 0, NH_ALL, 1, it)
        pool.wait_ge(unit_done, U_IN)
        nc.gpsimd.memset(kT[:, 0:PAD], 0.0).then_inc(pads_zero, 1)
        nc.gpsimd.memset(vT[:, 0:PAD], 0.0).then_inc(pads_zero, 1)
        nc.gpsimd.memset(up[:, :, 0:16], 0.0).then_inc(pads_zero, 1)
        nc.gpsimd.memset(wsum[:, :, 0:16], 0.0).then_inc(pads_zero, 1)
        pool.wait_ge(nsum_filled, 2)
        nc.gpsimd.memset(sqsum[:, :], 0.0).then_inc(sqsum_zero, 1)
        pool.wait_ge(mixin_loaded, 16 * 6)
        for x in range(5):
            cols = slice(0 if x == 0 else META, NT)
            pool.wait_ge(zg_ready, x + 1)
            if x == 1:
                pool.wait_ge(qk_ready, 1)
            nc.gpsimd.tensor_tensor(hid[:, cols], zg[:, x % 2, cols], cosT[:, cols], ALU.mult
                                    ).then_inc(cos_ready, 1)
            pool.wait_ge(cos_ready, x + 1)
            pool.wait_ge(sin_ready, x + 1)
            dst = hid[:, :] if x == 0 else qT[:, x - 1, :]
            nc.gpsimd.tensor_tensor(dst, hid[:, cols], sq[:, cols], ALU.add).then_inc(rot_ready, 1)
            pool.wait_ge(rot_ready, x + 1)
        pool.wait_ge(pads_zero, 4)

        def window_sums(g):
            pool.wait_ge(evacuated, E_USE[f"u{g}"] + 1)
            if g:
                pool.wait_ge(pooled, g)
            src = up[:, g % 2, :]
            for s in range(g + 1):
                dst = wsum[:, (2 * g - s) % 2, :]
                nc.gpsimd.tensor_tensor(dst[:, 16:16 + TP], src[:, 16:16 + TP],
                                        src[:, 16 - (1 << s):16 + TP - (1 << s)], ALU.add).then_inc(summed, 1)
                pool.wait_ge(summed, summed_at[g] - g + s)
                src = dst

        def pool_lo(g):
            pool.wait_ge(phi_ready, g + 1)
            nc.gpsimd.tensor_tensor(mlo[:, g, :], pooled_out[:, :], mhi[:, g, :].bitcast(F32), ALU.subtract
                                    ).then_inc(plo_ready, 1)

        window_sums(0)
        window_sums(1)
        pool_lo(0)
        window_sums(2)
        pool_lo(1)
        window_sums(3)
        pool_lo(2)
        pool.wait_ge(dohi_ready, 1)
        nc.gpsimd.tensor_tensor(mlo[:, NG:NG + GQ, SEQ:NOUT], dout[:, :, :].rearrange("p b j -> p j b"),
                                mhi[:, NG:NG + GQ, SEQ:NOUT].bitcast(F32), ALU.subtract).then_inc(dolo_ready, 1)
        pool_lo(3)
        pool.wait_ge(sqsum_zero, 2)
        with pool.Fori(0, KD) as it:
            square(0, E_OUT, META, NH_OUT, 2, it)

    ctx.close()


def constants():
    eye = np.eye(P, dtype=np.float32)
    swap = np.zeros((P, P), np.float32)
    half = ROPE // 2
    for h in range(0, P, HD):
        for i in range(half):
            swap[h + i, h + half + i] = swap[h + half + i, h + i] = 1
    i, j = np.arange(P)[:, None], np.arange(2 * P)[None, :]
    band = (j > i) & (j <= i + WIN)
    masks = [np.where(m, 0.0, NEG).astype(np.float32) for m in (band & (j >= PAD), band)]
    pos = np.concatenate([np.arange(TP), np.full(NDEC, PAST)]).astype(np.float32)
    freq = np.exp(np.float32(-math.log(500000.0)) * np.arange(half, dtype=np.float32) * np.float32(2.0 / ROPE))
    ang = (pos[None, :] * freq.astype(np.float32)[:, None]).astype(np.float64)
    cos, sin = np.ones((P, NT), np.float32), np.zeros((P, NT), np.float32)
    for h in range(0, P, HD):
        for b, sign in ((0, -1), (half, 1)):
            cos[h + b:h + b + half] = np.cos(ang)
            sin[h + b:h + b + half] = sign * np.sin(ang)
    return {"const": np.concatenate([swap, *masks], 1), "cos": cos, "sin": sin}, eye


def kernel(**inputs):
    import numpy as _np
    import concourse.bacc as _bacc
    from concourse import mybir as _mybir
    from concourse.bass_utils import run_bass_kernel_spmd as _run

    nc = _bacc.Bacc("TRN2", target_bir_lowering=False, num_devices=1)
    src = lambda name, *shape: _np.asarray(inputs[name]).reshape(shape)

    def units(w, rows, cols):
        return w.reshape(cols, rows, P, -1, P).transpose(2, 3, 0, 1, 4)

    fixed_in, eye = constants()
    heads = _np.arange(2 * POOLW).reshape(-1, HD)
    by_pair = _np.concatenate([heads[HEADS + h * GQ + j] for j in range(GQ) for h in range(KVH)])
    w_in, w_out = src("w_in", D, -1), src("w_out", D, D)
    w_in = _np.concatenate([w_in[:, 2 * POOLW:], w_in[:, by_pair], w_in[:, 0:POOLW]], 1)
    w_out = _np.concatenate([w_out[0:POOLW], w_out[by_pair]], 0)
    x = _np.concatenate([src("meta_tokens", META, D), src("x_prompt", SEQ, D), src("x_sample", NDEC, D)], 0)
    sinks = src("attn_sinks", 1, HEADS)
    two = lambda name: _np.concatenate([src(name, HD, 1)] * 2, 0)
    dsink = _np.zeros((P, 1), _np.float32)
    dsink[0:HD] = _np.repeat(sinks.reshape(KVH, 1, GQ), NDEC, 1).reshape(HD, 1)
    given = {
        "x": x.T.reshape(KD, P, NT).transpose(1, 0, 2),
        "fixed": _np.concatenate([src("ffn1_norm", KD, P).T, src("mix_norm", KD, P).T, src("ffn2_norm", KD, P).T,
                                  src("pool_scale", NG, P).T, two("q_norm"), two("k_norm"),
                                  _np.repeat(sinks, P, 0), dsink, eye], 1),
        "ck": _np.roll(src("cache_k", NDEC, WIN, P), -1, 1).transpose(2, 0, 1),
        "cv": _np.roll(src("cache_v", NDEC, WIN, P), -1, 1).transpose(1, 0, 2),
        "state": _np.pad(src("state_pool", NDEC, STATE, NG, P), ((0, 0), (0, 1), (0, 0), (0, 0))
                         ).transpose(3, 2, 0, 1),
        "pool_w": src("pool_w", NG, P, P).transpose(1, 0, 2),
        "w_in": units(w_in, KD, 1).reshape(P, -1), "w_out": units(w_out, KD, 1).reshape(P, -1),
    } | fixed_in
    for i in (1, 2):
        both = [units(src(f"ffn{i}_w_{w}", D, F), KD, 1) for w in ("gate", "up")]
        given[f"gu{i}"] = _np.concatenate(both, 2).reshape(P, -1)
        given[f"d{i}"] = units(src(f"ffn{i}_w_down", F, D), DOWN_T, 2).reshape(P, -1)
    given = {n: _np.ascontiguousarray(v) for n, v in given.items()}
    outs = {"o_y": (P, KD * NOUT), "o_pp": (P, NG, STATE), "o_kp": (P, WIN), "o_vp": (P, WIN),
            "o_ps": (P, NG, NDEC, STATE + 1), "o_ks": (P, NDEC, WIN), "o_vs": (WIN, NDEC, P)}
    f32 = _mybir.dt.float32
    a = {n: nc.dram_tensor(n, v.shape, f32, kind="ExternalInput").ap() for n, v in given.items()}
    a |= {n: nc.dram_tensor(n, v, f32, kind="ExternalOutput").ap() for n, v in outs.items()}
    build(nc, a)
    r = _run(nc, [given], core_ids=[0]).results[0]
    y = r["o_y"].reshape(P, KD, NOUT).transpose(2, 1, 0).reshape(NOUT, D)
    return tuple(_np.ascontiguousarray(v) for v in (
        y[0:SEQ].reshape(1, SEQ, D), y[SEQ:].reshape(NDEC, 1, D),
        r["o_pp"].transpose(2, 1, 0).reshape(1, 1, STATE, POOLW),
        r["o_kp"].T.reshape(1, 1, WIN, KVH, HD), r["o_vp"].T.reshape(1, 1, WIN, KVH, HD),
        r["o_ps"][:, :, :, 1:].transpose(2, 3, 1, 0).reshape(1, NDEC, STATE, POOLW),
        r["o_ks"].transpose(1, 2, 0).reshape(1, NDEC, WIN, KVH, HD),
        r["o_vs"].transpose(1, 0, 2).reshape(1, NDEC, WIN, KVH, HD)))
```

```python
import math
from contextlib import ExitStack

import numpy as np

import concourse.bass as bass
from concourse import mybir

ALU = mybir.AluOpType
ACT = mybir.ActivationFunctionType
F32 = mybir.dt.float32
F32R = mybir.dt.float32r
BF16 = mybir.dt.bfloat16
AX = mybir.AxisListType.X

P = 128
D = 1024
KD = D // P
F = 2816
KF = F // P
META, SEQ, NDEC = 16, 512, 8
TP = META + SEQ
NT = TP + NDEC
NH_ALL = NT // 2
NOUT = SEQ + NDEC
NH_OUT = NOUT // 2
HD = 64
HEADS, KVH = 8, 2
GQ = HEADS // KVH
WIN = 128
POOLW = 512
NG = 4
WINDOWS = (2, 4, 8, 16)
STATE = 15
BLKS = 6
PAD = (-META) % P
NBLK = (PAD + TP) // P
QT = SEQ // P
PAST = 4096
ROPE = HD // 4
EPS = 1e-6
SCALE = HD ** -0.5
NEG = -1e30

G_POOL, G_Q, G_K = 3 * KD, 3 * KD + NG, 3 * KD + NG + 1
N_GAIN = G_K + 1
C_SINK = N_GAIN
C_DSINK = C_SINK + HEADS
C_IDENT = C_DSINK + 1
N_FIXED = C_IDENT + P
RAW = 4
DOWN_T = KF // 2
A_UNITS, B_UNITS, IN_UNITS, OUT_UNITS = 2 * KF, 2 * KD, 10, KD
U_A1 = 0
U_B1 = U_A1 + A_UNITS
U_IN = U_B1 + B_UNITS
U_OUT = U_IN + IN_UNITS
U_A2 = U_OUT + OUT_UNITS
U_B2 = U_A2 + A_UNITS
U_END = U_B2 + B_UNITS

MIX = ["k", "v", "q0", "q1", "q2", "q3", "u0", "u1", "u2", "u3"]
PAIR_USES = ["k", "v", "q0", "q1", "q2", "q3", "u0", "u1", "P0", "u2", "P1", "u3", "P2", "so", "P3"]
PAIR1 = {"v", "q1", "q3", "u1"}
NORM_AT = (1, 2, 5)
POOL_SQ = 4
SQSUM_AT = (POOL_SQ, POOL_SQ + KD, POOL_SQ + 2 * KD)


def tiles_of(u):
    down = U_B1 <= u < U_IN or U_B2 <= u < U_END
    return DOWN_T if down else KD


def build(nc, a):
    ctx = ExitStack()
    at = [0]

    base = (nc.sbuf_base + 31) // 32 * 32
    ARENA = (nc.sbuf_usable_end - base) // 32 * 32 - 32
    ctx.enter_context(nc.sbuf_tensor("arena", [P, ARENA // 4], F32))

    def place(name, shape, dt=F32, offset=None):
        size = int(np.prod(shape[1:])) * (2 if dt == BF16 else 4)
        size = (size + 31) // 32 * 32
        o = at[0] if offset is None else offset
        if offset is None:
            at[0] += size
            assert at[0] <= ARENA, (name, at[0])
        return nc.alloc_sbuf_tensor_at(name, list(shape), dt, offset=base + o), o + size

    xT, _ = place("xT", [P, KD, NT])
    xhi_at = at[0]
    xhi, _ = place("xhi", [P, KD, NT], F32R)
    xlo, _ = place("xlo", [P, KD, NT], F32R)
    h_at = at[0]
    hhi, _ = place("hhi", [P, KF, NT], F32R)
    hlo, _ = place("hlo", [P, KF, NT], F32R)
    h_end = at[0]
    raw, _ = place("raw", [P, RAW, DOWN_T, P])
    whi, _ = place("whi", [P, 2, DOWN_T, P], F32R)
    wlo, _ = place("wlo", [P, 2, DOWN_T, P], F32R)
    rstd, _ = place("rstd", [P, NT])
    gate, _ = place("gate", [P, NT])
    act_gate, _ = place("act_gate", [P, NT])
    hid, _ = place("hid", [P, NT])
    sq, _ = place("sq", [P, NT])
    sqsum, _ = place("sqsum", [P, NT])
    fixed, _ = place("fixed", [P, N_FIXED])
    ones, _ = place("ones", [P, 1])
    headsel, _ = place("headsel", [P, 2])
    nrm, _ = place("nrm", [P, 2, 2 * BLKS])
    qnrm, _ = place("qnrm", [P, 2, GQ * QT * KVH])
    dnrm, _ = place("dnrm", [HD, 2])
    eps64, _ = place("eps64", [P, 1])
    identb, _ = place("identb", [P, P], BF16)
    maskb, _ = place("maskb", [P, 2, 2 * P], BF16)
    eps, _ = place("eps", [P, 1])
    warm, _ = place("warm", [P, 1])
    dsum, _ = place("dsum", [P, NDEC])
    small, _ = place("small", [P, 2, 32])
    nsink, _ = place("nsink", [P, HEADS + 1])
    gains, sink, ident = fixed[:, 0:N_GAIN], fixed[:, C_SINK:C_DSINK], fixed[:, C_IDENT:N_FIXED]
    dsink, ndsink = fixed[0:HD, C_DSINK:C_IDENT], nsink[0:HD, HEADS:HEADS + 1]
    o = h_at
    maskf, o = place("maskf", [P, 2, 2 * P], offset=o)
    sqx, o = place("sqx", [P, KD, NT], offset=o)
    o = h_at
    cosT, o = place("cosT", [P, NT], offset=o)
    sinT, o = place("sinT", [P, NT], offset=o)
    ckT, o = place("ckT", [P, NDEC, P], offset=o)
    cv, o = place("cv", [P, NDEC, P], offset=o)
    stT, o = place("stT", [P, NG, NDEC, STATE + 1], offset=o)
    poolw, o = place("poolw", [P, NG, P], offset=o)
    qT, o = place("qT", [P, GQ, NOUT], offset=o)
    kT, o = place("kT", [P, PAD + NT], offset=o)
    vT, o = place("vT", [P, PAD + NT], offset=o)
    tok, o = place("tok", [P, (NBLK + 1) * P], offset=o)
    mhi, o = place("mhi", [P, KD, NOUT], F32R, offset=o)
    mlo, o = place("mlo", [P, KD, NOUT], F32R, offset=o)
    ulast, o = place("ulast", [P, NG, STATE], offset=o)
    up, o = place("up", [P, 2, 16 + NT], offset=o)
    wsum, o = place("wsum", [P, 2, 16 + NT], offset=o)
    knrm, _ = place("knrm", [P, BLKS, P], offset=o)
    dscore, _ = place("dscore", [HD, P], offset=o)
    probT, o = place("probT", [P, 2, GQ * P], offset=o)
    dscoreT, _ = place("dscoreT", [P, HD], offset=o)
    dprobT, o = place("dprobT", [P, HD], offset=o)
    dprob, o = place("dprob", [HD, P], offset=o)
    dout, o = place("dout", [P, NDEC, GQ], offset=o)
    dsmall, o = place("dsmall", [HD, 8], offset=o)
    dzsq, o = place("dzsq", [P, NDEC, GQ], offset=o)
    dq, o = place("dq", [P, NDEC, KVH, GQ], offset=o)
    prob_at = o
    zg, o = place("zg", [P, 2, NT], offset=prob_at)
    zsq, o = place("zsq", [P, 2, NT], offset=o)
    partner, o = place("partner", [P, 2, NT], offset=o)
    prob, _ = place("prob", [P, 2, GQ, 2 * P], offset=prob_at)
    assert o <= h_end, (o, h_end)
    ybuf, _ = place("ybuf", [P, 2, NOUT], offset=xhi_at)
    pooled_out = act_gate[:, 0:NOUT]

    ps = ctx.enter_context(nc.psum_tensor("ps", [P, 8, 512], F32))
    pair = [ps[:, 0:2, :], ps[:, 2:4, :]]
    nsum = ps[:, 4:6, :]
    turn = ps[:, 6:8, :]
    scorebank = [ps[:, 2:4, :], ps[:, 4:6, :]]

    def sem(name):
        return ctx.enter_context(nc.semaphore(name))

    x_loaded = [sem(f"x_loaded{k}") for k in range(KD)]
    fixed_loaded = sem("fixed_loaded")
    mixin_loaded = sem("mixin_loaded")
    raw_loaded = [sem(f"raw_loaded{r}") for r in range(RAW)]
    whi_ready = sem("whi_ready")
    wlo_ready = sem("wlo_ready")
    unit_done = sem("unit_done")
    evacuated = sem("evacuated")
    consts_made = sem("consts_made")
    masks_loaded = sem("masks_loaded")
    masks_made = sem("masks_made")
    spread = sem("spread")
    rstd_ready = sem("rstd_ready")
    xhi_ready = sem("xhi_ready")
    xlo_ready = sem("xlo_ready")
    sq_ready = sem("sq_ready")
    sqx_ready = sem("sqx_ready")
    sqx_summed = sem("sqx_summed")
    sqsum_ready = sem("sqsum_ready")
    sqsum_zero = sem("sqsum_zero")
    nsum_filled = sem("nsum_filled")
    root_ready = sem("root_ready")
    inv_ready = sem("inv_ready")
    tok_filled = sem("tok_filled")
    silu_ready = sem("silu_ready")
    silu_scaled = sem("silu_scaled")
    hhi_ready = sem("hhi_ready")
    hlo_ready = sem("hlo_ready")
    zg_ready = sem("zg_ready")
    partner_there = [sem("partner_there0"), sem("partner_there1")]
    zsq_read = sem("zsq_read")
    cos_ready = sem("cos_ready")
    sin_ready = sem("sin_ready")
    rot_ready = sem("rot_ready")
    qk_ready = sem("qk_ready")
    pads_zero = sem("pads_zero")
    tok_ready = sem("tok_ready")
    newv_placed = sem("newv_placed")
    dq_ready = sem("dq_ready")
    dscores_filled = sem("dscores_filled")
    dscores_kept = sem("dscores_kept")
    dprobs_filled = sem("dprobs_filled")
    dprobs_kept = sem("dprobs_kept")
    warmed = sem("warmed")
    pair_filled = sem("pair_filled")
    summed = sem("summed")
    pooled = sem("pooled")
    phi_ready = sem("phi_ready")
    plo_ready = sem("plo_ready")
    step = sem("step")
    newk_placed = sem("newk_placed")
    scored = sem("scored")
    nmax_ready = sem("nmax_ready")
    exp_ready = sem("exp_ready")
    prob_ready = sem("prob_ready")
    probs_turned = sem("probs_turned")
    probT_ready = sem("probT_ready")
    attended = sem("attended")
    ohi_ready = sem("ohi_ready")
    olo_ready = sem("olo_ready")
    dnmax_ready = sem("dnmax_ready")
    dexp_ready = sem("dexp_ready")
    dprob_ready = sem("dprob_ready")
    dohi_ready = sem("dohi_ready")
    dolo_ready = sem("dolo_ready")
    y_sent = [sem("y_sent0"), sem("y_sent1")]
    mix_sent = sem("mix_sent")

    E_A1 = 0
    E_B1 = E_A1 + 2 * KF
    E_MIX = E_B1 + KD
    E_OUT = E_MIX + len(PAIR_USES)
    E_A2 = E_OUT + KD
    E_B2 = E_A2 + 2 * KF
    pair_of = {u: int(u in PAIR1) for u in PAIR_USES}
    extra = [u for u in PAIR_USES if u not in MIX]
    E_USE = {u: E_MIX + i for i, u in enumerate(PAIR_USES)}
    before = {}
    for i, u in enumerate(PAIR_USES):
        prev = [v for v in PAIR_USES[:i] if pair_of[v] == pair_of[u]]
        before[u] = E_USE[prev[-1]] + 1 if prev else E_MIX - 1 + pair_of[u]
    filled = {u: i + 1 for i, u in enumerate(extra)}
    summed_at = {0: 1, 1: 3, 2: 6, 3: 10}

    def up_to(const, slope=0, it=None):
        return const if it is None else const + it * slope

    STAGES = [dict(ua=U_A1, ub=U_B1, ea=E_A1, eb=E_B1, c0=0, n=NH_ALL, f0=0, x0=0),
              dict(ua=U_A2, ub=U_B2, ea=E_A2, eb=E_B2, c0=META, n=NH_OUT, f0=KF, x0=2 * KD)]

    def blocks(c0, n):
        return [(h, o) for h in range(2) for o in (0, P, n - P)]

    def halves(tile2d, n):
        return tile2d.rearrange("p (s n) -> p s n", n=n)

    def tile(t, d, it, c0, w, step=2):
        if it is None:
            return t[:, d, c0:c0 + w]
        return t[:, :, :].rearrange("p k n -> p (k n)")[:, bass.ds((it * step + d) * NT + c0, w)]

    def gain(g, d, it, step=2):
        if it is None:
            return gains[:, g * KD + d:g * KD + d + 1]
        return gains[:, bass.ds(it * step + g * KD + d, 1)]

    def qscale(i, j=None):
        t, g = divmod(i, KVH)
        if j is not None:
            c = (j * QT + t) * KVH + g
            return qnrm[:, 1, c:c + 1]
        return qnrm[:, 1, :].rearrange("p (j t g) -> p j t g", j=GQ, t=QT)[:, :, t, g]

    block = ctx.enter_context(nc.Block())

    @block.sync
    def _(sp):
        def free(c, it=None):
            if c >= RAW:
                sp.wait_ge(wlo_ready, up_to(c - RAW + 1, RAW, it))

        def load(c, src, u, it=None, slope=RAW):
            free(c, it)
            w = tiles_of(c) * P
            at = u * w if it is None else (it * slope + u) * w
            sp.dma_start(raw[:, c % RAW, 0:tiles_of(c), :].rearrange("p t c -> p (t c)"),
                         src[:, bass.ds(at, w)]).then_inc(raw_loaded[c % RAW], 16)

        def ffn(s, first):
            for u in range(first, RAW):
                load(s["ua"] + u, s["gate_up_w"], u)
            with sp.Fori(0, A_UNITS // RAW - 1) as it:
                for u in range(RAW, 2 * RAW):
                    load(s["ua"] + u, s["gate_up_w"], u, it)
            with sp.Fori(0, B_UNITS // RAW) as it:
                for u in range(RAW):
                    load(s["ub"] + u, s["down_w"], u, it)

        for s, i in zip(STAGES, (1, 2)):
            s.update(gate_up_w=a[f"gu{i}"], down_w=a[f"d{i}"])
        load(0, a["gu1"], 0)
        for k in range(KD):
            sp.dma_start(xT[:, k, :], a["x"][:, k, :]).then_inc(x_loaded[k], 16)
        ffn(STAGES[0], 1)

        for m in range(4):
            load(U_IN + m, a["w_in"], m)
        sp.wait_ge(unit_done, U_IN)
        for dst, src in ((cosT[:], a["cos"]), (sinT[:], a["sin"]), (ckT[:], a["ck"]), (cv[:], a["cv"]),
                         (stT[:], a["state"]), (poolw[:], a["pool_w"])):
            sp.dma_start(dst, src).then_inc(mixin_loaded, 16)
        for m in range(4, IN_UNITS):
            load(U_IN + m, a["w_in"], m)
        load(U_OUT, a["w_out"], 0)
        sp.wait_ge(qk_ready, 1)
        last = slice(PAD + TP - WIN, PAD + TP)
        sp.dma_start(a["o_kp"], kT[:, last]).then_inc(mix_sent, 16)
        sp.dma_start(a["o_vp"], vT[:, last]).then_inc(mix_sent, 16)
        sp.wait_ge(newk_placed, 1)
        sp.dma_start(a["o_ks"], ckT[:]).then_inc(mix_sent, 16)
        sp.wait_ge(tok_ready, 2)
        sp.wait_ge(mixin_loaded, 16 * 6)
        for b in range(NDEC):
            sp.dma_start(cv[WIN - 1:WIN, b, :], tok[b:b + 1, NBLK * P:(NBLK + 1) * P]).then_inc(newv_placed, 16)
        load(U_OUT + 1, a["w_out"], 1)
        sp.wait_ge(newv_placed, 16 * NDEC)
        sp.dma_start(a["o_vs"], cv[:]).then_inc(mix_sent, 16)
        for d in range(2, KD):
            load(U_OUT + d, a["w_out"], d)
        sp.wait_ge(pooled, NG)
        sp.dma_start(a["o_pp"], ulast[:]).then_inc(mix_sent, 16)
        sp.dma_start(a["o_ps"], stT[:]).then_inc(mix_sent, 16)
        ffn(STAGES[1], 0)
        sp.wait_ge(mix_sent, 16 * 6)

    @block.tensor
    def _(pe):
        def product(c, it, slope, dst, tiles, hi, lo, k0, kall, c0, n, wait_k=None, ks=None):
            if ks is None or ks[0] == 0:
                pe.wait_ge(wlo_ready, up_to(c + 1, slope, it))
            for kk in ks or range(tiles):
                k = k0 + kk
                if wait_k:
                    wait_k(k)
                for w, x in ((whi, hi), (whi, lo), (wlo, hi)):
                    for s in range(2):
                        last = nc.tensor.matmul(
                            dst[:, s, 0:n], w[:, c % 2, kk, :], x[:, k, c0 + s * n:c0 + (s + 1) * n],
                            start=(k == 0 and w is whi and x is hi), stop=(k == kall - 1 and w is wlo))
            if not ks or ks[-1] == tiles - 1:
                last.then_inc(unit_done, 1)

        flat = nsum.rearrange("p s n -> p (s n)")

        def norm_sums(i, c0, n):
            src = sqsum
            if i == 0:
                pe.wait_ge(sqx_summed, KD - POOL_SQ)
                src = sqx[:, POOL_SQ, :]
            else:
                pe.wait_ge(sqsum_ready, SQSUM_AT[i])
            for b, (h, o) in enumerate(blocks(c0, n)):
                col = c0 + h * n + o
                last = nc.tensor.matmul(nsum[:, 0, b:b + 1], src[:, col:col + P], ones[:, :], start=True, stop=True)
            last.then_inc(nsum_filled, 1)

        def norm_spread(i, c0, n, inv):
            pe.wait_ge(inv_ready, inv)
            for b, (h, o) in enumerate(blocks(c0, n)):
                last = nc.tensor.transpose(nsum[:, h, o:o + P], nrm[:, 1, b:b + 1].to_broadcast([P, P]), ident[:, :])
            last.then_inc(spread, 1)

        def ffn_products(s, second):
            ua, ub, ea, eb, c0, n = (s[x] for x in ("ua", "ub", "ea", "eb", "c0", "n"))

            def gate_or_up(j, it, ks=None, f=0, wait_k=None):
                if (ks is None or ks[0] == 0) and ea + 2 * f + j > 1:
                    pe.wait_ge(evacuated, up_to(ea + 2 * f + j - 1, 2, it))
                product(ua + 2 * f + j, it, 2, pair[j], KD, xhi, xlo, 0, KD, c0, n, wait_k, ks)

            def x_there(k):
                pe.wait_ge(xlo_ready, s["x0"] + k + 1)

            if second:
                gate_or_up(0, None, [0, 1, 2, 3, 4, 5], wait_k=x_there)
                norm_sums(2, c0, n)
                gate_or_up(0, None, [6, 7], wait_k=x_there)
                norm_spread(2, c0, n, 5)
                gate_or_up(1, None)
            else:
                gate_or_up(0, None, wait_k=x_there)
                gate_or_up(1, None, [0, 1, 2, 3, 4])
                norm_sums(0, c0, n)
                gate_or_up(1, None, [5])
                norm_spread(0, c0, n, 1)
                gate_or_up(1, None, [6, 7])
            with pe.Fori(0, KF - 1) as it:
                gate_or_up(0, it, f=1)
                gate_or_up(1, it, f=1)

            def down(d, it):
                for j in range(2):
                    if j == 0:
                        pe.wait_ge(evacuated, up_to(eb + d - 1, 2, it))

                    def h_there(k):
                        if k in (0, KF - 1):
                            pe.wait_ge(hlo_ready, s["f0"] + KF - (k == 0))
                    product(ub + 2 * d + j, it, 4, pair[d % 2], DOWN_T, hhi, hlo, j * DOWN_T, KF, c0, n, h_there)

            with pe.Fori(0, KD // 2) as it:
                down(0, it)
                down(1, it)

        ffn_products(STAGES[0], False)

        def project(m, ks=None, wait_k=None):
            name = MIX[m]
            if ks is None or ks[0] == 0:
                pe.wait_ge(evacuated, before[name])
            q = name[0] == "q"
            product(U_IN + m, None, 0, pair[pair_of[name]], KD, xhi, xlo, 0, KD,
                    META if q else 0, NH_OUT if q else NH_ALL, wait_k, ks)

        def k_sums():
            pe.wait_ge(zg_ready, 1)
            pe.wait_ge(rstd_ready, 2)
            for b, (h, o) in enumerate(blocks(0, NH_ALL)):
                col = h * NH_ALL + o
                last = nc.tensor.matmul(nsum[:, 0, 2 * b:2 * b + 2], zsq[:, 0, col:col + P], headsel[:, :],
                                        start=True, stop=True)
            last.then_inc(nsum_filled, 1)

        def k_spread():
            pe.wait_ge(inv_ready, 3)
            for b, (h, o) in enumerate(blocks(0, NH_ALL)):
                src = knrm[:, b, :]
                last = nc.tensor.transpose(nsum[:, h, o:o + P], src, ident[:, :])
            last.then_inc(spread, 1)

        def q_sums(j):
            if j == 0:
                pe.wait_ge(tok_ready, 2)
            pe.wait_ge(zg_ready, j + 2)
            for t in range(QT):
                c = (j * QT + t) * KVH
                last = nc.tensor.matmul(nsum[:, 0, c:c + KVH], zsq[:, (j + 1) % 2, META + t * P:META + (t + 1) * P],
                                 headsel[:, :], start=True, stop=True)
            if j == GQ - 1:
                for g in range(KVH):
                    rows = slice(g * HD, (g + 1) * HD)
                    last = nc.tensor.matmul(nsum[g * NDEC * GQ:(g + 1) * NDEC * GQ, 1, 0:1], dzsq[rows, :, :],
                                            headsel[rows, g:g + 1], start=True, stop=True)
                last.then_inc(nsum_filled, 1)
            else:
                last.then_inc(zsq_read, 1)

        def x_there(k):
            pe.wait_ge(xlo_ready, KD + k + 1)

        half = [[0, 1, 2, 3], [4, 5, 6, 7]]
        project(0, [0, 1, 2, 3, 4, 5], x_there)
        norm_sums(1, 0, NH_ALL)
        project(0, [6, 7], x_there)
        norm_spread(1, 0, NH_ALL, 2)
        project(1)
        k_sums()
        project(2, half[0])
        k_spread()
        project(2, half[1])
        project(3, half[0])
        pe.wait_ge(qk_ready, 1)
        pe.wait_ge(evacuated, E_USE["v"] + 1)
        pe.wait_ge(pads_zero, 2)
        for b in range(NBLK):
            nc.tensor.transpose(flat[:, b * P:(b + 1) * P], vT[:, b * P:(b + 1) * P], ident[:, :])
        nc.tensor.transpose(flat[0:NDEC, NBLK * P:(NBLK + 1) * P], vT[:, PAD + TP:PAD + NT], ident[:, :]
                            ).then_inc(tok_filled, 1)
        project(3, half[1])
        project(4, half[0])
        q_sums(0)
        project(4, half[1])
        project(5, half[0])
        q_sums(1)
        project(5, half[1])
        project(6, half[0])
        q_sums(2)
        project(6, half[1])

        def use(name):
            pe.wait_ge(evacuated, before[name])
            return pair[pair_of[name]]

        def pool_map(g):
            dst = use(f"P{g}")
            pe.wait_ge(pooled, g + 1)
            for s in range(2):
                last = nc.tensor.matmul(dst[:, s, 0:NH_OUT], poolw[:, g, :], gate[:, s * NH_OUT:(s + 1) * NH_OUT],
                                        start=True, stop=True)
            last.then_inc(pair_filled, 1)

        def scores(i):
            t, g = divmod(i, 2)
            rows = slice(g * HD, (g + 1) * HD)
            if i < 2:
                pe.wait_ge(masks_made, 1)
                pe.wait_ge(rot_ready, 5)
                pe.wait_ge(root_ready, 4)
                pe.wait_ge(evacuated, E_USE["u1"] + 1)
            else:
                pe.wait_ge(exp_ready, i - 1)
            if i == 3:
                pe.wait_ge(dprobs_kept, 1)
            for j in range(GQ):
                dst = scorebank[i % 2][:, j // 2, (j % 2) * 2 * P:(j % 2 + 1) * 2 * P]
                nc.tensor.matmul(dst, identb[:, :], maskb[:, min(t, 1), :], start=(j % 2 == 0), stop=False,
                                 skip_group_check=True)
                last = nc.tensor.matmul(dst, qT[rows, j, t * P:(t + 1) * P], kT[rows, t * P:(t + 2) * P],
                                        start=False, stop=True, skip_group_check=True)
            last.then_inc(scored, 1)

        def turn_probs(i):
            pe.wait_ge(prob_ready, i + 1)
            if i == 0:
                pe.wait_ge(dscores_kept, 2)
            else:
                pe.wait_ge(olo_ready, i)
            for b in range(2):
                for j in range(GQ):
                    last = nc.tensor.transpose(turn[:, b, j * P:(j + 1) * P], prob[:, i % 2, j, b * P:(b + 1) * P],
                                               ident[:, :])
            last.then_inc(probs_turned, 1)

        def attend(i):
            t, g = divmod(i, 2)
            rows = slice(g * HD, (g + 1) * HD)
            pe.wait_ge(probT_ready, i + 1)
            for b in range(2):
                last = nc.tensor.matmul(turn[rows, 0, :],
                                        tok[:, (t + b) * P + g * HD:(t + b) * P + (g + 1) * HD],
                                        probT[:, b, :], start=(b == 0), stop=(b == 1))
            last.then_inc(attended, 1)

        def decode_scores():
            pe.wait_ge(newk_placed, 1)
            pe.wait_ge(dq_ready, KVH)
            for b in range(NDEC):
                last = nc.tensor.matmul(turn[:, 0, b * HEADS:(b + 1) * HEADS], ckT[:, b, :], dq[:, b, :, :],
                                        start=True, stop=True)
            last.then_inc(dscores_filled, 1)

        def decode_turn():
            pe.wait_ge(dscores_kept, 1)
            nc.tensor.transpose(turn[0:HD, 0, 0:P], dscoreT[:, :], ident[:, :]).then_inc(dscores_filled, 1)

        def decode_turn_back():
            pe.wait_ge(dprob_ready, 1)
            pe.wait_ge(exp_ready, 2)
            nc.tensor.transpose(nsum[:, 0, 0:HD], dprob[:, :], ident[0:HD, 0:HD]).then_inc(dprobs_filled, 1)

        def decode_attend():
            dst = use("so")
            pe.wait_ge(newv_placed, 16 * NDEC)
            by_row = dprobT[:, :].rearrange("p (g b j) -> p g b j", g=KVH, b=NDEC)
            for b in range(NDEC):
                last = nc.tensor.matmul(dst[:, 0, b * HEADS:(b + 1) * HEADS], cv[:, b, :], by_row[:, :, b, :],
                                        start=True, stop=True)
            last.then_inc(pair_filled, 1)

        project(7, half[0])
        q_sums(3)
        project(7, half[1])
        pool_map(0)
        scores(0)
        decode_scores()
        scores(1)
        decode_turn()
        project(8)

        def out_product(d, ks=None, it=None):
            if ks is None or ks[0] == 0:
                if d == 0:
                    pe.wait_ge(evacuated, E_OUT)
                elif d == 1:
                    pe.wait_ge(exp_ready, 2 * QT - 1)
                    pe.wait_ge(plo_ready, NG - 1)
                else:
                    pe.wait_ge(evacuated, up_to(E_OUT + d - 1, 2, it))
            product(U_OUT + d, it, 2, pair[d % 2], KD, mhi, mlo, 0, KD, 0, NH_OUT, None, ks)

        for i in range(2 * QT):
            turn_probs(i)
            if i + 2 < 2 * QT:
                scores(i + 2)
            elif i == 6:
                out_product(1, [0])
            else:
                pool_map(3)
            attend(i)
            if i == 0:
                decode_turn_back()
                pool_map(1)
            elif i == 1:
                project(9, [0, 1, 2])
            elif i == 2:
                project(9, [3, 4])
            elif i == 3:
                project(9, [5, 6, 7])
            elif i == 4:
                pool_map(2)
            elif i == 5:
                decode_attend()
            elif i == 6:
                out_product(1, [1, 2])
            else:
                out_product(0, [0, 1, 2])
        pe.wait_ge(plo_ready, NG)
        pe.wait_ge(dolo_ready, 1)
        pe.wait_ge(olo_ready, 2 * QT)
        out_product(0, [3, 4, 5, 6, 7])
        out_product(1, [3, 4, 5, 6, 7])
        with pe.Fori(0, KD // 2 - 1) as it:
            out_product(2, it=it)
            out_product(3, it=it)
        ffn_products(STAGES[1], True)

    @block.scalar
    def _(act):
        act.dma_start(fixed[:], a["fixed"]).then_inc(fixed_loaded, 16)

        def late_consts():
            act.dma_start(maskf[:], a["masks"]).then_inc(masks_loaded, 16)

        def split_hi(c, it=None, slope=4):
            t = tiles_of(c)
            act.wait_ge(raw_loaded[c % RAW], up_to(16 * (c // RAW + 1), slope // RAW * 16, it))
            if c >= 2:
                act.wait_ge(unit_done, up_to(c - 1, slope, it))
            nc.scalar.copy(whi[:, c % 2, 0:t, :], raw[:, c % RAW, 0:t, :]).then_inc(whi_ready, 1)

        def x_hi(d, g, c0, n, it=None, step=2):
            nc.scalar.activation(tile(xhi, d, it, c0, 2 * n, step), tile(xT, d, it, c0, 2 * n, step), ACT.Copy,
                                 scale=gain(g, d, it, step)).then_inc(xhi_ready, 1)

        def root(dst, src, mean, i):
            act.wait_ge(nsum_filled, i)
            return nc.scalar.activation(dst, src, ACT.Sqrt, scale=1.0 / mean, bias=eps[0:dst.shape[0], 0:1])

        def norm(i, c0, n):
            root(nrm[:, 0, 0:BLKS], nsum[:, 0, 0:BLKS], D, NORM_AT[i]).then_inc(root_ready, 1)
            act.wait_ge(spread, i + 1 + (i == 2))
            nc.scalar.copy(halves(rstd[:, c0:c0 + 2 * n], n), nsum[:, :, 0:n]).then_inc(rstd_ready, 1)

        act.wait_ge(consts_made, 2)
        nc.scalar.copy(warm[:, :], eps[:, :]).then_inc(warmed, 1)
        act.wait_ge(fixed_loaded, 16)
        split_hi(0)
        for k in range(KD):
            act.wait_ge(x_loaded[k], 16)
            x_hi(k, 0, 0, NH_ALL)
        split_hi(1)
        for k in range(POOL_SQ, KD):
            nc.scalar.activation(sqx[:, k, :], xT[:, k, :], ACT.Square).then_inc(sqx_ready, 1)
        late_consts()
        split_hi(2)
        act.wait_ge(warmed, 1)
        nc.scalar.activation(warm[:, :], eps[:, :], ACT.Sqrt).then_inc(warmed, 1)
        norm(0, 0, NH_ALL)

        def ffn_act(s, second):
            ua, ub, ea, eb, c0, n = (s[x] for x in ("ua", "ub", "ea", "eb", "c0", "n"))
            cols = slice(c0, c0 + 2 * n)

            def step_a(f, it=None):
                if ua + f:
                    split_hi(ua + 2 * f + 2, it)
                act.wait_ge(evacuated, up_to(ea + 2 * f + 1, 4, it))
                nc.scalar.activation(act_gate[:, cols], gate[:, cols], ACT.Silu).then_inc(silu_ready, 1)
                split_hi(ua + 2 * f + 3, it)
                act.wait_ge(evacuated, up_to(ea + 2 * f + 2, 4, it))
                nc.scalar.copy(tile(hhi, f, it, c0, 2 * n), hid[:, cols]).then_inc(hhi_ready, 1)

            step_a(0)
            step_a(1)
            with act.Fori(0, KF // 2 - 2) as it:
                step_a(2, it)
                step_a(3, it)
            step_a(KF - 2)
            step_a(KF - 1)

            def step_b(d, it=None):
                if ub + 2 * d + 2 < U_END:
                    split_hi(ub + 2 * d + 2, it)
                    split_hi(ub + 2 * d + 3, it)
                if second:
                    act.wait_ge(evacuated, up_to(eb + d + 1, 2, it))
                    at = d * NOUT if it is None else (it * 2 + d) * NOUT
                    act.dma_start(a["o_y"][:, bass.ds(at, NOUT)], ybuf[:, d % 2, :]).then_inc(y_sent[d % 2], 16)
                else:
                    act.wait_ge(evacuated, up_to(eb + d + 1, 2, it))
                    x_hi(d, 1, c0, n, it)

            with act.Fori(0, KD // 2 - 1) as it:
                step_b(0, it)
                step_b(1, it)
            step_b(KD - 2)
            step_b(KD - 1)

        ffn_act(STAGES[0], False)
        norm(1, 0, NH_ALL)

        def split_next(m):
            split_hi(U_IN + m + 2)

        def spread_z(x):
            c0, n = (0, NH_ALL) if x == 0 else (META, NH_OUT)
            act.wait_ge(evacuated, E_USE[MIX[x + (x > 0)]] + 1)
            if x >= 2:
                act.wait_ge(sin_ready, x - 1)
                act.wait_ge(cos_ready, x - 1)
                if x == 2:
                    act.wait_ge(nsum_filled, 3)
                else:
                    act.wait_ge(zsq_read, x - 2)
            nc.scalar.activation(zg[:, x % 2, c0:c0 + 2 * n], gate[:, c0:c0 + 2 * n], ACT.Copy,
                                 scale=gains[:, G_Q + (x == 0):G_Q + (x == 0) + 1])
            sq_x = nc.scalar.activation(zsq[:, x % 2, c0:c0 + 2 * n], gate[:, c0:c0 + 2 * n], ACT.Square)
            if x:
                sq_x = nc.scalar.activation(dzsq[:, :, x - 1], gate[:, TP:NT], ACT.Square)
            sq_x.then_inc(zg_ready, 1)
            act.wait_ge(zg_ready, x + 1)
            act.wait_ge(pads_zero, 5)
            half = ROPE // 2
            for h in range(0, P, HD):
                for to, src in ((h, h + half), (h + half, h)):
                    act.dma_start(partner[to:to + half, x % 2, c0:c0 + 2 * n],
                                  zg[src:src + half, x % 2, c0:c0 + 2 * n]).then_inc(partner_there[x % 2], 16)

        def exps(i):
            act.wait_ge(nmax_ready, i + 1)
            if i >= 2:
                act.wait_ge(probs_turned, i - 1)
            s = i % 2
            for j in range(GQ):
                nc.scalar.activation(prob[:, s, j, :], scorebank[s][:, j // 2, (j % 2) * 2 * P:(j % 2 + 1) * 2 * P],
                                     ACT.Exp, scale=qscale(i, j), bias=small[:, s, 4 + j:5 + j],
                                     accum_out=small[:, s, 12 + j:13 + j])
            nc.scalar.activation(small[:, s, 16:20], small[:, s, 8:12], ACT.Exp).then_inc(exp_ready, 1)

        def out_probT(i):
            act.wait_ge(probs_turned, i + 1)
            if i >= 1:
                act.wait_ge(attended, i)
            else:
                act.wait_ge(dexp_ready, 1)
            nc.scalar.copy(probT[:, :, :], turn[:, :, :]).then_inc(probT_ready, 1)

        def out_hi(i):
            t, g = divmod(i, 2)
            rows = slice(g * HD, (g + 1) * HD)
            act.wait_ge(attended, i + 1)
            nc.scalar.copy(mhi[rows, NG:NG + GQ, t * P:(t + 1) * P],
                           turn[rows, 0, :].rearrange("p (j q) -> p j q", j=GQ)).then_inc(ohi_ready, 1)

        def pool_hi(g):
            act.wait_ge(evacuated, E_USE[f"P{g}"] + 1)
            nc.scalar.copy(mhi[:, g, :], pooled_out[:, :]).then_inc(phi_ready, 1)

        split_next(0)
        spread_z(0)
        split_next(1)
        root(nrm[:, 0, :], nsum[:, 0, 0:2 * BLKS], HD, 3).then_inc(root_ready, 1)
        split_next(2)
        spread_z(1)
        split_next(3)
        spread_z(2)
        split_next(4)
        spread_z(3)
        split_next(5)
        spread_z(4)
        split_next(6)
        act.wait_ge(nsum_filled, 4)
        nc.scalar.activation(qnrm[:, 0, :], nsum[:, 0, 0:GQ * QT * KVH], ACT.Sqrt, scale=1.0, bias=eps64[:, 0:1])
        nc.scalar.activation(dnrm[:, 0:1], nsum[0:HD, 1, 0:1], ACT.Sqrt, scale=1.0, bias=eps64[0:HD, 0:1]
                             ).then_inc(root_ready, 1)
        split_next(7)
        exps(0)
        exps(1)
        act.wait_ge(dnmax_ready, 1)
        nc.scalar.activation(dprob[:, :], dscore[:, :], ACT.Exp, scale=dnrm[:, 1:2], bias=dsmall[:, 1:2],
                             accum_out=dsmall[:, 3:4])
        nc.scalar.activation(dsmall[:, 4:5], dsmall[:, 2:3], ACT.Exp).then_inc(dexp_ready, 1)
        pool_hi(0)
        for i in range(2 * QT):
            out_probT(i)
            if i == 2:
                split_next(8)
            elif i == 5:
                split_next(9)
            elif i == 6:
                exps(7)
            out_hi(i)
            if i + 2 < 2 * QT and i != 5:
                exps(i + 2)
            if i == 0:
                pool_hi(1)
            elif i == 4:
                pool_hi(2)
            if i == 6:
                act.wait_ge(evacuated, E_USE["so"] + 1)
                nc.scalar.copy(mhi[:, NG:NG + GQ, SEQ:NOUT], dout[:, :, :].rearrange("p b j -> p j b")
                               ).then_inc(dohi_ready, 1)
            elif i == 7:
                pool_hi(3)

        with act.Fori(0, KD // RAW) as it:
            for d in range(RAW):
                split_hi(U_OUT + d + 2, it)
                act.wait_ge(evacuated, up_to(E_OUT + d + 1, RAW, it))
                x_hi(d, 2, META, NH_OUT, it, RAW)
        norm(2, META, NH_OUT)
        act.wait_ge(mix_sent, 16 * 6)
        ffn_act(STAGES[1], True)
        for r in range(2):
            act.wait_ge(y_sent[r], 16 * (KD // 2))

    @block.vector
    def _(dve):
        steps = [0]

        def chain(ins):
            steps[0] += 1
            ins.then_inc(step, 1)
            dve.wait_ge(step, steps[0])

        nc.vector.memset(ones[:, :], 1.0)
        for g in range(KVH):
            for h in range(KVH):
                nc.vector.memset(headsel[g * HD:(g + 1) * HD, h:h + 1], float(g == h))
        nc.vector.memset(eps[:, :], EPS).then_inc(consts_made, 1)
        nc.vector.memset(eps64[:, :], EPS * HD).then_inc(consts_made, 1)

        def split_lo(c, it=None, slope=4):
            t = tiles_of(c)
            dve.wait_ge(whi_ready, up_to(c + 1, slope, it))
            nc.vector.tensor_tensor(wlo[:, c % 2, 0:t, :], raw[:, c % RAW, 0:t, :],
                                    whi[:, c % 2, 0:t, :].bitcast(F32), ALU.subtract).then_inc(wlo_ready, 1)

        def x_lo(d, g, c0, n, it=None, step=2):
            dve.wait_ge(xhi_ready, up_to(g * KD + d + 1, step, it))
            nc.vector.scalar_tensor_tensor(
                out=tile(xlo, d, it, c0, 2 * n, step), in0=tile(xT, d, it, c0, 2 * n, step),
                scalar=gain(g, d, it, step), in1=tile(xhi, d, it, c0, 2 * n, step).bitcast(F32),
                op0=ALU.mult, op1=ALU.subtract).then_inc(xlo_ready, 1)

        def invert(i, dst, src):
            dve.wait_ge(root_ready, i)
            nc.vector.reciprocal(dst, src).then_inc(inv_ready, 1)

        dve.wait_ge(fixed_loaded, 16)
        nc.vector.tensor_scalar(nsink[:, :], fixed[:, C_SINK:C_IDENT], -1.0, None, ALU.mult)
        split_lo(0)
        for k in range(KD):
            x_lo(k, 0, 0, NH_ALL)
        split_lo(1)
        for i, k in enumerate(range(POOL_SQ + 1, KD)):
            dve.wait_ge(sqx_ready, i + 2)
            if i:
                dve.wait_ge(sqx_summed, i)
            nc.vector.tensor_tensor(sqx[:, POOL_SQ, :], sqx[:, POOL_SQ, :], sqx[:, k, :], ALU.add
                                    ).then_inc(sqx_summed, 1)
        dve.wait_ge(sqx_summed, KD - POOL_SQ - 1)
        dve.wait_ge(sqsum_ready, POOL_SQ)
        nc.vector.tensor_tensor(sqx[:, POOL_SQ, :], sqx[:, POOL_SQ, :], sqsum[:, :], ALU.add).then_inc(sqx_summed, 1)
        split_lo(2)
        invert(1, nrm[:, 1, 0:BLKS], nrm[:, 0, 0:BLKS])
        dve.wait_ge(masks_loaded, 16)
        nc.vector.tensor_copy(identb[:, :], ident[:, :])
        nc.vector.tensor_copy(maskb[:], maskf[:]).then_inc(masks_made, 1)
        dve.wait_ge(rstd_ready, 1)

        def ffn_vector(s, second):
            ua, ub, ea, eb, c0, n, f0 = (s[x] for x in ("ua", "ub", "ea", "eb", "c0", "n", "f0"))
            cols = slice(c0, c0 + 2 * n)

            def step_a(f, it=None):
                dve.wait_ge(unit_done, up_to(ua + 2 * f + 1, 4, it))
                nc.vector.tensor_tensor(halves(gate[:, cols], n), pair[0][:, :, 0:n], halves(rstd[:, cols], n),
                                        ALU.mult).then_inc(evacuated, 1)
                if ua + f:
                    split_lo(ua + 2 * f + 2, it)
                dve.wait_ge(silu_ready, up_to(f0 + f + 1, 2, it))
                nc.vector.tensor_tensor(hid[:, cols], act_gate[:, cols], rstd[:, cols], ALU.mult
                                        ).then_inc(silu_scaled, 1)
                dve.wait_ge(unit_done, up_to(ua + 2 * f + 2, 4, it))
                dve.wait_ge(silu_scaled, up_to(f0 + f + 1, 2, it))
                nc.vector.tensor_tensor(halves(hid[:, cols], n), pair[1][:, :, 0:n], halves(hid[:, cols], n),
                                        ALU.mult).then_inc(evacuated, 1)
                split_lo(ua + 2 * f + 3, it)
                dve.wait_ge(hhi_ready, up_to(f0 + f + 1, 2, it))
                nc.vector.tensor_tensor(tile(hlo, f, it, c0, 2 * n), hid[:, cols],
                                        tile(hhi, f, it, c0, 2 * n).bitcast(F32), ALU.subtract
                                        ).then_inc(hlo_ready, 1)

            step_a(0)
            step_a(1)
            with dve.Fori(0, KF // 2 - 2) as it:
                step_a(2, it)
                step_a(3, it)
            step_a(KF - 2)
            step_a(KF - 1)

            def step_b(d, it=None):
                if ub + 2 * d + 2 < U_END:
                    split_lo(ub + 2 * d + 2, it)
                dve.wait_ge(unit_done, up_to(ub + 2 * d + 2, 4, it))
                x_d = halves(tile(xT, d, it, c0, 2 * n), n)
                if second and d >= 2:
                    dve.wait_ge(y_sent[d % 2], up_to(16 * (d // 2), 16, it))
                dst = halves(ybuf[:, d % 2, :], n) if second else x_d
                nc.vector.scalar_tensor_tensor(out=dst, in0=pair[d % 2][:, :, 0:n], scalar=0.5, in1=x_d,
                                               op0=ALU.mult, op1=ALU.add).then_inc(evacuated, 1)
                if ub + 2 * d + 3 < U_END:
                    split_lo(ub + 2 * d + 3, it)
                if not second:
                    x_lo(d, 1, c0, n, it)

            if second:
                step_b(0)
                step_b(1)
                with dve.Fori(0, KD // 2 - 2) as it:
                    step_b(2, it)
                    step_b(3, it)
            else:
                with dve.Fori(0, KD // 2 - 1) as it:
                    step_b(0, it)
                    step_b(1, it)
            step_b(KD - 2)
            step_b(KD - 1)

        ffn_vector(STAGES[0], False)
        invert(2, nrm[:, 1, 0:BLKS], nrm[:, 0, 0:BLKS])
        dve.wait_ge(rstd_ready, 2)

        def split_next(m):
            split_lo(U_IN + m + 2)

        def scaled(m, dst, c0, n):
            dve.wait_ge(unit_done, U_IN + m + 1)
            nc.vector.tensor_tensor(halves(dst, n), pair[pair_of[MIX[m]]][:, :, 0:n],
                                    halves(rstd[:, c0:c0 + 2 * n], n), ALU.mult).then_inc(evacuated, 1)

        def take_z(x):
            c0, n = (0, NH_ALL) if x == 0 else (META, NH_OUT)
            dve.wait_ge(zg_ready, x) if x else None
            scaled(x + (x > 0), gate[:, c0:c0 + 2 * n], c0, n)

        def rotate(x):
            c0, n = (0, NH_ALL) if x == 0 else (META, NH_OUT)
            cols = slice(c0, c0 + 2 * n)
            if x:
                dve.wait_ge(rot_ready, x)
            dve.wait_ge(partner_there[x % 2], 16 * 2 * KVH * (x // 2 + 1))
            nc.vector.tensor_tensor(sq[:, cols], partner[:, x % 2, cols], sinT[:, cols], ALU.mult
                                    ).then_inc(sin_ready, 1)
            if x == 0:
                dve.wait_ge(rot_ready, 1)
                dve.wait_ge(spread, 3)
                nc.vector.tensor_tensor(halves(kT[:, PAD:PAD + NT], n), halves(hid[:, cols], n), nsum[:, :, 0:n],
                                        ALU.mult).then_inc(qk_ready, 1)

        def pool_mean(g):
            w = WINDOWS[g]
            src = up[:, g % 2, :]
            win = wsum[:, g % 2, :]
            if g:
                dve.wait_ge(pair_filled, filled[f"P{g - 1}"])
            dve.wait_ge(summed, summed_at[g])
            nc.vector.scalar_tensor_tensor(out=gate[:, 0:SEQ], in0=win[:, 16 + META:16 + TP], scalar=1.0 / w,
                                           in1=src[:, 16 + META:16 + TP], op0=ALU.mult, op1=ALU.subtract)
            nc.vector.tensor_copy(ulast[:, g, :], src[:, 16 + TP - STATE:16 + TP])
            chain(nc.vector.tensor_copy(stT[:, g, :, STATE], src[:, 16 + TP:16 + NT]))
            chain(nc.vector.tensor_reduce(dsum[:, :], stT[:, g, :, STATE + 1 - w:STATE + 1], AX, ALU.add))
            nc.vector.scalar_tensor_tensor(out=gate[:, SEQ:NOUT], in0=dsum[:, :], scalar=1.0 / w,
                                           in1=src[:, 16 + TP:16 + NT], op0=ALU.mult, op1=ALU.subtract
                                           ).then_inc(pooled, 1)

        def pool_out(g):
            dve.wait_ge(pair_filled, filled[f"P{g}"])
            if g:
                dve.wait_ge(plo_ready, g)
            nc.vector.tensor_scalar(halves(pooled_out[:, :], NH_OUT), pair[0][:, :, 0:NH_OUT],
                                    gains[:, G_POOL + g:G_POOL + g + 1], None, ALU.mult).then_inc(evacuated, 1)

        def take_u(g):
            if g >= 2:
                dve.wait_ge(pair_filled, filled[f"P{g - 2}"])
                dve.wait_ge(summed, summed_at[g - 2])
            scaled(6 + g, up[:, g % 2, 16:16 + NT], 0, NH_ALL)

        def maxima(i):
            s = i % 2
            g = i % 2
            dve.wait_ge(scored, i + 1)
            sc = scorebank[s].rearrange("p s (j k) -> p (s j) k", k=2 * P)
            chain(nc.vector.tensor_reduce(small[:, s, 0:4], sc, AX, ALU.max))
            chain(nc.vector.tensor_tensor(small[:, s, 28:32], small[:, s, 0:4], qscale(i), ALU.mult))
            chain(nc.vector.scalar_tensor_tensor(out=small[:, s, 4:8], in0=small[:, s, 28:32], scalar=-1.0,
                                                 in1=nsink[:, g * GQ:(g + 1) * GQ], op0=ALU.mult, op1=ALU.min))
            nc.vector.tensor_tensor(small[:, s, 8:12], small[:, s, 4:8], sink[:, g * GQ:(g + 1) * GQ], ALU.add
                                    ).then_inc(nmax_ready, 1)

        def normalise(i):
            s = i % 2
            dve.wait_ge(exp_ready, i + 1)
            chain(nc.vector.tensor_tensor(small[:, s, 20:24], small[:, s, 12:16], small[:, s, 16:20], ALU.add))
            chain(nc.vector.reciprocal(small[:, s, 24:28], small[:, s, 20:24]))
            for j in range(GQ):
                last = nc.vector.tensor_scalar(prob[:, s, j, :], prob[:, s, j, :], small[:, s, 24 + j:25 + j], None,
                                               ALU.mult)
            last.then_inc(prob_ready, 1)

        def out_lo(i):
            t, g = divmod(i, 2)
            rows = slice(g * HD, (g + 1) * HD)
            dve.wait_ge(ohi_ready, i + 1)
            nc.vector.tensor_tensor(mlo[rows, NG:NG + GQ, t * P:(t + 1) * P],
                                    turn[rows, 0, :].rearrange("p (j q) -> p j q", j=GQ),
                                    mhi[rows, NG:NG + GQ, t * P:(t + 1) * P].bitcast(F32), ALU.subtract
                                    ).then_inc(olo_ready, 1)

        take_z(0)
        split_next(0)
        scaled(1, vT[:, PAD:PAD + NT], 0, NH_ALL)
        split_next(1)
        dve.wait_ge(root_ready, 3)
        chain(nc.vector.reciprocal(nrm[:, 1, :], nrm[:, 0, :]))
        nc.vector.tensor_copy(knrm[:, :, :].rearrange("p b (g e) -> p (b g) e", g=KVH),
                              nrm[:, 1, :].rearrange("p (c o) -> p c o", o=1).to_broadcast([P, KVH * BLKS, HD])
                              ).then_inc(inv_ready, 1)
        dve.wait_ge(mixin_loaded, 16 * 6)
        rotate(0)
        take_z(1)
        split_next(2)
        dve.wait_ge(tok_filled, 1)
        tokps = nsum.rearrange("p s n -> p (s n)")
        vals, new = slice(0, NBLK * P), slice(NBLK * P, (NBLK + 1) * P)
        nc.vector.tensor_copy(tok[:, vals], tokps[:, vals]).then_inc(tok_ready, 1)
        nc.vector.tensor_copy(tok[0:NDEC, new], tokps[0:NDEC, new]).then_inc(tok_ready, 1)
        take_z(2)
        split_next(3)
        rotate(1)
        take_z(3)
        split_next(4)
        rotate(2)
        take_z(4)
        split_next(5)
        rotate(3)
        dve.wait_ge(pads_zero, 3)
        take_u(0)
        split_next(6)
        nc.vector.tensor_copy(ckT[:, :, WIN - 1], kT[:, PAD + TP:PAD + NT]).then_inc(newk_placed, 1)
        dve.wait_ge(zg_ready, 5)
        pool_mean(0)
        rotate(4)
        dve.wait_ge(root_ready, 4)
        nc.vector.reciprocal(qnrm[:, 1, :], qnrm[:, 0, :])
        nc.vector.reciprocal(dnrm[:, 1:2], dnrm[:, 0:1]).then_inc(inv_ready, 1)
        dve.wait_ge(inv_ready, 4)
        take_u(1)
        split_next(7)
        pool_out(0)
        maxima(0)
        dve.wait_ge(dscores_filled, 1)
        for g in range(KVH):
            last = nc.vector.tensor_copy(
                dscoreT[:, g * NDEC * GQ:(g + 1) * NDEC * GQ].rearrange("p (b j) -> p b j", b=NDEC),
                turn[:, 0, 0:HD].rearrange("p (b h) -> p b h", b=NDEC)[:, :, g * GQ:(g + 1) * GQ])
        last.then_inc(dscores_kept, 1)
        dve.wait_ge(dscores_filled, 2)
        nc.vector.tensor_copy(dscore[:, :], turn[0:HD, 0, 0:P]).then_inc(dscores_kept, 1)
        dve.wait_ge(dscores_kept, 2)
        maxima(1)
        normalise(0)
        chain(nc.vector.tensor_reduce(dsmall[:, 0:1], dscore[:, :], AX, ALU.max))
        chain(nc.vector.tensor_tensor(dsmall[:, 7:8], dsmall[:, 0:1], dnrm[:, 1:2], ALU.mult))
        chain(nc.vector.scalar_tensor_tensor(out=dsmall[:, 1:2], in0=dsmall[:, 7:8], scalar=-1.0,
                                             in1=ndsink, op0=ALU.mult, op1=ALU.min))
        nc.vector.tensor_tensor(dsmall[:, 2:3], dsmall[:, 1:2], dsink, ALU.add).then_inc(dnmax_ready, 1)
        pool_mean(1)
        dve.wait_ge(dexp_ready, 1)
        chain(nc.vector.tensor_tensor(dsmall[:, 5:6], dsmall[:, 3:4], dsmall[:, 4:5], ALU.add))
        chain(nc.vector.reciprocal(dsmall[:, 6:7], dsmall[:, 5:6]))
        nc.vector.tensor_scalar(dprob[:, :], dprob[:, :], dsmall[:, 6:7], None, ALU.mult).then_inc(dprob_ready, 1)
        take_u(2)
        for i in range(2 * QT):
            if i == 6:
                pool_mean(3)
            elif i == 7:
                pool_out(3)
            if i + 1 < 2 * QT:
                normalise(i + 1)
            if i == 5:
                split_next(9)
                out_lo(i)
                dve.wait_ge(pair_filled, filled["so"])
                for g in range(KVH):
                    rows = slice(g * HD, (g + 1) * HD)
                    last = nc.vector.tensor_copy(dout[rows, :, :],
                                                 pair[0][rows, 0, 0:HD].rearrange("p (b h) -> p b h", b=NDEC)[
                                                     :, :, g * GQ:(g + 1) * GQ])
                last.then_inc(evacuated, 1)
            if i + 2 < 2 * QT:
                maxima(i + 2)
            if i == 0:
                dve.wait_ge(dprobs_filled, 1)
                nc.vector.tensor_copy(dprobT[:, :], nsum[:, 0, 0:HD]).then_inc(dprobs_kept, 1)
            if i != 5:
                out_lo(i)
            if i == 0:
                pool_out(1)
                pool_mean(2)
            elif i == 2:
                split_next(8)
            elif i == 3:
                take_u(3)
            elif i == 4:
                pool_out(2)

        with dve.Fori(0, KD // RAW) as it:
            for d in range(RAW):
                dve.wait_ge(unit_done, up_to(U_OUT + d + 1, RAW, it))
                x_d = halves(tile(xT, d, it, META, NOUT, RAW), NH_OUT)
                nc.vector.tensor_tensor(x_d, pair[d % 2][:, :, 0:NH_OUT], x_d, ALU.add).then_inc(evacuated, 1)
                split_lo(U_OUT + d + 2, it)
                x_lo(d, 2, META, NH_OUT, it, RAW)
        invert(5, nrm[:, 1, 0:BLKS], nrm[:, 0, 0:BLKS])
        dve.wait_ge(rstd_ready, 3)
        dve.wait_ge(mix_sent, 16 * 6)
        ffn_vector(STAGES[1], True)

    @block.gpsimd
    def _(pool):
        def square(d, e0, c0, n, i, it=None):
            pool.wait_ge(evacuated, up_to(e0 + d + 1, 1, it))
            x_d = tile(xT, d, it, c0, 2 * n, 1)
            nc.gpsimd.tensor_tensor(sq[:, c0:c0 + 2 * n], x_d, x_d, ALU.mult).then_inc(sq_ready, 1)
            pool.wait_ge(sq_ready, up_to(SQSUM_AT[i - 1] + d, 1, it))
            nc.gpsimd.tensor_tensor(sqsum[:, c0:c0 + 2 * n], sqsum[:, c0:c0 + 2 * n], sq[:, c0:c0 + 2 * n],
                                    ALU.add).then_inc(sqsum_ready, 1)
            pool.wait_ge(sqsum_ready, up_to(SQSUM_AT[i - 1] + d + 1, 1, it))

        pool.wait_ge(x_loaded[0], 16)
        nc.gpsimd.tensor_tensor(sqsum[:, :], xT[:, 0, :], xT[:, 0, :], ALU.mult).then_inc(sqsum_ready, 1)
        for k in range(1, POOL_SQ):
            pool.wait_ge(x_loaded[k], 16)
            nc.gpsimd.tensor_tensor(sqx[:, k, :], xT[:, k, :], xT[:, k, :], ALU.mult).then_inc(sq_ready, 1)
            pool.wait_ge(sq_ready, k)
            pool.wait_ge(sqsum_ready, k)
            nc.gpsimd.tensor_tensor(sqsum[:, :], sqsum[:, :], sqx[:, k, :], ALU.add).then_inc(sqsum_ready, 1)
        pool.wait_ge(nsum_filled, 1)
        nc.gpsimd.memset(sqsum[:, :], 0.0).then_inc(sqsum_zero, 1)
        pool.wait_ge(sqsum_zero, 1)
        with pool.Fori(0, KD) as it:
            square(0, E_B1, 0, NH_ALL, 1, it)
        pool.wait_ge(unit_done, U_IN)
        nc.gpsimd.memset(kT[:, 0:PAD], 0.0).then_inc(pads_zero, 1)
        nc.gpsimd.memset(vT[:, 0:PAD], 0.0).then_inc(pads_zero, 1)
        nc.gpsimd.memset(up[:, :, 0:16], 0.0).then_inc(pads_zero, 1)
        nc.gpsimd.memset(wsum[:, :, 0:16], 0.0).then_inc(pads_zero, 1)
        nc.gpsimd.memset(partner[:, :, :], 0.0).then_inc(pads_zero, 1)
        nc.gpsimd.memset(dq[:, :, :, :], 0.0).then_inc(pads_zero, 1)
        pool.wait_ge(nsum_filled, 2)
        nc.gpsimd.memset(sqsum[:, :], 0.0).then_inc(sqsum_zero, 1)
        def window_sums(g):
            pool.wait_ge(evacuated, E_USE[f"u{g}"] + 1)
            if g:
                pool.wait_ge(pooled, g)
            src = up[:, g % 2, :]
            for s in range(g + 1):
                dst = wsum[:, (2 * g - s) % 2, :]
                nc.gpsimd.tensor_tensor(dst[:, 16:16 + TP], src[:, 16:16 + TP],
                                        src[:, 16 - (1 << s):16 + TP - (1 << s)], ALU.add).then_inc(summed, 1)
                pool.wait_ge(summed, summed_at[g] - g + s)
                src = dst

        pool.wait_ge(pads_zero, 4)
        pool.wait_ge(mixin_loaded, 16 * 6)
        for x in range(5):
            cols = slice(0 if x == 0 else META, NT)
            pool.wait_ge(zg_ready, x + 1)
            if x == 1:
                pool.wait_ge(qk_ready, 1)
            nc.gpsimd.tensor_tensor(hid[:, cols], zg[:, x % 2, cols], cosT[:, cols], ALU.mult
                                    ).then_inc(cos_ready, 1)
            if x == 4:
                window_sums(0)
            pool.wait_ge(cos_ready, x + 1)
            pool.wait_ge(sin_ready, x + 1)
            dst = hid[:, :] if x == 0 else qT[:, x - 1, :]
            nc.gpsimd.tensor_tensor(dst, hid[:, cols], sq[:, cols], ALU.add).then_inc(rot_ready, 1)
            pool.wait_ge(rot_ready, x + 1)
        pool.wait_ge(pads_zero, 6)
        for g in range(KVH):
            rows = slice(g * HD, (g + 1) * HD)
            nc.gpsimd.tensor_copy(dq[rows, :, g, :], qT[rows, :, SEQ:NOUT].rearrange("p j b -> p b j")
                                  ).then_inc(dq_ready, 1)
            pool.wait_ge(dq_ready, g + 1)

        def pool_lo(g):
            pool.wait_ge(phi_ready, g + 1)
            nc.gpsimd.tensor_tensor(mlo[:, g, :], pooled_out[:, :], mhi[:, g, :].bitcast(F32), ALU.subtract
                                    ).then_inc(plo_ready, 1)

        window_sums(1)
        pool_lo(0)
        window_sums(2)
        pool_lo(1)
        window_sums(3)
        pool_lo(2)
        pool.wait_ge(dohi_ready, 1)
        nc.gpsimd.tensor_tensor(mlo[:, NG:NG + GQ, SEQ:NOUT], dout[:, :, :].rearrange("p b j -> p j b"),
                                mhi[:, NG:NG + GQ, SEQ:NOUT].bitcast(F32), ALU.subtract).then_inc(dolo_ready, 1)
        pool_lo(3)
        pool.wait_ge(sqsum_zero, 2)
        with pool.Fori(0, KD) as it:
            square(0, E_OUT, META, NH_OUT, 2, it)

    ctx.close()


def constants():
    eye = np.eye(P, dtype=np.float32)
    half = ROPE // 2
    i, j = np.arange(P)[:, None], np.arange(2 * P)[None, :]
    band = (j > i) & (j <= i + WIN)
    masks = [np.where(m, 0.0, NEG).astype(np.float32) for m in (band & (j >= PAD), band)]
    pos = np.concatenate([np.arange(TP), np.full(NDEC, PAST)]).astype(np.float32)
    freq = np.exp(np.float32(-math.log(500000.0)) * np.arange(half, dtype=np.float32) * np.float32(2.0 / ROPE))
    ang = (pos[None, :] * freq.astype(np.float32)[:, None]).astype(np.float64)
    cos, sin = np.ones((P, NT), np.float32), np.zeros((P, NT), np.float32)
    for h in range(0, P, HD):
        for b, sign in ((0, -1), (half, 1)):
            cos[h + b:h + b + half] = np.cos(ang)
            sin[h + b:h + b + half] = sign * np.sin(ang)
    return {"masks": np.stack(masks, 1), "cos": cos, "sin": sin}, eye


def kernel(**inputs):
    import numpy as _np
    import concourse.bacc as _bacc
    from concourse import mybir as _mybir
    from concourse.bass_utils import run_bass_kernel_spmd as _run

    nc = _bacc.Bacc("TRN2", target_bir_lowering=False, num_devices=1)
    src = lambda name, *shape: _np.asarray(inputs[name]).reshape(shape)

    def units(w, rows, cols):
        return w.reshape(cols, rows, P, -1, P).transpose(2, 3, 0, 1, 4)

    fixed_in, eye = constants()
    heads = _np.arange(2 * POOLW).reshape(-1, HD)
    by_pair = _np.concatenate([heads[HEADS + h * GQ + j] for j in range(GQ) for h in range(KVH)])
    w_in, w_out = src("w_in", D, -1), src("w_out", D, D)
    w_in = _np.concatenate([w_in[:, 2 * POOLW:], w_in[:, by_pair], w_in[:, 0:POOLW]], 1)
    w_out = _np.concatenate([w_out[0:POOLW], w_out[by_pair]], 0)
    x = _np.concatenate([src("meta_tokens", META, D), src("x_prompt", SEQ, D), src("x_sample", NDEC, D)], 0)
    sinks = src("attn_sinks", 1, HEADS)
    two = lambda name: _np.concatenate([src(name, HD, 1)] * 2, 0)
    dsink = _np.zeros((P, 1), _np.float32)
    dsink[0:HD] = _np.repeat(sinks.reshape(KVH, 1, GQ), NDEC, 1).reshape(HD, 1)
    given = {
        "x": x.T.reshape(KD, P, NT).transpose(1, 0, 2),
        "fixed": _np.concatenate([src("ffn1_norm", KD, P).T, src("mix_norm", KD, P).T, src("ffn2_norm", KD, P).T,
                                  src("pool_scale", NG, P).T, two("q_norm"), two("k_norm"),
                                  _np.repeat(sinks, P, 0), dsink, eye], 1),
        "ck": _np.roll(src("cache_k", NDEC, WIN, P), -1, 1).transpose(2, 0, 1),
        "cv": _np.roll(src("cache_v", NDEC, WIN, P), -1, 1).transpose(1, 0, 2),
        "state": _np.pad(src("state_pool", NDEC, STATE, NG, P), ((0, 0), (0, 1), (0, 0), (0, 0))
                         ).transpose(3, 2, 0, 1),
        "pool_w": src("pool_w", NG, P, P).transpose(1, 0, 2),
        "w_in": units(w_in, KD, 1).reshape(P, -1), "w_out": units(w_out, KD, 1).reshape(P, -1),
    } | fixed_in
    for i in (1, 2):
        both = [units(src(f"ffn{i}_w_{w}", D, F), KD, 1) for w in ("gate", "up")]
        given[f"gu{i}"] = _np.concatenate(both, 2).reshape(P, -1)
        given[f"d{i}"] = units(src(f"ffn{i}_w_down", F, D), DOWN_T, 2).reshape(P, -1)
    given = {n: _np.ascontiguousarray(v) for n, v in given.items()}
    outs = {"o_y": (P, KD * NOUT), "o_pp": (P, NG, STATE), "o_kp": (P, WIN), "o_vp": (P, WIN),
            "o_ps": (P, NG, NDEC, STATE + 1), "o_ks": (P, NDEC, WIN), "o_vs": (WIN, NDEC, P)}
    f32 = _mybir.dt.float32
    a = {n: nc.dram_tensor(n, v.shape, f32, kind="ExternalInput").ap() for n, v in given.items()}
    a |= {n: nc.dram_tensor(n, v, f32, kind="ExternalOutput").ap() for n, v in outs.items()}
    build(nc, a)
    r = _run(nc, [given], core_ids=[0]).results[0]
    y = r["o_y"].reshape(P, KD, NOUT).transpose(2, 1, 0).reshape(NOUT, D)
    return tuple(_np.ascontiguousarray(v) for v in (
        y[0:SEQ].reshape(1, SEQ, D), y[SEQ:].reshape(NDEC, 1, D),
        r["o_pp"].transpose(2, 1, 0).reshape(1, 1, STATE, POOLW),
        r["o_kp"].T.reshape(1, 1, WIN, KVH, HD), r["o_vp"].T.reshape(1, 1, WIN, KVH, HD),
        r["o_ps"][:, :, :, 1:].transpose(2, 3, 1, 0).reshape(1, NDEC, STATE, POOLW),
        r["o_ks"].transpose(1, 2, 0).reshape(1, NDEC, WIN, KVH, HD),
        r["o_vs"].transpose(1, 0, 2).reshape(1, NDEC, WIN, KVH, HD)))
```
